# Optimizing a Trainium2 kernel written in Bass

```python
import math
import jax, jax.numpy as jnp
from jax import lax
import numpy as np

D_MODEL = 1024
BATCH = 1
SEQ = 256
DEPTH = 1

CONV_C = 1024
CONV_W = 31
FOX_HEADS = 16
FOX_HD = 64
FOX_W = FOX_HEADS * FOX_HD
Q_BLOCK = 128
IN_SPLITS = (CONV_C, CONV_C, FOX_W, FOX_W, FOX_W, FOX_HEADS, D_MODEL, D_MODEL)
IN_COLS = sum(IN_SPLITS)
PEER_HEADS = 8
PEER_NKEYS = 128
PEER_EXPERTS = PEER_NKEYS * PEER_NKEYS
PEER_DK = 256
PEER_TOPK = 16
PEER_CHUNK = 128
EPS = 1e-6
NEG = -1e30


def rmsnorm(x, g):
    xf = x.astype(jnp.float32)
    y = xf * lax.rsqrt(jnp.mean(xf * xf, axis=-1, keepdims=True) + EPS)
    return (y * g.astype(jnp.float32)).astype(x.dtype)

def layernorm(x, g, b):
    xf = x.astype(jnp.float32)
    mu = jnp.mean(xf, axis=-1, keepdims=True)
    var = jnp.mean(jnp.square(xf - mu), axis=-1, keepdims=True)
    y = (xf - mu) * lax.rsqrt(var + EPS)
    return (y * g.astype(jnp.float32) + b.astype(jnp.float32)).astype(x.dtype)

def conformer_conv(z_val, z_gate, conv_w, conv_b, ln_g, ln_b, w_conv_out):
    z = z_val * jax.nn.sigmoid(z_gate)
    z = lax.conv_general_dilated(
        z, conv_w[:, None, :].astype(z.dtype), window_strides=(1,),
        padding=[(CONV_W - 1, 0)], dimension_numbers=("NWC", "WIO", "NWC"),
        feature_group_count=CONV_C) + conv_b
    z = layernorm(z, ln_g, ln_b)
    z = z * jax.nn.sigmoid(z)
    return z @ w_conv_out

def forgetting_attention(q, k, v, c):
    B, H, S, hd = q.shape
    nb = S // Q_BLOCK
    scale = 1.0 / math.sqrt(hd)
    qb = q.reshape(B, H, nb, Q_BLOCK, hd).transpose(2, 0, 1, 3, 4)
    cb = c.reshape(B, H, nb, Q_BLOCK).transpose(2, 0, 1, 3)
    kf = k.astype(jnp.float32)
    vf = v.astype(jnp.float32)
    kpos = jnp.arange(S)

    def one_block(args):
        qi, ci, i = args
        s = jnp.einsum("bhqd,bhkd->bhqk", qi.astype(jnp.float32), kf) * scale
        s = s + ci[..., :, None] - c[:, :, None, :]
        qpos = i * Q_BLOCK + jnp.arange(Q_BLOCK)
        mask = kpos[None, :] <= qpos[:, None]
        p = jax.nn.softmax(jnp.where(mask, s, NEG), axis=-1)
        return jnp.einsum("bhqk,bhkd->bhqd", p, vf)

    out = lax.map(one_block, (qb, cb, jnp.arange(nb)))
    return out.transpose(1, 2, 0, 3, 4).reshape(B, H, S, hd).astype(q.dtype)

def peer_ffn(h, peer_wq, peer_k1, peer_k2, peer_u, peer_v):
    B, S, D = h.shape
    T = B * S
    ht = h.reshape(T, D)
    q = (ht @ peer_wq).reshape(T, PEER_HEADS, PEER_DK).astype(jnp.float32)
    half = PEER_DK // 2
    s1 = jnp.einsum("thd,hnd->thn", q[..., :half], peer_k1.astype(jnp.float32))
    s2 = jnp.einsum("thd,hnd->thn", q[..., half:], peer_k2.astype(jnp.float32))
    v1, i1 = lax.top_k(s1, PEER_TOPK)
    v2, i2 = lax.top_k(s2, PEER_TOPK)
    cand = (v1[..., :, None] + v2[..., None, :]).reshape(T, PEER_HEADS, PEER_TOPK * PEER_TOPK)
    sc, pos = lax.top_k(cand, PEER_TOPK)
    e1 = jnp.take_along_axis(i1, pos // PEER_TOPK, axis=-1)
    e2 = jnp.take_along_axis(i2, pos % PEER_TOPK, axis=-1)
    experts = (e1 * PEER_NKEYS + e2).reshape(T, PEER_HEADS * PEER_TOPK)
    gates = jax.nn.softmax(sc, axis=-1).reshape(T, PEER_HEADS * PEER_TOPK)
    nc = T // PEER_CHUNK

    def chunk(args):
        hc, ec, gc = args
        u = peer_u[ec]
        a = jax.nn.gelu(jnp.einsum("ckd,cd->ck", u, hc).astype(jnp.float32)) * gc
        vv = peer_v[ec]
        return jnp.einsum("ck,ckd->cd", a.astype(vv.dtype), vv)

    out = lax.map(chunk, (ht.reshape(nc, PEER_CHUNK, D),
                          experts.reshape(nc, PEER_CHUNK, -1),
                          gates.reshape(nc, PEER_CHUNK, -1)))
    return out.reshape(B, S, D).astype(h.dtype)

def first_inputs(seed: int = 0) -> dict:
    key = jax.random.key(seed)
    ks = jax.random.split(key, 20)
    f32 = jnp.float32
    D = D_MODEL
    nrm = lambda k, shape, s: jax.random.normal(k, shape, f32) * s
    return {
        "x": nrm(ks[0], (BATCH, SEQ, D), 1.0),
        "norm1_g": 1.0 + nrm(ks[1], (D,), 0.02),
        "w_in": nrm(ks[2], (D, IN_COLS), D ** -0.5),
        "conv_w": nrm(ks[3], (CONV_W, CONV_C), CONV_W ** -0.5),
        "conv_b": nrm(ks[4], (CONV_C,), 0.02),
        "conv_ln_g": 1.0 + nrm(ks[5], (CONV_C,), 0.02),
        "conv_ln_b": nrm(ks[6], (CONV_C,), 0.02),
        "w_conv_out": nrm(ks[7], (CONV_C, D), CONV_C ** -0.5),
        "fox_bf": 1.0 + 4.0 * jax.random.uniform(ks[8], (FOX_HEADS,), f32),
        "w_fox_out": nrm(ks[9], (FOX_W, D), FOX_W ** -0.5),
        "w_out": nrm(ks[10], (D, D), D ** -0.5),
        "norm2_g": 1.0 + nrm(ks[11], (D,), 0.02),
        "peer_wq": nrm(ks[12], (D, PEER_HEADS * PEER_DK), D ** -0.5),
        "peer_k1": nrm(ks[13], (PEER_HEADS, PEER_NKEYS, PEER_DK // 2), (PEER_DK // 2) ** -0.5),
        "peer_k2": nrm(ks[14], (PEER_HEADS, PEER_NKEYS, PEER_DK // 2), (PEER_DK // 2) ** -0.5),
        "peer_u": nrm(ks[15], (PEER_EXPERTS, D), D ** -0.5),
        "peer_v": nrm(ks[16], (PEER_EXPERTS, D), PEER_HEADS ** -0.5),
        "normf_g": 1.0 + nrm(ks[17], (D,), 0.02),
    }

def first_block(x, norm1_g, w_in, conv_w, conv_b, conv_ln_g, conv_ln_b, w_conv_out,
              fox_bf, w_fox_out, w_out, norm2_g, peer_wq, peer_k1, peer_k2,
              peer_u, peer_v, normf_g):
    B, S, D = x.shape
    idx = np.cumsum(IN_SPLITS)[:-1].tolist()
    for _ in range(DEPTH):
        h = rmsnorm(x, norm1_g)
        z = h @ w_in
        a_val, a_gate, q, k, v, f_logit, g_a, g_b = jnp.split(z, idx, axis=-1)
        ya = conformer_conv(a_val, a_gate, conv_w, conv_b, conv_ln_g, conv_ln_b, w_conv_out)
        heads = lambda t: t.reshape(B, S, FOX_HEADS, FOX_HD).transpose(0, 2, 1, 3)
        log_f = jax.nn.log_sigmoid(f_logit.astype(jnp.float32) + fox_bf.astype(jnp.float32))
        c = jnp.cumsum(log_f, axis=1).transpose(0, 2, 1)
        ob = forgetting_attention(heads(q), heads(k), heads(v), c)
        yb = ob.transpose(0, 2, 1, 3).reshape(B, S, FOX_W) @ w_fox_out
        mix = (jax.nn.sigmoid(g_a) * ya + jax.nn.sigmoid(g_b) * yb) @ w_out
        x = x + mix
        x = x + peer_ffn(rmsnorm(x, norm2_g), peer_wq, peer_k1, peer_k2, peer_u, peer_v)
    return rmsnorm(x, normf_g)


MEM_LEN = 256
MIX_WIDTH = 768
N_BRANCHES = 3
RNN_BLOCKS = 8
RNN_BLOCK = MIX_WIDTH // RNN_BLOCKS
RNN_CONV = 4
LRU_C = 8.0
GLA_HEADS = 4
GLA_DK = MIX_WIDTH // 2 // GLA_HEADS
GLA_DV = MIX_WIDTH // GLA_HEADS
GLA_LOW_RANK = 16
GLA_NORMALIZER = 16.0
GLA_CHUNK = 64
MEM_HEADS = 4
MEM_HEAD_DIM = MIX_WIDTH // MEM_HEADS
D_FF = 3 * D_MODEL
FFN_CONV = 3

IN_SPLITS_2 = (MIX_WIDTH, GLA_HEADS * GLA_DK, GLA_HEADS * GLA_DK, GLA_HEADS * GLA_DV,
             GLA_HEADS * GLA_DV, GLA_LOW_RANK, MEM_HEADS * MEM_HEAD_DIM, N_BRANCHES * D_MODEL)
N_IN = sum(IN_SPLITS_2)


def rms_norm(x, gain):
    x32 = x.astype(jnp.float32)
    y = x32 * lax.rsqrt(jnp.mean(x32 * x32, axis=-1, keepdims=True) + EPS)
    return (y * gain.astype(jnp.float32)).astype(x.dtype)

def causal_dwconv(x, w, b):
    width, ch = w.shape
    y = lax.conv_general_dilated(
        x, w[:, None, :].astype(x.dtype), window_strides=(1,), padding=[(width - 1, 0)],
        dimension_numbers=("NWC", "WIO", "NWC"), feature_group_count=ch)
    return y + b.astype(x.dtype)

def _linear_combine(left, right):
    a_l, b_l = left
    a_r, b_r = right
    return a_l * a_r, a_r * b_l + b_r

def rg_lru(xr, w_a, b_a, w_x, b_x, lam):
    bsz, slen, ch = xr.shape
    xb = xr.reshape(bsz, slen, RNN_BLOCKS, RNN_BLOCK)
    r = jax.nn.sigmoid(jnp.einsum("bshi,hij->bshj", xb, w_a) + b_a).reshape(bsz, slen, ch)
    i = jax.nn.sigmoid(jnp.einsum("bshi,hij->bshj", xb, w_x) + b_x).reshape(bsz, slen, ch)
    log_a = LRU_C * r.astype(jnp.float32) * jax.nn.log_sigmoid(lam.astype(jnp.float32))
    a = jnp.exp(log_a)
    u = jnp.sqrt(-jnp.expm1(2.0 * log_a)) * (i * xr).astype(jnp.float32)
    _, h = lax.associative_scan(_linear_combine, (a, u), axis=1)
    return h.astype(xr.dtype)

def chunked_gla(q, k, v, log_alpha):
    bsz, slen, nh, dk = q.shape
    dv = v.shape[-1]
    n_chunks = slen // GLA_CHUNK

    def to_chunks(t):
        return t.reshape(bsz, n_chunks, GLA_CHUNK, nh, t.shape[-1]).transpose(0, 1, 3, 2, 4)

    qc, kc, vc, gc = to_chunks(q), to_chunks(k), to_chunks(v), to_chunks(log_alpha)
    g_cum = jnp.cumsum(gc, axis=3)
    g_last = g_cum[:, :, :, -1:, :]
    q_e = qc * (dk ** -0.5) * jnp.exp(g_cum)
    k_e = kc * jnp.exp(-g_cum)
    k_end = kc * jnp.exp(g_last - g_cum)
    decay = jnp.exp(g_last[:, :, :, 0, :])
    mask = jnp.tril(jnp.ones((GLA_CHUNK, GLA_CHUNK), dtype=bool))
    scores = jnp.where(mask, jnp.einsum("bnhid,bnhjd->bnhij", q_e, k_e), 0.0)
    o_intra = jnp.einsum("bnhij,bnhjv->bnhiv", scores, vc)

    def step(state, xs):
        q_n, k_n, v_n, d_n = xs
        o_n = jnp.einsum("bhid,bhdv->bhiv", q_n, state)
        state = d_n[..., None] * state + jnp.einsum("bhjd,bhjv->bhdv", k_n, v_n)
        return state, o_n

    xs = (jnp.moveaxis(q_e, 1, 0), jnp.moveaxis(k_end, 1, 0), jnp.moveaxis(vc, 1, 0),
          jnp.moveaxis(decay, 1, 0))
    state0 = jnp.zeros((bsz, nh, dk, dv), jnp.float32)
    _, o_inter = lax.scan(step, state0, xs)
    o = o_intra + jnp.moveaxis(o_inter, 0, 1)
    return o.transpose(0, 1, 3, 2, 4).reshape(bsz, slen, nh, dv)

def second_inputs(seed: int = 0) -> dict:
    key = jax.random.key(seed)
    ks = jax.random.split(key, 32)

    def nrm(k, shape, scale):
        return jax.random.normal(k, shape, jnp.float32) * scale

    def gain(k, shape):
        return 1.0 + 0.02 * jax.random.normal(k, shape, jnp.float32)

    u = jax.random.uniform(ks[10], (DEPTH, MIX_WIDTH), jnp.float32, minval=0.9, maxval=0.999)
    p = u ** (1.0 / LRU_C)
    rg_lambda = jnp.log(p) - jnp.log1p(-p)
    return {
        "x": nrm(ks[0], (BATCH, SEQ, D_MODEL), 1.0),
        "mem": nrm(ks[1], (BATCH, MEM_LEN, D_MODEL), 1.0),
        "norm_mix": gain(ks[2], (DEPTH, D_MODEL)),
        "w_in": nrm(ks[3], (DEPTH, D_MODEL, N_IN), D_MODEL ** -0.5),
        "rnn_conv_w": nrm(ks[4], (DEPTH, RNN_CONV, MIX_WIDTH), RNN_CONV ** -0.5),
        "rnn_conv_b": nrm(ks[5], (DEPTH, MIX_WIDTH), 0.01),
        "rg_w_a": nrm(ks[6], (DEPTH, RNN_BLOCKS, RNN_BLOCK, RNN_BLOCK), RNN_BLOCK ** -0.5),
        "rg_b_a": nrm(ks[7], (DEPTH, RNN_BLOCKS, RNN_BLOCK), 0.01),
        "rg_w_x": nrm(ks[8], (DEPTH, RNN_BLOCKS, RNN_BLOCK, RNN_BLOCK), RNN_BLOCK ** -0.5),
        "rg_b_x": nrm(ks[9], (DEPTH, RNN_BLOCKS, RNN_BLOCK), 0.01),
        "rg_lambda": rg_lambda,
        "gla_w_decay": nrm(ks[11], (DEPTH, GLA_LOW_RANK, GLA_HEADS * GLA_DK), GLA_LOW_RANK ** -0.5),
        "gla_b_decay": nrm(ks[12], (DEPTH, GLA_HEADS * GLA_DK), 0.01),
        "gla_norm": gain(ks[13], (DEPTH, GLA_HEADS * GLA_DV)),
        "mem_norm": gain(ks[14], (DEPTH, D_MODEL)),
        "w_mem_kv": nrm(ks[15], (DEPTH, D_MODEL, 2 * MEM_HEADS * MEM_HEAD_DIM), D_MODEL ** -0.5),
        "w_branch": nrm(ks[16], (DEPTH, N_BRANCHES, MIX_WIDTH, D_MODEL), MIX_WIDTH ** -0.5),
        "w_out": nrm(ks[17], (DEPTH, D_MODEL, D_MODEL), D_MODEL ** -0.5),
        "norm_ffn": gain(ks[18], (DEPTH, D_MODEL)),
        "w_up": nrm(ks[19], (DEPTH, D_MODEL, 2 * D_FF), D_MODEL ** -0.5),
        "ffn_conv_w": nrm(ks[20], (DEPTH, FFN_CONV, 2 * D_FF), FFN_CONV ** -0.5),
        "ffn_conv_b": nrm(ks[21], (DEPTH, 2 * D_FF), 0.01),
        "w_down": nrm(ks[22], (DEPTH, D_FF, D_MODEL), D_FF ** -0.5),
        "final_norm": gain(ks[23], (D_MODEL,)),
    }

def second_block(x, mem, norm_mix, w_in, rnn_conv_w, rnn_conv_b, rg_w_a, rg_b_a, rg_w_x, rg_b_x,
              rg_lambda, gla_w_decay, gla_b_decay, gla_norm, mem_norm, w_mem_kv, w_branch, w_out,
              norm_ffn, w_up, ffn_conv_w, ffn_conv_b, w_down, final_norm):
    bsz, slen, _ = x.shape
    split_idx = np.cumsum(IN_SPLITS_2)[:-1].tolist()
    for l in range(DEPTH):
        h = rms_norm(x, norm_mix[l])
        z = h @ w_in[l]
        z_rnn, z_q, z_k, z_v, z_g, z_dec, z_mq, z_gate = jnp.split(z, split_idx, axis=-1)

        xr = causal_dwconv(z_rnn, rnn_conv_w[l], rnn_conv_b[l])
        out_a = rg_lru(xr, rg_w_a[l], rg_b_a[l], rg_w_x[l], rg_b_x[l], rg_lambda[l])

        dec_logit = (z_dec @ gla_w_decay[l] + gla_b_decay[l]).astype(jnp.float32)
        log_alpha = (jax.nn.log_sigmoid(dec_logit) / GLA_NORMALIZER).reshape(bsz, slen, GLA_HEADS, GLA_DK)
        o_gla = chunked_gla(
            z_q.astype(jnp.float32).reshape(bsz, slen, GLA_HEADS, GLA_DK),
            z_k.astype(jnp.float32).reshape(bsz, slen, GLA_HEADS, GLA_DK),
            z_v.astype(jnp.float32).reshape(bsz, slen, GLA_HEADS, GLA_DV),
            log_alpha).astype(x.dtype)
        o_gla = rms_norm(o_gla, gla_norm[l].reshape(GLA_HEADS, GLA_DV)).reshape(bsz, slen, -1)
        out_b = o_gla * jax.nn.silu(z_g)

        m = rms_norm(mem, mem_norm[l])
        mk, mv = jnp.split(m @ w_mem_kv[l], 2, axis=-1)
        mk = mk.reshape(bsz, MEM_LEN, MEM_HEADS, MEM_HEAD_DIM)
        mv = mv.reshape(bsz, MEM_LEN, MEM_HEADS, MEM_HEAD_DIM)
        mq = z_mq.reshape(bsz, slen, MEM_HEADS, MEM_HEAD_DIM)
        s = jnp.einsum("bshd,bmhd->bhsm", mq, mk).astype(jnp.float32) * (MEM_HEAD_DIM ** -0.5)
        prob = jax.nn.softmax(s, axis=-1).astype(mv.dtype)
        out_c = jnp.einsum("bhsm,bmhd->bshd", prob, mv).reshape(bsz, slen, MIX_WIDTH)

        branches = jnp.stack([out_a, out_b, out_c], axis=2)
        proj = jnp.einsum("bsnc,ncd->bsnd", branches, w_branch[l])
        gates = jax.nn.sigmoid(z_gate).reshape(bsz, slen, N_BRANCHES, D_MODEL)
        merged = jnp.sum(gates * proj, axis=2)
        x = x + merged @ w_out[l]

        h2 = rms_norm(x, norm_ffn[l])
        up = causal_dwconv(h2 @ w_up[l], ffn_conv_w[l], ffn_conv_b[l])
        gate_h, val_h = jnp.split(up, 2, axis=-1)
        x = x + (jax.nn.gelu(gate_h, approximate=True) * val_h) @ w_down[l]
    return rms_norm(x, final_norm)


def setup_inputs(seed=0):
    out = dict(first_inputs(seed))
    for name, value in second_inputs(seed + 1).items():
        if name != "x":
            out[name + "_2"] = value
    return out


def reference(
    x, norm1_g, w_in, conv_w, conv_b, conv_ln_g, conv_ln_b, w_conv_out, fox_bf, w_fox_out,
    w_out, norm2_g, peer_wq, peer_k1, peer_k2, peer_u, peer_v, normf_g, mem_2, norm_mix_2,
    w_in_2, rnn_conv_w_2, rnn_conv_b_2, rg_w_a_2, rg_b_a_2, rg_w_x_2, rg_b_x_2, rg_lambda_2,
    gla_w_decay_2, gla_b_decay_2, gla_norm_2, mem_norm_2, w_mem_kv_2, w_branch_2, w_out_2,
    norm_ffn_2, w_up_2, ffn_conv_w_2, ffn_conv_b_2, w_down_2, final_norm_2,
):
    x = first_block(
        x, norm1_g, w_in, conv_w, conv_b, conv_ln_g, conv_ln_b, w_conv_out, fox_bf, w_fox_out,
        w_out, norm2_g, peer_wq, peer_k1, peer_k2, peer_u, peer_v, normf_g,
    )
    return second_block(
        x, mem_2, norm_mix_2, w_in_2, rnn_conv_w_2, rnn_conv_b_2, rg_w_a_2, rg_b_a_2, rg_w_x_2,
        rg_b_x_2, rg_lambda_2, gla_w_decay_2, gla_b_decay_2, gla_norm_2, mem_norm_2, w_mem_kv_2,
        w_branch_2, w_out_2, norm_ffn_2, w_up_2, ffn_conv_w_2, ffn_conv_b_2, w_down_2,
        final_norm_2,
    )


_drawn_inputs = setup_inputs


def setup_inputs(seed=0):
    import zlib

    import numpy as np

    out = dict(_drawn_inputs(seed))
    spreads = {}
    factors = {'norm_mix_2': 3.541,
     'rnn_conv_b_2': 23.264,
     'rg_b_a_2': 200.0,
     'rg_b_x_2': 64.0,
     'gla_b_decay_2': 21.751,
     'gla_norm_2': 8.0,
     'mem_norm_2': 8.0,
     'norm_ffn_2': 12.233,
     'ffn_conv_b_2': 24.776,
     'final_norm_2': 23.399}
    for name, (base, spread) in spreads.items():
        noise = np.random.default_rng([zlib.crc32(name.encode()), seed]).standard_normal(out[name].shape)
        drawn = base * np.exp(spread * noise) if base else spread * noise
        out[name] = __import__('jax').numpy.asarray(drawn.astype(out[name].dtype))
    for name, factor in factors.items():
        out[name] = (out[name] * factor).astype(out[name].dtype)
    return out
```

```python
from contextlib import ExitStack
import math

import numpy as np

import concourse.bass as bass
from concourse import mybir

F32 = mybir.dt.float32
U32 = mybir.dt.uint32
ALU = mybir.AluOpType
ACT = mybir.ActivationFunctionType
AX = mybir.AxisListType

P = 128
T = 256
TT = T // P
D = 1024
KD = D // P
EPS = 1e-6
NEG = -1e30
RING = 4
SLOT = 2048
CW = 256

CONV_W = 31
HEADS, HD = 16, 64
QB = T // P
PH, NK, DK, TOPK = 8, 128, 256, 16
HALVES = 2 * PH
CHOICES = PH * TOPK
LOWEST = -3.4e38
A_VAL, A_GATE, Q0, K0, V0 = 0, 1024, 2048, 3072, 4096
F0 = 5120
GA0, GB0 = F0 + HEADS, F0 + HEADS + D

MEM = 256
MW = 768
C96 = 96
K96 = MW // C96
RNN_CONV = 4
GH, GDK, GDV, LOW = 4, 96, 192, 16
GCHUNK = 64
NCH = T // GCHUNK
MH, MHD = 4, 192
DFF = 3072
KF = DFF // P
Z_RNN = 0
Z_Q = Z_RNN + MW
Z_K = Z_Q + GH * GDK
Z_V = Z_K + GH * GDK
Z_G = Z_V + MW
Z_DEC = Z_G + MW
Z_MQ = Z_DEC + LOW
Z_GATE = Z_MQ + MW

_VEC128 = ["norm1_g", "conv_b", "conv_ln_g", "conv_ln_b", "norm2_g", "normf_g",
           "norm_mix_2", "mem_norm_2", "norm_ffn_2", "final_norm_2"]
PCOL = {}
_at = 0
for _n in _VEC128:
    PCOL[_n] = _at
    _at += KD
for _n, _w in (("conv_w", KD * CONV_W), ("ffn_conv_w_2", 2 * KF * 3), ("ffn_conv_b_2", 2 * KF),
               ("fox_bf", 1), ("rnn_conv_w_2", K96 * RNN_CONV), ("rnn_conv_b_2", K96),
               ("rg_b_a_2", K96), ("rg_b_x_2", K96), ("rg_lambda_2", K96),
               ("gla_b_decay_2", GH), ("gla_norm_2", K96)):
    PCOL[_n] = _at
    _at += _w
NPAR = _at


class Chunk:

    def __init__(self, slot, use, bank_use):
        self.slot, self.use, self.bank_use = slot, use, bank_use


def plan_chunks():
    uses, bank_uses, n = [0] * RING, [0] * RING, 0
    plan = {}

    def section(name, count, banked=True):
        nonlocal n
        plan[name] = []
        for _ in range(count):
            s = n % RING
            n += 1
            uses[s] += 1
            bank_uses[s] += banked
            plan[name].append(Chunk(s, uses[s], bank_uses[s]))

    def align():
        nonlocal n
        n += -n % RING

    for j in range(4):
        section(f"conv_in{j}", 2)
    for name, count in (("f", 1), ("q", 4), ("k", 4), ("v", 4), ("ga", 4), ("gb", 4),
                        ("conv_out", 4), ("fox_out", 4), ("mix_out", 4), ("peer_q", 8)):
        section(name, count)
    section("keys", 1, banked=False)
    align()
    section("u", P // 2)
    section("ev", P // 2, banked=False)
    for name, count in (("mem_k", 4), ("mem_v", 3), ("z_rnn", 4), ("dec", 1), ("zq", 2), ("zk", 2),
                        ("zv", 3), ("gate0", 4), ("zg", 4), ("zmq", 4), ("branch0", 4), ("gate1", 4),
                        ("branch1", 4), ("gate2", 4), ("branch2", 4), ("out2", 4)):
        section(name, count)
    align()
    section("up", KF)
    section("down", 3 * 4, banked=False)
    return plan


def build(nc, t):
    plan = plan_chunks()
    ctx = ExitStack()
    with ctx:
        def sb(name, shape, dt=F32):
            return ctx.enter_context(nc.sbuf_tensor(name, shape, dt))

        def sem(name):
            return ctx.enter_context(nc.semaphore(name))

        gemm = [ctx.enter_context(nc.psum_tensor(f"gemm{i}", [P, 512], F32)) for i in range(RING)]
        aux = [ctx.enter_context(nc.psum_tensor(f"aux{i}", [P, 512], F32)) for i in range(4)]

        def pair(bank, rows=P):
            return bank[0:rows, :].rearrange("p (n t) -> p n t", n=2)

        ring = [sb(f"ring{i}", [P, SLOT]) for i in range(RING)]
        xres = sb("xres", [P, KD, T])
        hT = sb("hT", [P, KD, T])
        std = sb("std", [P, T])
        rstd = sb("rstd", [P, T])
        params = sb("params", [P, NPAR])
        ones = sb("ones", [P, P])
        ident = sb("ident", [P, P])
        zeros = sb("zeros", [P, P])
        iota = sb("iota", [P, P])
        keep = sb("keep", [P, T])
        epsc = sb("epsc", [P, 1])
        small = sb("small", [P, 12 * T])
        hots = sb("hots", [P, 8 * T])
        big = sb("big", [P, P * T])

        def carver(base, start=0):
            at = [start]

            def carve(*shape, rows=P, dt=F32):
                n = math.prod(shape)
                v = base[0:rows, at[0]:at[0] + n]
                at[0] += n
                assert at[0] <= base.shape[1], (at[0], shape)
                if dt != F32:
                    v = v.bitcast(dt)
                names = "abcd"[:len(shape)]
                if len(shape) == 1:
                    return v
                return v.rearrange(f"p ({' '.join(names)}) -> p {' '.join(names)}",
                                   **dict(zip(names, shape)))
            return carve

        carve = carver(big)
        PADC = CONV_W - 1
        sq = carve(KD, T)
        zc = carve(KD, PADC + T)
        zv = carve(KD, T)
        sig = carve(2, 2, T)
        qT = carve(KD, T)
        kT = carve(KD, T)
        vtok = carve(TT, D)
        fy, fa, fe, fl, fc, fc8 = [carve(T, rows=HEADS) for _ in range(6)]
        sel = carve(HEADS, P, rows=HEADS)
        mask = carve(T)
        s_sb = carve(2, T)
        p_sb = carve(2, T)
        pT_sb = carve(2, T)
        ob = carve(KD, T)
        ga = carve(KD, T)
        gb = carve(KD, T)
        nmax, rsum, rrec = [carve(HEADS * QB) for _ in range(3)]
        act_peer = big[:, :].rearrange("p (i t) -> p i t", t=T)
        carve = carver(big, 96 * T)
        qp = carve(HALVES, T)
        ks = carve(TT, HALVES, NK)
        carve = carver(big, 96 * T)
        cand = carve(PH, TOPK * TOPK)
        eq = carve(PH, TOPK, TOPK)
        carve = carver(small)
        topv = carve(PH, 2, TOPK)
        topi = carve(PH, 2, TOPK, dt=U32)
        topif = carve(PH, 2, TOPK)
        sc = carve(TT, PH, TOPK)
        pos = carve(PH, TOPK, dt=U32)
        posp = carve(2, PH, TOPK, dt=U32)
        posf = carve(2, PH, TOPK)
        e1 = carve(TT, PH, TOPK)
        e2 = carve(TT, PH, TOPK)
        gsum = carve(TT, PH)
        grec = carve(TT, PH)
        e1T, e2T, gT = [carve(T) for _ in range(3)]
        carve = carver(hots)
        hot1 = carve(2, 4, P)
        hot2 = carve(2, 4, P)
        carve = carver(big, KD * T)
        gate = carve(KD, T)
        merged = carve(KD, T)
        out_a = carve(K96, T, rows=C96)
        out_b = carve(K96, T, rows=C96)
        mk = carve(K96, T, rows=C96)
        mv = carve(TT, MW)
        memr = carve(KD, T)
        memT = carve(KD, T)
        zr = carve(K96, RNN_CONV - 1 + T, rows=C96)
        xr = carve(K96, T, rows=C96)
        states = carve(GH, NCH - 1, GDV, rows=GDK)
        zq = carve(GH, T, rows=GDK)
        zk = carve(GH, T, rows=GDK)
        vg = carve(TT, MW)
        eg = carve(GH, T, rows=GDK)
        emg = carve(GH, T, rows=GDK)
        kendT = carve(TT, GH, GDK)
        rwa = carve(K96, C96, rows=C96)
        rwx = carve(K96, C96, rows=C96)
        lam = [carve(K96, rows=C96) for _ in range(7)]
        decay = carve(GH, NCH, rows=GDK)
        mnm, msum, mrec = [carve(MH * QB) for _ in range(3)]
        rg = memr[0:C96]
        ig = memT[0:C96]
        ra = zr.rearrange("p a b -> p (a b)")[:, 0:K96 * T].rearrange("p (a b) -> p a b", b=T)
        rt = states.rearrange("p h n v -> p (h n v)")[:, 0:K96 * T].rearrange("p (a b) -> p a b", b=T)
        sg = xr
        mq = ig
        out_c = out_a
        carve = carver(small)
        gy = carve(GH, T, rows=GDK)
        gl = carve(GH, T, rows=GDK)
        ekd = gy
        carve = carver(small, 2 * GH * T)
        mp = carve(2, MEM)
        carve = carver(hots)
        sT = carve(GH, TT, GCHUNK)
        mpT = carve(TT, T)
        dec = carve(T, rows=LOW)
        wdec = carve(GH, GDK, rows=LOW)
        carve = carver(big, KD * T)
        ub = carve(2, 2, 2 + T)
        uc = carve(2, 2, T)
        ffa = carve(KF, T)
        yout = carve(KD, T)

        landed = [sem(f"landed{i}") for i in range(RING)]
        multiplied = [sem(f"multiplied{i}") for i in range(RING)]
        evacuated = [sem(f"evacuated{i}") for i in range(RING)]
        (x_in, params_in, consts, squared, sumsq, stdev, rstd_done, normed,
         dve_step, f_logit, f_abs, f_exp, f_soft, c_ready, conv_done, mean_ready, centered,
         ln_squared, ln_sumsq, ln_std, ln_scaled, ln_sig, conv_act, gates_on,
         scores_ready, scores_moved, negmax_ready, exp_done, probs_ready, pT_psum, pT_ready, pv_done,
         ob_ready, mix_ready) = [sem(n) for n in (
             "x_in params_in consts squared sumsq stdev rstd_done normed "
             "dve_step f_logit f_abs f_exp f_soft c_ready conv_done mean_ready centered "
             "ln_squared ln_sumsq ln_std ln_scaled ln_sig conv_act gates_on "
             "scores_ready scores_moved negmax_ready exp_done probs_ready pT_psum pT_ready pv_done "
             "ob_ready mix_ready").split()]
        (keys_scored, keys_moved, topk_done, gate_exp, gates_ready, routed_psum, routed,
         x2_done, experts_done) = [sem(n) for n in (
             "keys_scored keys_moved topk_done gate_exp gates_ready routed_psum routed "
             "x2_done experts_done").split()]
        hots_ready = [sem(f"hots_ready{b}") for b in range(2)]
        planes_ready = [sem(f"planes_ready{b}") for b in range(2)]
        planes_used = [sem(f"planes_used{b}") for b in range(2)]
        (mem_in, rg_in, wdec_in, pads2, rnn_conv, rg_psum, rg_moved, lam_abs, lam_exp, lam_ln, lam_ready,
         la_ready, a_ready, tanh_ready, w_ready, root_ready, ig_used, rnn_done,
         dec_psum, gla_y, gla_abs, gla_soft, gla_sum, gla_exp, gla_qk, kend_psum, kend_moved,
         gla_scored, gla_scores_moved, gla_masked, states_psum, states_done, o_psum, o_moved, o_squared,
         o_sumsq, o_std, out_b_done, sg_sig,
         ms_psum, ms_max, ms_exp, ms_probs, mpT_psum, mpT_moved, mo_psum, mo_moved, merge_done,
         ffn_pads, ffn_conv, ffn_gelu, ffn_act, down_done, x4_done, stored) = [sem(n) for n in (
             "mem_in rg_in wdec_in pads2 rnn_conv rg_psum rg_moved lam_abs lam_exp lam_ln lam_ready "
             "la_ready a_ready tanh_ready w_ready root_ready ig_used rnn_done "
             "dec_psum gla_y gla_abs gla_soft gla_sum gla_exp gla_qk kend_psum kend_moved "
             "gla_scored gla_scores_moved gla_masked states_psum states_done o_psum o_moved o_squared "
             "o_sumsq o_std out_b_done sg_sig "
             "ms_psum ms_max ms_exp ms_probs mpT_psum mpT_moved mo_psum mo_moved merge_done "
             "ffn_pads ffn_conv ffn_gelu ffn_act down_done x4_done stored").split()]
        N_CONSTS = 12

        def par(name, col=0, rows=P, n=1):
            c = PCOL[name] + col
            return params[0:rows, c:c + n]

        def weights(slot, n, rows=P):
            return ring[slot][0:rows, 0:8 * n].rearrange("p (k n) -> p k n", n=n)

        def taken(eng, c):
            eng.wait_ge(multiplied[c.slot], c.use)

        def moved(eng, chunks):
            for s in sorted({c.slot for c in chunks}):
                eng.wait_ge(evacuated[s], max(c.bank_use for c in chunks if c.slot == s))

        block = ctx.enter_context(nc.Block())

        @block.sync
        def _(sp):
            sp.dma_start(xres[:, :, :], t["xT"].rearrange("(k p) t -> p k t", p=P)).then_inc(x_in, 16)
            sp.dma_start(params[:, :], t["params"]).then_inc(params_in, 16)

            def load(c, dst, src):
                if c.use > 1:
                    sp.wait_ge(multiplied[c.slot], c.use - 1)
                sp.dma_start(dst, src).then_inc(landed[c.slot], 16)

            def columns(name, w, first, n, rows=P):
                for i, c in enumerate(plan[name]):
                    cols = w[:, first + i * n:first + (i + 1) * n]
                    load(c, weights(c.slot, n, rows), cols.rearrange("(k p) n -> p k n", p=rows))

            w_in = t["w_in"]
            for j in range(4):
                for c, first in zip(plan[f"conv_in{j}"], (A_GATE, A_VAL)):
                    cols = w_in[:, first + j * CW:first + (j + 1) * CW]
                    load(c, weights(c.slot, CW), cols.rearrange("(k p) n -> p k n", p=P))
            columns("f", w_in, F0, HEADS)
            columns("q", w_in, Q0, CW)
            columns("k", w_in, K0, CW)
            columns("v", w_in, V0, CW)
            columns("ga", w_in, GA0, CW)
            columns("gb", w_in, GB0, CW)
            columns("conv_out", t["w_conv_out"], 0, CW)
            columns("fox_out", t["w_fox_out"], 0, CW)
            columns("mix_out", t["w_out"], 0, CW)
            columns("peer_q", t["peer_wq"], 0, CW)
            kc = plan["keys"][0]
            load(kc, ring[kc.slot][:, :], t["keys"])
            for name, w in (("u", t["uT"]), ("ev", t["peer_v"])):
                base = [c.use - 1 for c in plan[name][:RING]]
                with sp.Fori(0, P // (2 * RING)) as it:
                    for s in range(RING):
                        sp.wait_ge(multiplied[s], it + base[s])
                        sp.dma_start(ring[s][:, :].rearrange("p (i d) -> p i d", i=2),
                                     w[bass.ds(it * 2 * RING + 2 * s, 2), :, :].rearrange("i p d -> p i d")
                                     ).then_inc(landed[s], 16)
            columns("mem_k", t["w_mem_kv_2"], 0, 2 * C96)
            columns("mem_v", t["w_mem_kv_2"], MW, CW)
            w_in2 = t["w_in_2"]
            columns("z_rnn", w_in2, Z_RNN, 2 * C96)
            columns("dec", w_in2, Z_DEC, LOW)
            columns("zq", w_in2, Z_Q, 2 * C96)
            columns("zk", w_in2, Z_K, 2 * C96)
            columns("zv", w_in2, Z_V, CW)
            columns("gate0", w_in2, Z_GATE, CW)
            columns("zg", w_in2, Z_G, 2 * C96)
            columns("zmq", w_in2, Z_MQ, 2 * C96)
            columns("branch0", t["w_branch_2"][0], 0, CW, C96)
            columns("gate1", w_in2, Z_GATE + D, CW)
            columns("branch1", t["w_branch_2"][1], 0, CW, C96)
            columns("gate2", w_in2, Z_GATE + 2 * D, CW)
            columns("branch2", t["w_branch_2"][2], 0, CW, C96)
            columns("out2", t["w_out_2"], 0, CW)
            base = [c.use - 1 for c in plan["up"][:RING]]
            up = t["w_up_2"].rearrange("(k p) (v n) -> p v k n", p=P, v=2)
            with sp.Fori(0, KF // RING) as it:
                for s in range(RING):
                    sp.wait_ge(multiplied[s], it + base[s])
                    sp.dma_start(ring[s][:, :].rearrange("p (v k n) -> p v k n", v=2, k=KD),
                                 up[:, :, :, bass.ds((it * RING + s) * P, P)]).then_inc(landed[s], 16)
            for i, c in enumerate(plan["down"]):
                pr, g = divmod(i, 3)
                rows = t["w_down_2"][g * D:(g + 1) * D, pr * CW:(pr + 1) * CW]
                load(c, weights(c.slot, CW), rows.rearrange("(k p) n -> p k n", p=P))
            sp.wait_ge(normed, 7)
            sp.dma_start(t["yT"].rearrange("(k p) t -> p k t", p=P), yout[:, :, :]).then_inc(stored, 16)
            sp.wait_ge(stored, 16)

        @block.gpsimd
        def _(pool):
            pool.memset(ones[:, :], 1.0).then_inc(consts, 1)
            pool.memset(zeros[:, :], 0.0).then_inc(consts, 1)
            pool.memset(epsc[:, :], EPS).then_inc(consts, 1)
            pool.memset(zc[:, :, 0:PADC], 0.0).then_inc(consts, 1)
            pool.iota(iota[:, :], [[1, P]], base=0, channel_multiplier=0,
                      allow_small_or_imprecise_dtypes=True).then_inc(consts, 1)
            pool.memset(ident[:, :], 0.0).then_inc(consts, 1)
            pool.memset(mask, 0.0).then_inc(consts, 1)
            pool.memset(sel, 0.0).then_inc(consts, 1)
            pool.memset(keep[:, :], 1.0).then_inc(consts, 1)
            pool.wait_ge(consts, 9)
            pool.memset(keep[:, :].rearrange("p (n i) -> p n i", i=GCHUNK)[:, :, 0:1], 0.0).then_inc(consts, 1)
            pool.affine_select(out=ident[:, :], in_=ident[:, :], compare_op=ALU.not_equal, fill=1.0,
                               base=0, pattern=[[-1, P]], channel_multiplier=1)
            pool.affine_select(out=sel, in_=sel, compare_op=ALU.not_equal, fill=1.0, base=0,
                               pattern=[[-1, HEADS], [0, P]], channel_multiplier=1).then_inc(consts, 1)
            pool.affine_select(out=mask[:, P:T], in_=mask[:, P:T], compare_op=ALU.is_ge, fill=NEG, base=0,
                               pattern=[[-1, P]], channel_multiplier=1).then_inc(consts, 1)
            pool.wait_ge(x2_done, 1)
            pool.dma_start(memr, t["memT"].rearrange("(k p) t -> p k t", p=P)).then_inc(mem_in, 16)
            pool.dma_start(rwa, t["rg_w_a_2"].rearrange("h i j -> i h j")).then_inc(rg_in, 16)
            pool.dma_start(rwx, t["rg_w_x_2"].rearrange("h i j -> i h j")).then_inc(rg_in, 16)
            pool.dma_start(wdec, t["gla_w_decay_2"].rearrange("l (h d) -> l h d", h=GH)).then_inc(wdec_in, 16)
            pool.memset(zr[:, :, 0:RNN_CONV - 1], 0.0).then_inc(pads2, 1)
            pool.wait_ge(gla_scores_moved, 1)
            for hp in range(2):
                part = sT[hp * GCHUNK:(hp + 1) * GCHUNK].rearrange("p h n i -> p (h n) i")
                pool.affine_select(out=part, in_=part, compare_op=ALU.is_ge, fill=0.0, base=0,
                                   pattern=[[0, GH * TT], [1, GCHUNK]], channel_multiplier=-1
                                   ).then_inc(gla_masked, 1)
            pool.wait_ge(normed, 6)
            pool.memset(ub[:, :, :, 0:2], 0.0).then_inc(ffn_pads, 1)

        @block.tensor
        def _(pe):
            def product(c, m, src, rows=P, ready=None):
                pe.wait_ge(landed[c.slot], 16 * c.use)
                if c.bank_use > 1:
                    pe.wait_ge(evacuated[c.slot], c.bank_use - 1)
                w = weights(c.slot, 2 * m, rows)
                for n in range(2):
                    for k in range(KD):
                        mm = pe.matmul(pair(gemm[c.slot], m)[:, n, :], w[:, k, n * m:(n + 1) * m],
                                       src[:, k, :], start=(k == 0), stop=(k == KD - 1))
                mm.then_inc(multiplied[c.slot], 1)

            def narrow(c, m, src):
                pe.wait_ge(landed[c.slot], 16 * c.use)
                pe.wait_ge(evacuated[c.slot], c.bank_use - 1)
                w = weights(c.slot, m)
                for k in range(KD):
                    mm = pe.matmul(gemm[c.slot][0:m, 0:T], w[:, k, :], src[:, k, :],
                                   start=(k == 0), stop=(k == KD - 1))
                mm.then_inc(multiplied[c.slot], 1)

            def product_by_token(c, src):
                pe.wait_ge(landed[c.slot], 16 * c.use)
                pe.wait_ge(evacuated[c.slot], c.bank_use - 1)
                w = weights(c.slot, CW)
                for tt in range(TT):
                    for k in range(KD):
                        mm = pe.matmul(pair(gemm[c.slot])[:, tt, :], src[:, k, tt * P:(tt + 1) * P],
                                       w[:, k, :], start=(k == 0), stop=(k == KD - 1))
                mm.then_inc(multiplied[c.slot], 1)

            def sum_squares(i):
                for k in range(KD):
                    if k % 4 == 0:
                        pe.wait_ge(squared, 2 * i + k // 4 + 1)
                    mm = pe.matmul(aux[3][:, 0:T], ones[:, :], sq[:, k, :], start=(k == 0), stop=(k == KD - 1))
                mm.then_inc(sumsq, 1)

            pe.wait_ge(consts, N_CONSTS)
            sum_squares(0)
            pe.wait_ge(normed, 1)
            for j in range(4):
                for c in plan[f"conv_in{j}"]:
                    product(c, P, hT)
            narrow(plan["f"][0], HEADS, hT)
            for c in plan["q"] + plan["k"]:
                product(c, P, hT)
            for c in plan["v"]:
                product_by_token(c, hT)
            pe.wait_ge(conv_done, 1)
            for k in range(KD):
                mm = pe.matmul(aux[2][:, 0:T], ones[:, :], zv[:, k, :], start=(k == 0), stop=(k == KD - 1))
            mm.then_inc(mean_ready, 1)
            product(plan["ga"][0], P, hT)
            product(plan["ga"][1], P, hT)
            pe.wait_ge(ln_squared, 2)
            for k in range(KD):
                mm = pe.matmul(aux[3][:, 0:T], ones[:, :], sq[:, k, :], start=(k == 0), stop=(k == KD - 1))
            mm.then_inc(ln_sumsq, 1)
            for c in plan["ga"][2:] + plan["gb"]:
                product(c, P, hT)

            def scores(u):
                h, qb = divmod(u, QB)
                lo, nk = (h % 2) * HD, (qb + 1) * P
                if u >= 2:
                    pe.wait_ge(scores_moved, u - 1)
                pe.matmul(aux[u % 2][:, 0:nk], qT[lo:lo + HD, h // 2, qb * P:(qb + 1) * P],
                          kT[lo:lo + HD, h // 2, 0:nk], start=True, stop=False)
                pe.matmul(aux[u % 2][:, 0:nk], sel[:, h, :], fc8[:, 0:nk],
                          start=False, stop=True).then_inc(scores_ready, 1)

            def turn_probs(u):
                qb = u % QB
                pe.wait_ge(probs_ready, u + 1)
                if u >= 1:
                    pe.wait_ge(pT_ready, u)
                for kb in range(qb + 1):
                    mm = pe.transpose(aux[2][:, kb * P:(kb + 1) * P], p_sb[:, u % 2, kb * P:(kb + 1) * P],
                                      ident[:, :])
                mm.then_inc(pT_psum, 1)

            def values(u):
                h, qb = divmod(u, QB)
                lo = (h % 2) * HD
                pe.wait_ge(pT_ready, u + 1)
                if u % 4 == 0 and u:
                    pe.wait_ge(ob_ready, u // 4)
                for kb in range(qb + 1):
                    mm = pe.matmul(aux[3][lo:lo + HD, qb * P:(qb + 1) * P], vtok[:, kb, h * HD:(h + 1) * HD],
                                   pT_sb[:, u % 2, kb * P:(kb + 1) * P], start=(kb == 0), stop=(kb == qb))
                mm.then_inc(pv_done, 1)

            moved(pe, plan["q"] + plan["k"] + plan["v"])
            pe.wait_ge(c_ready, 1)
            pe.wait_ge(ln_std, 1)
            UNITS = HEADS * QB
            for u in range(UNITS + 3):
                if u < UNITS:
                    scores(u)
                if 2 <= u < UNITS + 2:
                    turn_probs(u - 2)
                if u >= 3:
                    values(u - 3)
                if u == 6:
                    pe.wait_ge(conv_act, 1)
                if u >= 6 and u % 6 == 0 and u // 6 <= 4:
                    product(plan["conv_out"][u // 6 - 1], P, zv)
            pe.wait_ge(ob_ready, KD)
            for c in plan["fox_out"]:
                product(c, P, ob)
            pe.wait_ge(mix_ready, 4)
            for c in plan["mix_out"]:
                product(c, P, ga)

            sum_squares(1)
            pe.wait_ge(normed, 2)
            for c in plan["peer_q"]:
                product(c, P, hT)
            kc = plan["keys"][0]
            pe.wait_ge(landed[kc.slot], 16 * kc.use)
            moved(pe, plan["peer_q"])
            keys = ring[kc.slot][:, :].rearrange("p (h n) -> p h n", h=HALVES)
            for g in range(TT * 4):
                tt, h0 = divmod(4 * g, HALVES)
                if g >= 4:
                    pe.wait_ge(keys_moved, g - 3)
                for i in range(4):
                    mm = pe.matmul(aux[g % 4][:, i * NK:(i + 1) * NK], qp[:, h0 + i, tt * P:(tt + 1) * P],
                                   keys[:, h0 + i, :], start=True, stop=True)
                mm.then_inc(keys_scored, 1)
            pe.wait_ge(keys_scored, TT * 4)
            pe.sem_inc(multiplied[kc.slot], 1)

            def expert_scores(first, last):
                base = [(c.use - 1, c.bank_use - 1) for c in plan["u"][:RING]]
                with pe.Fori(first, last) as it:
                    for s in range(RING):
                        use, bank_use = base[s]
                        pe.wait_ge(landed[s], it * 16 + 16 * (use + 1))
                        pe.wait_ge(evacuated[s], it + bank_use)
                        w = ring[s][:, :].rearrange("p (i k j) -> p i k j", i=2, k=KD)
                        for i in range(2):
                            for k in range(KD):
                                mm = pe.matmul(pair(gemm[s])[:, i, :], w[:, i, k, :], hT[:, k, :],
                                               start=(k == 0), stop=(k == KD - 1))
                        mm.then_inc(multiplied[s], 1)

            ITS = P // (2 * RING)
            expert_scores(0, ITS // 2)
            pe.wait_ge(gates_ready, 1)
            for n, src in enumerate((e1, e2, sc)):
                for tt in range(TT):
                    mm = pe.transpose(aux[n][:, tt * P:(tt + 1) * P],
                                      src[:, tt].rearrange("p h k -> p (h k)"), ident[:, :])
                mm.then_inc(routed_psum, 1)
            expert_scores(ITS // 2, ITS)
            with pe.Fori(0, T // 8) as it:
                for b in range(2):
                    pe.wait_ge(hots_ready[b], it + 1)
                    for n in range(4):
                        mm = pe.matmul(aux[b][:, n * P:(n + 1) * P], hot2[:, b, n, :], hot1[:, b, n, :],
                                       start=True, stop=True)
                    mm.then_inc(planes_ready[b], 1)
            for b in range(2):
                pe.wait_ge(planes_used[b], T // 8)
            for b in range(4):
                pe.matmul(aux[b][:, :], zeros[:, :],
                          zeros[:, :].unsqueeze(1).to_broadcast([P, 4, P]), start=True, stop=False,
                          skip_group_check=True)
            base = [c.use for c in plan["ev"][:RING]]
            with pe.Fori(0, ITS) as it:
                for s in range(RING):
                    pe.wait_ge(landed[s], it * 16 + 16 * base[s])
                    for i in range(2):
                        for d in range(KD):
                            mm = pe.matmul(pair(aux[d // 2])[:, d % 2, :],
                                           ring[s][:, i * D + d * P:i * D + (d + 1) * P],
                                           act_peer[:, bass.ds(it * 2 * RING + (2 * s + i), 1), :],
                                           start=False, stop=False, skip_group_check=True)
                    mm.then_inc(multiplied[s], 1)
            for b in range(4):
                mm = pe.matmul(aux[b][:, :], zeros[:, :],
                               zeros[:, :].unsqueeze(1).to_broadcast([P, 4, P]), start=False, stop=True,
                               skip_group_check=True)
            mm.then_inc(experts_done, 1)

            pe.wait_ge(x2_done, 1)
            sum_squares(2)
            pe.wait_ge(normed, 3)
            for c in plan["mem_k"]:
                product(c, C96, memT)
            sum_squares(3)
            for c in plan["mem_v"]:
                product_by_token(c, memT)
            sum_squares(4)
            pe.wait_ge(normed, 5)
            for c in plan["z_rnn"]:
                product(c, C96, hT)
            narrow(plan["dec"][0], LOW, hT)
            for c in plan["zq"] + plan["zk"]:
                product(c, C96, hT)
            for c in plan["zv"]:
                product_by_token(c, hT)
            moved(pe, plan["dec"])
            pe.wait_ge(wdec_in, 16)
            for h in range(GH):
                mm = pe.matmul(pair(aux[h // 2], GDK)[:, h % 2, :], wdec[:, h, :], dec, start=True, stop=True)
            mm.then_inc(dec_psum, 1)
            pe.wait_ge(rnn_conv, K96)
            pe.wait_ge(rg_in, 32)
            for h in range(K96):
                if h >= 2:
                    pe.wait_ge(rg_moved, 2 * (h - 1))
                bank = pair(aux[2 + h % 2], C96)
                pe.matmul(bank[:, 0, :], rwa[:, h, :], xr[:, h, :], start=True, stop=True)
                pe.matmul(bank[:, 1, :], rwx[:, h, :], xr[:, h, :], start=True, stop=True).then_inc(rg_psum, 1)
            for c in plan["gate0"]:
                product(c, P, hT)
            pe.wait_ge(gla_qk, 3)
            pe.wait_ge(gla_y, GH)
            for tt in range(TT):
                for h in range(GH):
                    mm = pe.transpose(aux[tt][:, h * GDK:(h + 1) * GDK], ekd[:, h, tt * P:(tt + 1) * P],
                                      ident[0:GDK, 0:GDK])
                mm.then_inc(kend_psum, 1)
            pe.wait_ge(rg_moved, 2 * K96)
            for h in range(GH):
                for n in range(NCH):
                    lo, cols = (n % 2) * GCHUNK, slice(n * GCHUNK, (n + 1) * GCHUNK)
                    at_col = (h * TT + n // 2) * GCHUNK
                    mm = pe.matmul(aux[2][lo:lo + GCHUNK, at_col:at_col + GCHUNK], emg[:, h, cols],
                                   eg[:, h, cols], start=True, stop=True)
            mm.then_inc(gla_scored, 1)
            for c in plan["zg"] + plan["zmq"]:
                product(c, C96, hT)
            pe.wait_ge(kend_moved, TT)
            moved(pe, plan["zv"])
            for n in range(NCH - 1):
                lo = (n % 2) * GCHUNK
                for half in range(2):
                    bank = aux[half if n % 2 == 0 else 2 + half]
                    if n == 1:
                        pe.wait_ge(gla_scores_moved, 1)
                    if n == 2:
                        pe.wait_ge(states_done, half + 1)
                    for i in range(2):
                        h = 2 * half + i
                        mm = pe.matmul(bank[0:GDK, i * GDV:(i + 1) * GDV],
                                       kendT[lo:lo + GCHUNK, n // 2, h, :],
                                       vg[lo:lo + GCHUNK, n // 2, h * GDV:(h + 1) * GDV],
                                       start=True, stop=True)
                    mm.then_inc(states_psum, 1)
            pe.wait_ge(rnn_done, 1)
            for c in plan["branch0"]:
                product(c, P, out_a, C96)
            pe.wait_ge(gla_masked, 2)
            pe.wait_ge(states_done, 2 + GH * (NCH - 2))
            def gla_out(h):
                for parity in range(2):
                    lo = parity * GCHUNK
                    bank = aux[2 * (h % 2) + parity][0:C96, 0:T].rearrange("p (v n i) -> p v n i", v=2, n=TT)
                    if h >= 2 and parity == 0:
                        pe.wait_ge(o_std, h - 1)
                    for vh in range(2):
                        vcols = slice(h * GDV + vh * C96, h * GDV + (vh + 1) * C96)
                        for half in range(TT):
                            n = 2 * half + parity
                            cols = slice(n * GCHUNK, (n + 1) * GCHUNK)
                            mm = pe.matmul(bank[:, vh, half, :], vg[lo:lo + GCHUNK, half, vcols],
                                           sT[lo:lo + GCHUNK, h, half, :], start=True, stop=(n == 0))
                            if n:
                                mm = pe.matmul(bank[:, vh, half, :], states[:, h, n - 1, vh * C96:(vh + 1) * C96],
                                               eg[:, h, cols], start=False, stop=True)
                    mm.then_inc(o_psum, 1)

            def gla_sumsq(h):
                pe.wait_ge(o_squared, 2 * h + 2)
                for vh in range(2):
                    mm = pe.matmul(aux[2 * (h % 2)][0:C96, 0:T], ones[0:C96, 0:C96], sq[0:C96, 2 * h + vh, :],
                                   start=(vh == 0), stop=(vh == 1))
                mm.then_inc(o_sumsq, 1)

            for h0 in range(0, GH, 2):
                for stage in (gla_out, gla_sumsq):
                    stage(h0)
                    stage(h0 + 1)

            def mem_scores(u):
                h, qb = divmod(u, QB)
                if u >= 2:
                    pe.wait_ge(ms_exp, u - 1)
                for vh in range(2):
                    mm = pe.matmul(aux[u % 2][:, 0:MEM], mq[:, 2 * h + vh, qb * P:(qb + 1) * P],
                                   mk[:, 2 * h + vh, :], start=(vh == 0), stop=(vh == 1))
                mm.then_inc(ms_psum, 1)

            def mem_turn(u):
                pe.wait_ge(ms_probs, u + 1)
                if u:
                    pe.wait_ge(mpT_moved, u)
                for mt in range(TT):
                    mm = pe.transpose(aux[2][:, mt * P:(mt + 1) * P], mp[:, u % 2, mt * P:(mt + 1) * P],
                                      ident[:, :])
                mm.then_inc(mpT_psum, 1)

            def mem_values(h):
                pe.wait_ge(mpT_moved, 2 * h + 2)
                if h:
                    pe.wait_ge(mo_moved, h)
                for vh in range(2):
                    for mt in range(TT):
                        mm = pe.matmul(pair(aux[3], C96)[:, vh, :],
                                       mv[:, mt, h * MHD + vh * C96:h * MHD + (vh + 1) * C96],
                                       mpT[:, mt, :], start=(mt == 0), stop=(mt == TT - 1))
                mm.then_inc(mo_psum, 1)

            pe.wait_ge(o_std, GH)
            moved(pe, plan["zmq"] + plan["mem_k"] + plan["mem_v"])
            for u in range(MH * QB + 1):
                if u < MH * QB:
                    mem_scores(u)
                if u % 2 == 0 and u < MH * QB:
                    product(plan["gate1"][u // 2], P, hT)
                if u:
                    mem_turn(u - 1)
                if u and u % 2 == 0:
                    mem_values(u // 2 - 1)
            pe.wait_ge(out_b_done, 1)
            for c in plan["branch1"]:
                product(c, P, out_b, C96)
            for c in plan["gate2"]:
                product(c, P, hT)
            pe.wait_ge(mo_moved, MH)
            for c in plan["branch2"]:
                product(c, P, out_c, C96)
            pe.wait_ge(merge_done, 8)
            for c in plan["out2"]:
                product(c, P, merged)

            sum_squares(5)
            pe.wait_ge(normed, 6)
            base = [(c.use - 1, c.bank_use - 1) for c in plan["up"][:RING]]
            with pe.Fori(0, KF // RING) as it:
                for s in range(RING):
                    use, bank_use = base[s]
                    pe.wait_ge(landed[s], it * 16 + 16 * (use + 1))
                    pe.wait_ge(evacuated[s], it + bank_use)
                    w = ring[s][:, :].rearrange("p (v k n) -> p v k n", v=2, k=KD)
                    for v in range(2):
                        for k in range(KD):
                            mm = pe.matmul(pair(gemm[s])[:, v, :], w[:, v, k, :], hT[:, k, :],
                                           start=(k == 0), stop=(k == KD - 1))
                    mm.then_inc(multiplied[s], 1)
            pe.wait_ge(ffn_act, KF)
            for i, c in enumerate(plan["down"]):
                pr, g = divmod(i, 3)
                pe.wait_ge(landed[c.slot], 16 * c.use)
                w = weights(c.slot, CW)
                for n in range(2):
                    for k in range(KD):
                        mm = pe.matmul(pair(aux[pr])[:, n, :], w[:, k, n * P:(n + 1) * P],
                                       ffa[:, g * KD + k, :], start=(g == 0 and k == 0 and n == 0),
                                       stop=(g == 2 and k == KD - 1), skip_group_check=True)
                mm.then_inc(multiplied[c.slot], 1)
            sum_squares(6)

        @block.scalar
        def _(act):
            def squares(i, src):
                for half in range(2):
                    part = slice(4 * half, 4 * half + 4)
                    act.activation(sq[:, part, :], src[:, part, :], ACT.Square).then_inc(squared, 1)

            def deviation(i):
                act.wait_ge(sumsq, i + 1)
                if i:
                    act.wait_ge(rstd_done, i)
                act.activation(std[:, :], aux[3][:, 0:T], ACT.Sqrt, bias=epsc[:, :],
                               scale=1.0 / D).then_inc(stdev, 1)

            def evacuate(c, out, src, func=ACT.Copy, **kw):
                taken(act, c)
                act.activation(out, src, func, **kw).then_inc(evacuated[c.slot], 1)

            act.wait_ge(x_in, 16)
            squares(0, xres)
            act.wait_ge(consts, N_CONSTS)
            deviation(0)
            for j in range(4):
                gc, vc = plan[f"conv_in{j}"]
                if j >= 2:
                    moved(act, plan[f"conv_in{j - 2}"][1:])
                evacuate(gc, sig[:, j % 2], pair(gemm[gc.slot]), ACT.Sigmoid)
            fchunk = plan["f"][0]
            act.wait_ge(params_in, 16)
            evacuate(fchunk, fy, gemm[fchunk.slot][0:HEADS, 0:T], ACT.Identity, bias=par("fox_bf", rows=HEADS))
            for i, c in enumerate(plan["q"]):
                evacuate(c, qT[:, 2 * i:2 * i + 2, :], pair(gemm[c.slot]))
            for i, c in enumerate(plan["k"]):
                evacuate(c, kT[:, 2 * i:2 * i + 2, :], pair(gemm[c.slot]))
            for i, c in enumerate(plan["v"]):
                evacuate(c, vtok[:, :, i * CW:(i + 1) * CW], pair(gemm[c.slot]))
            act.wait_ge(f_abs, 1)
            act.activation(fe, fa, ACT.Exp).then_inc(f_exp, 1)
            act.wait_ge(f_exp, 1)
            act.activation(fl, fe, ACT.Ln, bias=1.0).then_inc(f_soft, 1)
            def gate_raw(i):
                c = (plan["ga"] + plan["gb"])[i]
                dst = ga if i < 4 else gb
                evacuate(c, dst[:, 2 * (i % 4):2 * (i % 4) + 2, :], pair(gemm[c.slot]))

            gate_raw(0)
            act.wait_ge(centered, 1)
            for half in range(2):
                part = slice(4 * half, 4 * half + 4)
                act.activation(sq[:, part, :], zv[:, part, :], ACT.Square).then_inc(ln_squared, 1)
            gate_raw(1)
            act.wait_ge(ln_sumsq, 1)
            act.wait_ge(rstd_done, 1)
            act.activation(std[:, :], aux[3][:, 0:T], ACT.Sqrt, bias=epsc[:, :], scale=1.0 / D).then_inc(ln_std, 1)
            for i in range(2, 8):
                gate_raw(i)
            for k in range(KD):
                act.wait_ge(ln_scaled, k + 1)
                act.activation(sq[:, k, :], zv[:, k, :], ACT.Sigmoid, bias=par("conv_ln_b", k)).then_inc(ln_sig, 1)
            moved(act, plan["ga"] + plan["gb"])
            act.activation(ga, ga, ACT.Sigmoid).then_inc(gates_on, 1)
            act.activation(gb, gb, ACT.Sigmoid).then_inc(gates_on, 1)

            def exponent(u):
                nk = (u % QB + 1) * P
                act.wait_ge(negmax_ready, u + 1)
                if u >= 2:
                    act.wait_ge(pT_psum, u - 1)
                act.activation(p_sb[:, u % 2, 0:nk], s_sb[:, u % 2, 0:nk], ACT.Exp, bias=nmax[:, u:u + 1],
                               accum_out=rsum[:, u:u + 1]).then_inc(exp_done, 1)

            def copy_turned(u):
                nk = (u % QB + 1) * P
                act.wait_ge(pT_psum, u + 1)
                if u >= 2:
                    act.wait_ge(pv_done, u - 1)
                act.activation(pT_sb[:, u % 2, 0:nk], aux[2][:, 0:nk], ACT.Copy).then_inc(pT_ready, 1)

            UNITS = HEADS * QB
            for u in range(UNITS + 4):
                if u < UNITS:
                    exponent(u)
                if 2 <= u < UNITS + 2:
                    copy_turned(u - 2)
                if u >= 7 and u % 4 == 3:
                    i = (u - 7) // 4
                    act.wait_ge(pv_done, 4 * i + 4)
                    act.activation(ob[:, i, :], aux[3][:, 0:T], ACT.Copy).then_inc(ob_ready, 1)

            moved(act, plan["mix_out"])
            squares(1, xres)
            deviation(1)
            for i, c in enumerate(plan["peer_q"]):
                evacuate(c, qp[:, 2 * i:2 * i + 2, :], pair(gemm[c.slot]))
            for g in range(TT * 4):
                tt, h0 = divmod(4 * g, HALVES)
                act.wait_ge(keys_scored, g + 1)
                act.activation(ks[:, tt, h0:h0 + 4, :], aux[g % 4][:, :].rearrange("p (h n) -> p h n", h=4),
                               ACT.Copy).then_inc(keys_moved, 1)

            def gelus(first, last):
                base = [c.use for c in plan["u"][:RING]]
                with act.Fori(first, last) as it:
                    for s in range(RING):
                        act.wait_ge(multiplied[s], it + base[s])
                        act.activation(act_peer[:, bass.ds(it * 2 * RING + 2 * s, 2), :], pair(gemm[s]),
                                       ACT.Gelu_apprx_tanh).then_inc(evacuated[s], 1)

            ITS = P // (2 * RING)
            gelus(0, ITS // 2)
            act.wait_ge(topk_done, 1)
            act.activation(sc, sc, ACT.Exp).then_inc(gate_exp, 1)
            gelus(ITS // 2, ITS)

            act.wait_ge(mem_in, 16)
            squares(2, memr)
            deviation(2)
            act.wait_ge(x2_done, 1)
            squares(3, xres)
            for i, c in enumerate(plan["mem_k"]):
                evacuate(c, mk[:, 2 * i:2 * i + 2, :], pair(gemm[c.slot], C96))
            deviation(3)
            act.wait_ge(normed, 4)
            squares(4, xres)
            for i, c in enumerate(plan["mem_v"]):
                evacuate(c, mv[:, :, i * CW:(i + 1) * CW], pair(gemm[c.slot]))
            deviation(4)
            act.wait_ge(lam_abs, 1)
            act.activation(lam[1], lam[0], ACT.Exp).then_inc(lam_exp, 1)
            act.wait_ge(lam_exp, 1)
            act.activation(lam[2], lam[1], ACT.Ln, bias=1.0).then_inc(lam_ln, 1)
            act.wait_ge(pads2, 1)
            for i, c in enumerate(plan["z_rnn"]):
                evacuate(c, zr[:, 2 * i:2 * i + 2, RNN_CONV - 1:], pair(gemm[c.slot], C96))
            c = plan["dec"][0]
            evacuate(c, dec, gemm[c.slot][0:LOW, 0:T])
            for name, dst in (("zq", zq), ("zk", zk)):
                for i, c in enumerate(plan[name]):
                    evacuate(c, dst[:, 2 * i:2 * i + 2, :], pair(gemm[c.slot], GDK))
            for i, c in enumerate(plan["zv"]):
                evacuate(c, vg[:, :, i * CW:(i + 1) * CW], pair(gemm[c.slot]))
            act.wait_ge(dec_psum, 1)
            for h in range(GH):
                act.activation(gy[:, h, :], pair(aux[h // 2], GDK)[:, h % 2, :], ACT.Identity,
                               bias=par("gla_b_decay_2", h, GDK)).then_inc(gla_y, 1)
            act.wait_ge(gla_abs, 1)
            act.activation(eg, eg, ACT.Exp).then_inc(gla_soft, 1)
            act.wait_ge(gla_soft, 1)
            act.activation(emg, eg, ACT.Ln, bias=1.0).then_inc(gla_soft, 1)
            for h in range(K96):
                act.wait_ge(rg_psum, h + 1)
                bank = pair(aux[2 + h % 2], C96)
                act.activation(rg[:, h, :], bank[:, 0, :], ACT.Sigmoid, bias=par("rg_b_a_2", h, C96)).then_inc(rg_moved, 1)
                act.activation(ig[:, h, :], bank[:, 1, :], ACT.Sigmoid, bias=par("rg_b_x_2", h, C96)).then_inc(rg_moved, 1)
            for i, c in enumerate(plan["gate0"]):
                evacuate(c, gate[:, 2 * i:2 * i + 2, :], pair(gemm[c.slot]), ACT.Sigmoid)
            act.wait_ge(gla_sum, 2)
            last = gl.rearrange("p h (n i) -> p (h n) i", i=GCHUNK)[:, :, GCHUNK - 1]
            act.activation(eg, gl, ACT.Exp, scale=1.0 / 16).then_inc(gla_exp, 1)
            act.activation(emg, gl, ACT.Exp, scale=-1.0 / 16).then_inc(gla_exp, 1)
            act.activation(ekd, gy, ACT.Exp, scale=1.0 / 16).then_inc(gla_exp, 1)
            act.activation(decay.rearrange("p h n -> p (h n)"), last, ACT.Exp, scale=1.0 / 16).then_inc(gla_exp, 1)
            act.wait_ge(la_ready, 1)
            act.activation(ra, rg, ACT.Exp).then_inc(a_ready, 1)
            act.wait_ge(a_ready, 1)
            act.activation(rg, rg, ACT.Tanh, scale=-1.0).then_inc(tanh_ready, 1)
            for tt in range(TT):
                act.wait_ge(kend_psum, tt + 1)
                act.activation(kendT[:, tt].rearrange("p h d -> p (h d)"), aux[tt][:, 0:GH * GDK],
                               ACT.Copy).then_inc(kend_moved, 1)
            act.wait_ge(gla_scored, 1)
            act.activation(sT, aux[2][:, :].rearrange("p (h n i) -> p h n i", h=GH, n=TT),
                           ACT.Copy).then_inc(gla_scores_moved, 1)
            act.wait_ge(w_ready, 1)
            act.activation(rg, rg, ACT.Sqrt).then_inc(root_ready, 1)
            act.wait_ge(ig_used, 1)
            for i, c in enumerate(plan["zg"]):
                taken(act, c)
                act.activation(sg[:, 2 * i:2 * i + 2, :], pair(gemm[c.slot], C96), ACT.Sigmoid).then_inc(sg_sig, 1)
            act.wait_ge(rnn_done, 1)
            for i, c in enumerate(plan["zmq"]):
                evacuate(c, mq[:, 2 * i:2 * i + 2, :], pair(gemm[c.slot], C96))
            def by_parity(tile, h, parity):
                return tile[0:C96, 2 * h:2 * h + 2, :].rearrange(
                    "p v (n q i) -> p v n q i", q=2, i=GCHUNK)[:, :, :, parity, :]

            for h0 in range(0, GH, 2):
                for h in (h0, h0 + 1):
                    for parity in range(2):
                        bank = aux[2 * (h % 2) + parity][0:C96, 0:T].rearrange("p (v n i) -> p v n i", v=2, n=TT)
                        act.wait_ge(o_psum, 2 * h + parity + 1)
                        act.activation(by_parity(out_b, h, parity), bank, ACT.Copy).then_inc(o_moved, 1)
                        act.activation(by_parity(sq, h, parity), bank, ACT.Square).then_inc(o_squared, 1)
                for h in (h0, h0 + 1):
                    act.wait_ge(o_sumsq, h + 1)
                    act.activation(eg[:, h, :], aux[2 * (h % 2)][0:C96, 0:T], ACT.Sqrt, bias=epsc[0:C96, :],
                                   scale=1.0 / GDV).then_inc(o_std, 1)

            def gate_evac(b, i):
                c = plan[f"gate{b}"][i]
                if b == 1:
                    moved(act, plan["branch0"][i:i + 1])
                else:
                    act.wait_ge(merge_done, i + 1)
                evacuate(c, gate[:, 2 * i:2 * i + 2, :], pair(gemm[c.slot]), ACT.Sigmoid)

            def mem_exp(u):
                act.wait_ge(ms_max, u + 1)
                if u >= 2:
                    act.wait_ge(mpT_psum, u - 1)
                act.activation(mp[:, u % 2, :], aux[u % 2][:, 0:MEM], ACT.Exp, bias=mnm[:, u:u + 1],
                               scale=MHD ** -0.5, accum_out=msum[:, u:u + 1]).then_inc(ms_exp, 1)

            def mem_copy(u):
                h, qb = divmod(u, QB)
                act.wait_ge(mpT_psum, u + 1)
                if qb == 0 and h:
                    act.wait_ge(mo_psum, h)
                act.activation(mpT[:, :, qb * P:(qb + 1) * P],
                               aux[2][:, 0:MEM].rearrange("p (m q) -> p m q", m=TT), ACT.Copy).then_inc(mpT_moved, 1)

            for u in range(MH * QB + 1):
                if u < MH * QB:
                    mem_exp(u)
                if u % 2 == 0 and u < MH * QB:
                    gate_evac(1, u // 2)
                if u:
                    mem_copy(u - 1)
                if u and u % 2 == 0:
                    h = u // 2 - 1
                    act.wait_ge(mo_psum, h + 1)
                    act.activation(out_c[:, 2 * h:2 * h + 2, :], pair(aux[3], C96), ACT.Copy).then_inc(mo_moved, 1)
            for i in range(4):
                gate_evac(2, i)
            moved(act, plan["out2"])
            squares(5, xres)
            deviation(5)
            act.wait_ge(ffn_pads, 1)
            base = [c.use for c in plan["up"][:RING]]
            with act.Fori(0, KF // RING) as it:
                for s in range(RING):
                    b = s % 2
                    act.wait_ge(multiplied[s], it + base[s])
                    act.activation(ub[:, b, :, 2:], pair(gemm[s]), ACT.Copy).then_inc(evacuated[s], 1)
                    act.wait_ge(ffn_conv, it * RING + (s + 1))
                    act.activation(uc[:, b, 0, :], uc[:, b, 0, :], ACT.Gelu_apprx_tanh).then_inc(ffn_gelu, 1)
            act.wait_ge(x4_done, 4)
            squares(6, xres)
            deviation(6)

        @block.vector
        def _(dve):
            count = [0]

            def step(ins):
                count[0] += 1
                ins.then_inc(dve_step, 1)

            def settle(behind=0):
                if count[0] > behind:
                    dve.wait_ge(dve_step, count[0] - behind)

            def normalise(i, src, dst, gain):
                dve.wait_ge(stdev, i + 1)
                dve.reciprocal(rstd[:, :], std[:, :]).then_inc(rstd_done, 1)
                dve.wait_ge(rstd_done, i + 1)
                for k in range(KD):
                    ins = dve.scalar_tensor_tensor(dst[:, k, :], src[:, k, :], par(gain, k), rstd[:, :],
                                                   ALU.mult, ALU.mult)
                ins.then_inc(normed, 1)

            def add_to_residual(name):
                for i, c in enumerate(plan[name]):
                    taken(dve, c)
                    part = xres[:, 2 * i:2 * i + 2, :]
                    dve.tensor_tensor(part, part, pair(gemm[c.slot]), ALU.add).then_inc(evacuated[c.slot], 1)

            dve.wait_ge(params_in, 16)
            normalise(0, xres, hT, "norm1_g")
            dve.wait_ge(consts, N_CONSTS)
            for j in range(4):
                gc, vc = plan[f"conv_in{j}"]
                taken(dve, vc)
                moved(dve, [gc])
                dve.tensor_tensor(zc[:, 2 * j:2 * j + 2, PADC:], pair(gemm[vc.slot]), sig[:, j % 2],
                                  ALU.mult).then_inc(evacuated[vc.slot], 1)
                moved(dve, [vc])
                for w in range(CONV_W):
                    for k in (2 * j, 2 * j + 1):
                        tap = par("conv_w", k * CONV_W + w)
                        if w == 0:
                            step(dve.tensor_scalar(zv[:, k, :], zc[:, k, 0:T], tap, par("conv_b", k),
                                                   ALU.mult, ALU.add))
                        else:
                            settle(1)
                            step(dve.scalar_tensor_tensor(zv[:, k, :], zc[:, k, w:w + T], tap, zv[:, k, :],
                                                          ALU.mult, ALU.add))
            settle()
            dve.tensor_copy(grec[0:1, 0, 0:1], ones[0:1, 0:1]).then_inc(conv_done, 1)
            moved(dve, plan["f"])
            dve.scalar_tensor_tensor(fa, fy, -1.0, fy, ALU.mult, ALU.min).then_inc(f_abs, 1)
            dve.wait_ge(f_soft, 1)
            step(dve.scalar_tensor_tensor(fa, fy, 0.0, fl, ALU.min, ALU.subtract))
            settle()
            step(dve.tensor_tensor_scan(fc, keep[0:HEADS, 1:2].to_broadcast([HEADS, T]), fa, 0.0, ALU.mult, ALU.add))
            settle()
            dve.tensor_scalar(fc8, fc, -math.sqrt(HD), None, ALU.mult).then_inc(c_ready, 1)
            dve.wait_ge(mean_ready, 1)
            for k in range(KD):
                ins = dve.scalar_tensor_tensor(zv[:, k, :], aux[2][:, 0:T], -1.0 / D, zv[:, k, :], ALU.mult, ALU.add)
            ins.then_inc(centered, 1)
            dve.wait_ge(ln_std, 1)
            step(dve.reciprocal(rstd[:, :], std[:, :]))
            settle()
            for k in range(KD):
                dve.scalar_tensor_tensor(zv[:, k, :], zv[:, k, :], par("conv_ln_g", k), rstd[:, :],
                                         ALU.mult, ALU.mult).then_inc(ln_scaled, 1)
            for k in range(KD):
                dve.wait_ge(ln_sig, k + 1)
                ins = dve.scalar_tensor_tensor(zv[:, k, :], zv[:, k, :], par("conv_ln_b", k), sq[:, k, :],
                                               ALU.add, ALU.mult)
            ins.then_inc(conv_act, 1)

            def move_scores(u):
                qb = u % QB
                nk = (qb + 1) * P
                dve.wait_ge(scores_ready, u + 1)
                if u >= 2:
                    dve.wait_ge(exp_done, u - 1)
                dve.scalar_tensor_tensor(s_sb[:, u % 2, 0:nk], aux[u % 2][:, 0:nk], HD ** -0.5,
                                         mask[:, T - nk:T], ALU.mult, ALU.add).then_inc(scores_moved, 1)
                dve.wait_ge(scores_moved, u + 1)
                dve.tensor_reduce(nmax[:, u:u + 1], s_sb[:, u % 2, 0:nk], AX.X, ALU.max,
                                  negate=True).then_inc(negmax_ready, 1)

            def divide(u):
                nk = (u % QB + 1) * P
                dve.wait_ge(exp_done, u + 1)
                step(dve.reciprocal(rrec[:, u:u + 1], rsum[:, u:u + 1]))
                settle()
                dve.tensor_scalar(p_sb[:, u % 2, 0:nk], p_sb[:, u % 2, 0:nk], rrec[:, u:u + 1], None,
                                  ALU.mult).then_inc(probs_ready, 1)

            UNITS = HEADS * QB
            for u in range(UNITS + 1):
                if u < UNITS:
                    move_scores(u)
                if u:
                    divide(u - 1)
                if u >= 7 and (u - 1) % 6 == 0 and (u - 1) // 6 <= 4:
                    i = (u - 1) // 6 - 1
                    c = plan["conv_out"][i]
                    taken(dve, c)
                    dve.wait_ge(gates_on, 2)
                    part = ga[:, 2 * i:2 * i + 2, :]
                    dve.tensor_tensor(part, part, pair(gemm[c.slot]), ALU.mult).then_inc(evacuated[c.slot], 1)
            for i, c in enumerate(plan["fox_out"]):
                taken(dve, c)
                a, b = ga[:, 2 * i:2 * i + 2, :], gb[:, 2 * i:2 * i + 2, :]
                dve.tensor_tensor(b, b, pair(gemm[c.slot]), ALU.mult).then_inc(evacuated[c.slot], 1)
                moved(dve, [c, plan["conv_out"][i]])
                dve.tensor_tensor(a, a, b, ALU.add).then_inc(mix_ready, 1)
            add_to_residual("mix_out")

            moved(dve, plan["mix_out"])
            normalise(1, xres, hT, "norm2_g")

            def best(outs, src):
                for v, i, s in outs:
                    step(dve.max(v[:, 0:8], s))
                for n, (v, i, s) in enumerate(outs):
                    settle(len(outs) - 1)
                    step(dve.max_index(i[:, 0:8], v[:, 0:8], s))
                for v, i, s in outs:
                    settle(len(outs) - 1)
                    step(dve.match_replace(s, v[:, 0:8], s, LOWEST))
                for v, i, s in outs:
                    settle(len(outs) - 1)
                    step(dve.max(v[:, 8:16], s))
                for v, i, s in outs:
                    settle(len(outs) - 1)
                    step(dve.max_index(i[:, 8:16], v[:, 8:16], s))

            for tt in range(TT):
                dve.wait_ge(keys_moved, 4 * tt + 4)
                if tt == 0:
                    dve.wait_ge(keys_moved, 8)
                for h in range(PH):
                    best([(topv[:, h, f], topi[:, h, f], ks[:, tt, 2 * h + f, :]) for f in range(2)], None)
                settle()
                step(dve.tensor_copy(topif, topi))
                step(dve.tensor_tensor(cand.rearrange("p h (a b) -> p h a b", a=TOPK),
                                       topv[:, :, 0].unsqueeze(3).to_broadcast([P, PH, TOPK, TOPK]),
                                       topv[:, :, 1].unsqueeze(2).to_broadcast([P, PH, TOPK, TOPK]), ALU.add))
                settle()
                for h in range(0, PH, 2):
                    best([(sc[:, tt, g], pos[:, g], cand[:, g]) for g in (h, h + 1)], None)
                settle()
                step(dve.tensor_scalar(posp[:, 0], pos, 4, None, ALU.logical_shift_right))
                step(dve.tensor_scalar(posp[:, 1], pos, TOPK - 1, None, ALU.bitwise_and))
                settle()
                step(dve.tensor_copy(posf, posp))
                settle()
                for f, e in ((0, e1), (1, e2)):
                    step(dve.tensor_tensor(eq, posf[:, f].unsqueeze(3).to_broadcast([P, PH, TOPK, TOPK]),
                                           iota[:, 0:TOPK].unsqueeze(1).unsqueeze(1).to_broadcast([P, PH, TOPK, TOPK]),
                                           ALU.is_equal))
                    settle()
                    step(dve.tensor_tensor(eq, eq, topif[:, :, f].unsqueeze(2).to_broadcast([P, PH, TOPK, TOPK]),
                                           ALU.mult))
                    settle()
                    step(dve.tensor_reduce(e[:, tt], eq, AX.X, ALU.add))
                    settle()
            for tt in range(TT):
                step(dve.tensor_copy(grec[:, tt], sc[:, tt, :, 0]))
            settle()
            for tt in range(TT):
                ins = dve.tensor_tensor(sc[:, tt], sc[:, tt], grec[:, tt].unsqueeze(2).to_broadcast([P, PH, TOPK]),
                                        ALU.subtract)
            ins.then_inc(topk_done, 1)
            dve.wait_ge(gate_exp, 1)
            step(dve.tensor_reduce(gsum.rearrange("p t h -> p (t h)"), sc.rearrange("p t h k -> p (t h) k"),
                                   AX.X, ALU.add))
            settle()
            step(dve.reciprocal(grec, gsum))
            settle()
            dve.tensor_tensor(sc.rearrange("p t h k -> p (t h) k"), sc.rearrange("p t h k -> p (t h) k"),
                              grec.rearrange("p t h -> p (t h)").unsqueeze(2).to_broadcast([P, TT * PH, TOPK]),
                              ALU.mult).then_inc(gates_ready, 1)
            for n, dst in enumerate((e1T, e2T, gT)):
                dve.wait_ge(routed_psum, n + 1)
                ins = dve.tensor_copy(dst, aux[n][:, 0:T])
            ins.then_inc(routed, 1)
            dve.wait_ge(routed, 1)
            moved(dve, plan["u"])
            with dve.Fori(0, T // 8) as it:
                for b in range(2):
                    for n in range(4):
                        tok = bass.ds(it * 8 + (4 * b + n), 1)
                        dve.tensor_scalar(hot1[:, b, n, :], iota[:, :], e1T[:, tok], gT[:, tok],
                                          ALU.is_equal, ALU.mult)
                        ins = dve.tensor_scalar(hot2[:, b, n, :], iota[:, :], e2T[:, tok], None, ALU.is_equal)
                    ins.then_inc(hots_ready[b], 1)
                for b in range(2):
                    dve.wait_ge(planes_ready[b], it + 1)
                    part = act_peer[:, :, bass.ds(it * 8 + 4 * b, 4)]
                    dve.tensor_tensor(part, part, aux[b][:, :].rearrange("p (t i) -> p i t", t=4),
                                      ALU.mult).then_inc(planes_used[b], 1)
            dve.wait_ge(experts_done, 1)
            for b in range(4):
                part = xres[:, 2 * b:2 * b + 2, :]
                ins = dve.tensor_tensor(part, part, pair(aux[b]), ALU.add)
            ins.then_inc(x2_done, 1)

            dve.wait_ge(x2_done, 1)
            dve.wait_ge(mem_in, 16)
            normalise(2, memr, memT, "mem_norm_2")
            normalise(3, xres, xres, "normf_g")
            dve.wait_ge(normed, 4)
            normalise(4, xres, hT, "norm_mix_2")
            lamv = par("rg_lambda_2", 0, C96, K96)
            dve.scalar_tensor_tensor(lam[0], lamv, -1.0, lamv, ALU.mult, ALU.min).then_inc(lam_abs, 1)
            dve.wait_ge(lam_ln, 1)
            step(dve.tensor_scalar(lam[3], lam[1], 1.0, 1.0, ALU.add, ALU.subtract))
            settle()
            step(dve.tensor_scalar(lam[4], lam[3], 0.0, None, ALU.is_equal))
            settle()
            step(dve.tensor_tensor(lam[3], lam[3], lam[4], ALU.add))
            step(dve.tensor_tensor(lam[2], lam[2], lam[4], ALU.add))
            settle()
            step(dve.reciprocal(lam[5], lam[3]))
            step(dve.tensor_tensor(lam[2], lam[2], lam[1], ALU.mult))
            settle()
            step(dve.tensor_tensor(lam[2], lam[2], lam[5], ALU.mult))
            settle()
            step(dve.scalar_tensor_tensor(lam[6], lamv, 0.0, lam[2], ALU.min, ALU.subtract))
            settle()
            dve.tensor_scalar(lam[6], lam[6], 8.0, None, ALU.mult).then_inc(lam_ready, 1)
            for h0 in range(0, K96, 2):
                moved(dve, [plan["z_rnn"][h0 // 2]])
                for w in range(RNN_CONV):
                    for h in (h0, h0 + 1):
                        tap = par("rnn_conv_w_2", h * RNN_CONV + w, C96)
                        if w == 0:
                            step(dve.tensor_scalar(xr[:, h, :], zr[:, h, 0:T], tap, par("rnn_conv_b_2", h, C96),
                                                   ALU.mult, ALU.add))
                            continue
                        settle(0 if w == RNN_CONV - 1 and h > h0 else 1)
                        ins = dve.scalar_tensor_tensor(xr[:, h, :], zr[:, h, w:w + T], tap, xr[:, h, :],
                                                       ALU.mult, ALU.add)
                        if w < RNN_CONV - 1:
                            step(ins)
                        else:
                            ins.then_inc(rnn_conv, 1)
            dve.wait_ge(gla_y, GH)
            dve.scalar_tensor_tensor(eg, gy, -1.0, gy, ALU.mult, ALU.min).then_inc(gla_abs, 1)
            dve.wait_ge(gla_soft, 2)
            step(dve.scalar_tensor_tensor(gy, gy, 0.0, emg, ALU.min, ALU.subtract))
            settle()
            for h in range(GH):
                ins = dve.tensor_tensor_scan(gl[:, h, :], keep[0:GDK, :], gy[:, h, :], 0.0, ALU.mult, ALU.add)
            ins.then_inc(gla_sum, 1)
            dve.wait_ge(gla_sum, 1)
            glc = gl.rearrange("p h (n i) -> p (h n) i", i=GCHUNK)
            dve.tensor_tensor(gy.rearrange("p h (n i) -> p (h n) i", i=GCHUNK),
                              glc[:, :, GCHUNK - 1:GCHUNK].to_broadcast([GDK, GH * NCH, GCHUNK]), glc,
                              ALU.subtract).then_inc(gla_sum, 1)
            dve.wait_ge(lam_ready, 1)
            dve.wait_ge(rg_moved, 2 * K96)
            dve.tensor_tensor(rg, rg, lam[6].unsqueeze(2).to_broadcast([C96, K96, T]), ALU.mult).then_inc(la_ready, 1)
            moved(dve, plan["zq"] + plan["zk"])
            dve.wait_ge(gla_exp, 3)
            dve.scalar_tensor_tensor(eg, zq, GDK ** -0.5, eg, ALU.mult, ALU.mult).then_inc(gla_qk, 1)
            dve.tensor_tensor(emg, zk, emg, ALU.mult).then_inc(gla_qk, 1)
            dve.tensor_tensor(ekd, zk, ekd, ALU.mult).then_inc(gla_qk, 1)
            step(dve.tensor_tensor(ig, ig, xr, ALU.mult))
            settle()
            dve.wait_ge(a_ready, 1)
            step(dve.tensor_tensor(rt, ra, ra, ALU.mult))
            settle()
            dve.wait_ge(tanh_ready, 1)
            dve.scalar_tensor_tensor(rg, rt, 1.0, rg, ALU.add, ALU.mult).then_inc(w_ready, 1)
            dve.wait_ge(root_ready, 1)
            dve.tensor_tensor(ig, ig, rg, ALU.mult).then_inc(ig_used, 1)
            dve.wait_ge(ig_used, 1)
            for h in range(K96):
                ins = dve.tensor_tensor_scan(out_a[:, h, :], ra[:, h, :], ig[:, h, :], 0.0, ALU.mult, ALU.add)
            ins.then_inc(rnn_done, 1)
            for i, c in enumerate(plan["zg"]):
                dve.wait_ge(sg_sig, i + 1)
                part = sg[:, 2 * i:2 * i + 2, :]
                dve.tensor_tensor(part, part, pair(gemm[c.slot], C96), ALU.mult).then_inc(evacuated[c.slot], 1)
            dve.wait_ge(gla_exp, 4)
            for n in range(NCH - 1):
                for half in range(2):
                    bank = aux[half if n % 2 == 0 else 2 + half]
                    dve.wait_ge(states_psum, 2 * n + half + 1)
                    if n == 0:
                        dve.tensor_copy(states[:, 2 * half:2 * half + 2, 0, :],
                                        bank[0:GDK, 0:2 * GDV].rearrange("p (h v) -> p h v", h=2)).then_inc(states_done, 1)
                        continue
                    for i in range(2):
                        h = 2 * half + i
                        dve.wait_ge(states_done, 2 if n == 1 else 2 + h + 1)
                        dve.scalar_tensor_tensor(states[:, h, n, :], states[:, h, n - 1, :], decay[:, h, n:n + 1],
                                                 bank[0:GDK, i * GDV:(i + 1) * GDV],
                                                 ALU.mult, ALU.add).then_inc(states_done, 1)

            def merge(b, i):
                c = plan[f"branch{b}"][i]
                m, g = merged[:, 2 * i:2 * i + 2, :], gate[:, 2 * i:2 * i + 2, :]
                taken(dve, c)
                moved(dve, [plan[f"gate{b}"][i]])
                if b == 0:
                    dve.tensor_tensor(m, g, pair(gemm[c.slot]), ALU.mult).then_inc(evacuated[c.slot], 1)
                    return
                dve.tensor_tensor(g, g, pair(gemm[c.slot]), ALU.mult).then_inc(evacuated[c.slot], 1)
                moved(dve, [c, plan["branch0"][i]])
                if b == 2:
                    dve.wait_ge(merge_done, i + 1)
                dve.tensor_tensor(m, m, g, ALU.add).then_inc(merge_done, 1)

            for i in range(4):
                merge(0, i)
            dve.wait_ge(o_std, GH)
            step(dve.reciprocal(eg, eg))
            settle()
            for h in range(GH):
                for vh in range(2):
                    k = 2 * h + vh
                    step(dve.scalar_tensor_tensor(out_b[:, k, :], out_b[:, k, :], par("gla_norm_2", k, C96),
                                                  eg[:, h, :], ALU.mult, ALU.mult))
            settle()
            moved(dve, plan["zg"])
            dve.tensor_tensor(out_b, out_b, sg, ALU.mult).then_inc(out_b_done, 1)

            def mem_max(u):
                dve.wait_ge(ms_psum, u + 1)
                step(dve.tensor_reduce(mnm[:, u:u + 1], aux[u % 2][:, 0:MEM], AX.X, ALU.max, negate=True))
                settle()
                dve.tensor_scalar(mnm[:, u:u + 1], mnm[:, u:u + 1], MHD ** -0.5, None, ALU.mult).then_inc(ms_max, 1)

            def mem_divide(u):
                dve.wait_ge(ms_exp, u + 1)
                step(dve.reciprocal(mrec[:, u:u + 1], msum[:, u:u + 1]))
                settle()
                dve.tensor_scalar(mp[:, u % 2, :], mp[:, u % 2, :], mrec[:, u:u + 1], None, ALU.mult).then_inc(ms_probs, 1)

            for u in range(MH * QB + 1):
                if u < MH * QB:
                    mem_max(u)
                if u:
                    mem_divide(u - 1)
            for b in (1, 2):
                for i in range(4):
                    merge(b, i)
            add_to_residual("out2")
            moved(dve, plan["out2"])

            normalise(5, xres, hT, "norm_ffn_2")
            dve.wait_ge(ffn_pads, 1)
            base = [c.bank_use for c in plan["up"][:RING]]
            b0 = count[0]
            with dve.Fori(0, KF // RING) as it:
                n = 0
                for s in range(RING):
                    b = s % 2
                    dve.wait_ge(evacuated[s], it + base[s])
                    for w in range(3):
                        for v in range(2):
                            j = it * RING + (s + v * KF)
                            tap = params[:, bass.ds(j * 3 + (PCOL["ffn_conv_w_2"] + w), 1)]
                            if w == 0:
                                bias = params[:, bass.ds(j + PCOL["ffn_conv_b_2"], 1)]
                                ins = dve.tensor_scalar(uc[:, b, v, :], ub[:, b, v, 0:T], tap, bias, ALU.mult, ALU.add)
                            else:
                                dve.wait_ge(dve_step, it * (4 * RING) + (b0 + n - (w == 1 or v == 0)))
                                ins = dve.scalar_tensor_tensor(uc[:, b, v, :], ub[:, b, v, w:w + T], tap,
                                                               uc[:, b, v, :], ALU.mult, ALU.add)
                            if w < 2:
                                ins.then_inc(dve_step, 1)
                                n += 1
                            elif v == 1:
                                ins.then_inc(ffn_conv, 1)
                    dve.wait_ge(ffn_gelu, it * RING + (s + 1))
                    dve.tensor_tensor(ffa[:, bass.ds(it * RING + s, 1), :].rearrange("p a t -> p (a t)"),
                                      uc[:, b, 0, :], uc[:, b, 1, :], ALU.mult).then_inc(ffn_act, 1)
            for pr in range(4):
                c = plan["down"][3 * pr + 2]
                taken(dve, c)
                part = xres[:, 2 * pr:2 * pr + 2, :]
                dve.tensor_tensor(part, part, pair(aux[pr]), ALU.add).then_inc(x4_done, 1)
            dve.wait_ge(x4_done, 4)
            normalise(6, xres, yout, "final_norm_2")


def _per_partition(v, rows=P):
    v = np.moveaxis(np.asarray(v), -1, 0)
    v = v.reshape((v.shape[0] // rows, rows) + v.shape[1:])
    v = np.moveaxis(v, 1, 0).reshape(rows, -1)
    return np.concatenate([v, np.zeros((P - rows, v.shape[1]), v.dtype)]) if rows < P else v


def _layout(a):
    names = list(_VEC128) + ["conv_w", "ffn_conv_w_2", "ffn_conv_b_2"]
    flat = {n: (a[n][0] if n.endswith("_2") and a[n].ndim > 1 else a[n]) for n in names}
    cols = [_per_partition(flat[n]) for n in names]
    cols.append(_per_partition(a["fox_bf"], HEADS))
    for n in ("rnn_conv_w_2", "rnn_conv_b_2"):
        cols.append(_per_partition(a[n][0], C96))
    for n in ("rg_b_a_2", "rg_b_x_2", "rg_lambda_2", "gla_b_decay_2", "gla_norm_2"):
        cols.append(_per_partition(a[n][0].reshape(-1), C96))
    params = np.concatenate(cols, axis=1)
    keys = np.stack([a["peer_k1"], a["peer_k2"]], axis=1).reshape(HALVES, NK, DK // 2)
    u = a["peer_u"].reshape(P, P, KD, P)
    return {
        "xT": a["x"][0].T, "memT": a["mem_2"][0].T, "params": params, "w_in": a["w_in"],
        "w_conv_out": a["w_conv_out"], "w_fox_out": a["w_fox_out"], "w_out": a["w_out"],
        "peer_wq": a["peer_wq"], "keys": keys.transpose(2, 0, 1).reshape(P, -1),
        "uT": u.transpose(0, 3, 2, 1).reshape(P, P, D), "peer_v": a["peer_v"].reshape(P, P, D),
        "w_in_2": a["w_in_2"][0], "rg_w_a_2": a["rg_w_a_2"][0], "rg_w_x_2": a["rg_w_x_2"][0],
        "gla_w_decay_2": a["gla_w_decay_2"][0], "w_mem_kv_2": a["w_mem_kv_2"][0],
        "w_branch_2": a["w_branch_2"][0], "w_out_2": a["w_out_2"][0], "w_up_2": a["w_up_2"][0],
        "w_down_2": a["w_down_2"][0],
    }


def kernel(**inputs):
    import concourse.bacc as bacc
    from concourse.bass_utils import run_bass_kernel_spmd

    arrays = {n: np.ascontiguousarray(v) for n, v in _layout({n: np.asarray(v) for n, v in inputs.items()}).items()}
    nc = bacc.Bacc("TRN2", target_bir_lowering=False, num_devices=1)
    t = {n: nc.dram_tensor(f"in_{n}", v.shape, F32, kind="ExternalInput").ap() for n, v in arrays.items()}
    t["yT"] = nc.dram_tensor("yT", (D, T), F32, kind="ExternalOutput").ap()
    build(nc, t)
    r = run_bass_kernel_spmd(nc, [{f"in_{n}": v for n, v in arrays.items()}], core_ids=[0])
    return r.results[0]["yT"].T.reshape(1, T, D)
```

```python
from contextlib import ExitStack
import math

import numpy as np

import concourse.bass as bass
from concourse import mybir

F32 = mybir.dt.float32
F32R = mybir.dt.float32r
U32 = mybir.dt.uint32
ALU = mybir.AluOpType
ACT = mybir.ActivationFunctionType
AX = mybir.AxisListType

P = 128
T = 256
TT = T // P
D = 1024
KD = D // P
EPS = 1e-6
NEG = -1e30
TILE = 1024
RAW = 2
BANKS = 4
CW = 256
GROUP = 8

CONV_W = 31
HEADS, HD = 16, 64
QB = T // P
PH, NK, DK, TOPK = 8, 128, 256, 16
HALVES = 2 * PH
CHOICES = PH * TOPK
LOWEST = -3.4e38
A_VAL, A_GATE, Q0, K0, V0 = 0, 1024, 2048, 3072, 4096
F0 = 5120
GA0, GB0 = F0 + HEADS, F0 + HEADS + D

MEM = 256
MW = 768
C96 = 96
K96 = MW // C96
RNN_CONV = 4
GH, GDK, GDV, LOW = 4, 96, 192, 16
GCHUNK = 64
NCH = T // GCHUNK
MH, MHD = 4, 192
DFF = 3072
KF = DFF // P
Z_RNN = 0
Z_Q = Z_RNN + MW
Z_K = Z_Q + GH * GDK
Z_V = Z_K + GH * GDK
Z_G = Z_V + MW
Z_DEC = Z_G + MW
Z_MQ = Z_DEC + LOW
Z_GATE = Z_MQ + MW

_VEC128 = ["norm1_g", "conv_b", "conv_ln_g", "conv_ln_b", "norm2_g", "normf_g",
           "norm_mix_2", "mem_norm_2", "norm_ffn_2", "final_norm_2"]
PCOL = {}
_at = 0
for _n in _VEC128:
    PCOL[_n] = _at
    _at += KD
for _n, _w in (("conv_w", KD * CONV_W), ("ffn_conv_w_2", 2 * KF * 3), ("ffn_conv_b_2", 2 * KF),
               ("fox_bf", 1), ("rnn_conv_w_2", K96 * RNN_CONV), ("rnn_conv_b_2", K96),
               ("rg_b_a_2", K96), ("rg_b_x_2", K96), ("rg_lambda_2", K96),
               ("gla_b_decay_2", GH), ("gla_norm_2", K96)):
    PCOL[_n] = _at
    _at += _w
NPAR = _at


class Chunk:

    def __init__(self, index, raw, bank, split):
        self.index = index
        self.raw = raw
        self.bank = bank
        self.split = split
        self.landing = {}
        self.last = {}
        self.bank_use = 0
        self.tenant = 0


def plan_chunks():
    plan, order = {}, []
    landings, holder, bank_uses = {}, {}, [0] * BANKS
    banked_so_far, splits, tenant = 0, 0, 0

    def section(name, count, banked=True, split=True, tiles=(0, 1)):
        nonlocal banked_so_far, splits, tenant
        plan[name] = []
        for _ in range(count):
            c = Chunk(len(order), len(order) % RAW, banked_so_far % BANKS, splits if split else None)
            for v in tiles:
                at = (c.raw, v)
                landings[at] = landings.get(at, 0) + 1
                c.landing[v], c.last[v] = landings[at], holder.get(at)
                holder[at] = c
            if banked:
                bank_uses[c.bank] += 1
                c.bank_use = bank_uses[c.bank]
                banked_so_far += 1
            c.tenant = tenant
            if split:
                splits += 1
                tenant = c.index + 1
            order.append(c)
            plan[name].append(c)

    for j in range(4):
        section(f"conv_in{j}", 2)
    section("f", 1, split=False, tiles=(1,))
    for name in ("q", "k", "v", "ga", "gb"):
        section(name, 4)
    for name in ("conv_out", "fox_out", "mix_out"):
        section(name, 4, split=False)
    section("peer_q", 8)
    section("keys", 1, banked=False, split=False)
    section("u", P // 2)
    section("ev", P // 2, banked=False)
    section("mem_k", 4, split=False)
    section("mem_v", 3, split=False)
    section("z_rnn", 4)
    section("dec", 1, split=False, tiles=(1,))
    for name, count, split in (("zq", 2, True), ("zk", 2, True), ("zv", 3, True), ("gate0", 4, True),
                               ("zg", 4, True), ("zmq", 4, True), ("branch0", 4, False), ("gate1", 4, True),
                               ("branch1", 4, False), ("gate2", 4, True), ("branch2", 4, False),
                               ("out2", 4, False)):
        section(name, count, split=split)
    section("up", KF)
    section("down", 3 * 4, banked=False)
    return plan, order


def build(nc, t):
    plan, order = plan_chunks()
    ctx = ExitStack()
    with ctx:
        def sb(name, shape, dt=F32):
            return ctx.enter_context(nc.sbuf_tensor(name, shape, dt))

        def sem(name):
            return ctx.enter_context(nc.semaphore(name))

        gemm = [ctx.enter_context(nc.psum_tensor(f"gemm{i}", [P, 512], F32)) for i in range(BANKS)]
        aux = [ctx.enter_context(nc.psum_tensor(f"aux{i}", [P, 512], F32)) for i in range(4)]

        def pair(bank, rows=P):
            return bank[0:rows, :].rearrange("p (n t) -> p n t", n=2)

        raw = [[sb(f"raw{r}{v}", [P, TILE]) for v in range(2)] for r in range(RAW)]
        w_hi = [sb(f"w_hi{v}", [P, TILE], F32R) for v in range(2)]
        w_lo = [sb(f"w_lo{v}", [P, TILE], F32R) for v in range(2)]
        xres = sb("xres", [P, KD, T])
        h_hi = sb("h_hi", [P, KD, T], F32R)
        with nc.sbuf_tensor("mem_sq", [P, KD, T], F32) as mem_sq:
            pass
        h_lo = sb("h_lo", [P, KD, T], F32R)
        std = sb("std", [P, T])
        rstd = sb("rstd", [P, T])
        params = sb("params", [P, NPAR])
        ones = sb("ones", [P, P])
        ident = sb("ident", [P, P])
        zeros = sb("zeros", [P, P])
        iota = sb("iota", [P, P])
        keep = sb("keep", [P, T])
        epsc = sb("epsc", [P, 1])
        small = sb("small", [P, 15 * T])
        with nc.sbuf_tensor("big", [P, P * T], F32) as big:
            pass
        sb("ffn_area", [P, 3 * KD * T])
        ff_hi = sb("ff_hi", [P, KF, T], F32R)
        ff_lo = sb("ff_lo", [P, KF, T], F32R)

        def carver(base, start=0):
            at = [start]

            def carve(*shape, rows=P, dt=F32):
                n = math.prod(shape)
                v = base[0:rows, at[0]:at[0] + n]
                at[0] += n
                assert at[0] <= base.shape[1], (at[0], shape)
                if dt != F32:
                    v = v.bitcast(dt)
                names = "abcd"[:len(shape)]
                if len(shape) == 1:
                    return v
                return v.rearrange(f"p ({' '.join(names)}) -> p {' '.join(names)}",
                                   **dict(zip(names, shape)))
            return carve

        carve = carver(big)
        PADC = CONV_W - 1
        sq = carve(KD, T)
        zc = carve(KD, PADC + T)
        zv = carve(KD, T)
        sig = carve(2, 2, T)
        qT = carve(KD, T)
        kT = carve(KD, T)
        vtok = carve(TT, D)
        fy, fa, fe, fl, fc, fc8 = [carve(T, rows=HEADS) for _ in range(6)]
        sel = carve(HEADS, P, rows=HEADS)
        mask = carve(T)
        s_sb = carve(2, T)
        p_sb = carve(2, T)
        pT_sb = carve(2, T)
        ob = carve(KD, T)
        ga = carve(KD, T)
        gb = carve(KD, T)
        nmax, rsum, rrec = [carve(HEADS * QB) for _ in range(3)]
        act_peer = big[:, :].rearrange("p (i t) -> p i t", t=T)
        carve = carver(big, 64 * T)
        qp = carve(HALVES, T)
        ks = carve(TT, HALVES, NK)
        cand = carve(PH, TOPK * TOPK)
        eq = carve(PH, TOPK, TOPK)
        topv = carve(PH, 2, TOPK)
        topi = carve(PH, 2, TOPK, dt=U32)
        topif = carve(PH, 2, TOPK)
        sc = carve(TT, PH, TOPK)
        pos = carve(PH, TOPK, dt=U32)
        posp = carve(2, PH, TOPK, dt=U32)
        posf = carve(2, PH, TOPK)
        e1 = carve(TT, PH, TOPK)
        e2 = carve(TT, PH, TOPK)
        gsum = carve(TT, PH)
        grec = carve(TT, PH)
        carve = carver(small)
        hot1 = carve(2, GROUP, P // 2)
        hot2 = carve(2, GROUP, P)
        e1T, e2T, gT = [carve(T) for _ in range(3)]
        a_hi, a_lo = [h_hi[:, i:i + 4, :].rearrange("p (c v) t -> p c v t", c=2) for i in (0, 4)]
        memT = small[:, 0:KD * T].rearrange("p (k t) -> p k t", t=T)
        carve = carver(big, KD * T)
        gate = carve(KD, T)
        merged = carve(KD, T)
        out_a = carve(K96, T, rows=C96)
        out_b = carve(K96, T, rows=C96)
        mk = carve(K96, T, rows=C96)
        mv = carve(TT, MW)
        rg = carve(K96, T, rows=C96)
        ig = carve(K96, T, rows=C96)
        zr = carve(K96, RNN_CONV - 1 + T, rows=C96)
        xr = carve(K96, T, rows=C96)
        states = carve(GH, NCH - 1, GDV, rows=GDK)
        zq = carve(GH, T, rows=GDK)
        zk = carve(GH, T, rows=GDK)
        vg = carve(TT, MW)
        eg = carve(GH, T, rows=GDK)
        emg = carve(GH, T, rows=GDK)
        kendT = carve(TT, GH, GDK)
        rwa = carve(K96, C96, rows=C96)
        rwx = carve(K96, C96, rows=C96)
        lam = [carve(K96, rows=C96) for _ in range(7)]
        decay = carve(GH, NCH, rows=GDK)
        mnm, msum, mrec = [carve(MH * QB) for _ in range(3)]
        ra = zr.rearrange("p a b -> p (a b)")[:, 0:K96 * T].rearrange("p (a b) -> p a b", b=T)
        rt = states.rearrange("p h n v -> p (h n v)")[:, 0:K96 * T].rearrange("p (a b) -> p a b", b=T)
        sg = xr
        mq = ig
        out_c = out_a
        carve = carver(small)
        gy = carve(GH, T, rows=GDK)
        gl = carve(GH, T, rows=GDK)
        ekd = gy
        mp = carve(2, MEM)
        sT = carve(GH, TT, GCHUNK)
        mpT = carve(TT, T)
        carve = carver(big, 2 * KD * T)
        dec = carve(T, rows=LOW)
        wdec = carve(GH, GDK, rows=LOW)
        carve = carver(big, KD * T)
        ub = carve(2, 2, 2 + T)
        uc = carve(2, 2, T)
        ffp = carve(2, T)
        yout = carve(KD, T)

        landed = [[sem(f"landed{r}{v}") for v in range(2)] for r in range(RAW)]
        hi_ready = [sem(f"hi_ready{v}") for v in range(2)]
        lo_ready = [sem(f"lo_ready{v}") for v in range(2)]
        hi_used = [sem(f"hi_used{v}") for v in range(2)]
        tile_done = [sem(f"tile_done{v}") for v in range(2)]
        evacuated = [sem(f"evacuated{i}") for i in range(BANKS)]
        (x_in, params_in, consts, squared, sumsq, stdev, rstd_done, normed, h_ready, h_rounded, h_split,
         dve_step, f_logit, f_abs, f_exp, f_soft, c_ready, conv_done, mean_ready, centered,
         ln_squared, ln_sumsq, ln_std, ln_scaled, ln_sig, conv_act, gates_on,
         scores_ready, scores_moved, negmax_ready, exp_done, probs_ready, pT_psum, pT_ready, pv_done,
         ob_ready, mix_ready) = [sem(n) for n in (
             "x_in params_in consts squared sumsq stdev rstd_done normed h_ready h_rounded h_split "
             "dve_step f_logit f_abs f_exp f_soft c_ready conv_done mean_ready centered "
             "ln_squared ln_sumsq ln_std ln_scaled ln_sig conv_act gates_on "
             "scores_ready scores_moved negmax_ready exp_done probs_ready pT_psum pT_ready pv_done "
             "ob_ready mix_ready").split()]
        (keys_scored, keys_moved, topk_done, gate_exp, gates_ready, routed_psum, routed,
         a_rounded, a_split, x2_done, experts_done) = [sem(n) for n in (
             "keys_scored keys_moved topk_done gate_exp gates_ready routed_psum routed "
             "a_rounded a_split x2_done experts_done").split()]
        hots_ready = [sem(f"hots_ready{b}") for b in range(2)]
        planes_ready = [sem(f"planes_ready{b}") for b in range(2)]
        planes_used = [sem(f"planes_used{b}") for b in range(2)]
        (mem_in, rg_in, wdec_in, pads2, rnn_conv, rg_psum, rg_moved, lam_abs, lam_exp, lam_ln, lam_ready,
         la_ready, a_ready, tanh_ready, w_ready, root_ready, ig_used, rnn_done,
         dec_psum, gla_y, gla_abs, gla_soft, gla_sum, gla_exp, gla_qk, kend_psum, kend_moved,
         gla_scored, gla_scores_moved, gla_masked, states_psum, states_done, o_psum, o_moved, o_squared,
         o_sumsq, o_std, out_b_done, sg_sig,
         ms_psum, ms_max, ms_exp, ms_probs, mpT_psum, mpT_moved, mo_psum, mo_moved, merge_done,
         ffn_pads, ffn_conv, ffn_gelu, ffn_act, ffn_rounded, ffn_split, x4_done, stored) = [sem(n) for n in (
             "mem_in rg_in wdec_in pads2 rnn_conv rg_psum rg_moved lam_abs lam_exp lam_ln lam_ready "
             "la_ready a_ready tanh_ready w_ready root_ready ig_used rnn_done "
             "dec_psum gla_y gla_abs gla_soft gla_sum gla_exp gla_qk kend_psum kend_moved "
             "gla_scored gla_scores_moved gla_masked states_psum states_done o_psum o_moved o_squared "
             "o_sumsq o_std out_b_done sg_sig "
             "ms_psum ms_max ms_exp ms_probs mpT_psum mpT_moved mo_psum mo_moved merge_done "
             "ffn_pads ffn_conv ffn_gelu ffn_act ffn_rounded ffn_split x4_done stored").split()]
        N_CONSTS = 12

        def par(name, col=0, rows=P, n=1):
            c = PCOL[name] + col
            return params[0:rows, c:c + n]

        def by_k(tile, m, rows=P, n=KD):
            return tile[0:rows, 0:n * m].rearrange("p (k m) -> p k m", m=m)

        def taken(eng, c, it=0):
            eng.wait_ge(tile_done[1], it * BANKS + (c.index + 1))

        def moved(eng, chunks):
            for b in sorted({c.bank for c in chunks}):
                eng.wait_ge(evacuated[b], max(c.bank_use for c in chunks if c.bank == b))

        def subtract(eng, c, it=None, tiles=(0, 1), n=TILE):
            for v in tiles:
                if it is None:
                    eng.wait_ge(hi_ready[v], c.split + 1)
                    if c.tenant:
                        eng.wait_ge(tile_done[v], c.tenant)
                else:
                    eng.wait_ge(hi_ready[v], it * BANKS + (c.split + 1))
                    eng.wait_ge(tile_done[v], it * BANKS + c.index)
                eng.tensor_tensor(w_lo[v][:, 0:n], raw[c.raw][v][:, 0:n], w_hi[v][:, 0:n],
                                  ALU.subtract).then_inc(lo_ready[v], 1)

        NARROW = {name: KD * C96 for name in ("z_rnn", "zq", "zk", "zg", "zmq")}
        floats = {c.index: NARROW.get(name, TILE) for name, chunks in plan.items() for c in chunks}
        ITS = P // (2 * BANKS)
        HALF = P // 4

        block = ctx.enter_context(nc.Block())

        @block.sync
        def _(sp):
            sp.dma_start(xres[:, :, :], t["xT"].rearrange("(k p) t -> p k t", p=P)).then_inc(x_in, 16)
            sp.dma_start(params[:, :], t["params"]).then_inc(params_in, 16)

            def load(c, v, src, rows=P):
                last = c.last[v]
                if last is not None and last.split is not None:
                    sp.wait_ge(lo_ready[v], last.split + 1)
                elif last is not None:
                    sp.wait_ge(tile_done[v], last.index + 1)
                dst = raw[c.raw][v][0:rows, 0:math.prod(src.shape[1:])]
                if len(src.shape) == 3:
                    dst = dst.rearrange("p (k n) -> p k n", n=src.shape[2])
                sp.dma_start(dst, src).then_inc(landed[c.raw][v], 16)

            def columns(name, w, first, m, rows=P):
                for i, c in enumerate(plan[name]):
                    for n, v in enumerate(c.landing):
                        at = first + (len(c.landing) * i + n) * m
                        load(c, v, w[:, at:at + m].rearrange("(k p) n -> p k n", p=rows), rows)

            def half_columns(name, w, first):
                for i, c in enumerate(plan[name]):
                    cols = w[:, first + i * CW:first + (i + 1) * CW].rearrange("(k p) n -> p k n", p=P)
                    for v in range(2):
                        load(c, v, cols[:, v * KD // 2:(v + 1) * KD // 2, :])

            def looped(name, tile):
                for s in range(BANKS):
                    for v in range(2):
                        load(plan[name][s], v, tile(s, v))
                with sp.Fori(1, len(plan[name]) // BANKS) as it:
                    for s in range(BANKS):
                        c = plan[name][s]
                        for v in range(2):
                            sp.wait_ge(lo_ready[v], it * BANKS + (c.split - RAW + 1))
                            src = tile(it * BANKS + s, v)
                            dst = raw[c.raw][v][:, :]
                            if len(src.shape) == 3:
                                dst = dst.rearrange("p (k n) -> p k n", n=src.shape[2])
                            sp.dma_start(dst, src).then_inc(landed[c.raw][v], 16)

            w_in = t["w_in"]
            for j in range(4):
                for c, first in zip(plan[f"conv_in{j}"], (A_GATE, A_VAL)):
                    for v in range(2):
                        at = first + (2 * j + v) * P
                        load(c, v, w_in[:, at:at + P].rearrange("(k p) n -> p k n", p=P))
            columns("f", w_in, F0, HEADS)
            columns("q", w_in, Q0, P)
            columns("k", w_in, K0, P)
            half_columns("v", w_in, V0)
            columns("ga", w_in, GA0, P)
            columns("gb", w_in, GB0, P)
            columns("conv_out", t["w_conv_out"], 0, P)
            columns("fox_out", t["w_fox_out"], 0, P)
            columns("mix_out", t["w_out"], 0, P)
            columns("peer_q", t["peer_wq"], 0, P)
            for v in range(2):
                load(plan["keys"][0], v, t["keys"][:, v * TILE:(v + 1) * TILE])

            def plane(w):
                def tile(n, v):
                    if isinstance(n, int):
                        return w[2 * n + v]
                    return w[bass.ds(n * 2 + v, 1), :, :].rearrange("i p d -> p (i d)")
                return tile

            looped("u", plane(t["uT"]))
            looped("ev", plane(t["peer_v"]))
            columns("mem_k", t["w_mem_kv_2"], 0, C96)
            half_columns("mem_v", t["w_mem_kv_2"], MW)
            w_in2 = t["w_in_2"]
            columns("z_rnn", w_in2, Z_RNN, C96)
            columns("dec", w_in2, Z_DEC, LOW)
            columns("zq", w_in2, Z_Q, C96)
            columns("zk", w_in2, Z_K, C96)
            half_columns("zv", w_in2, Z_V)
            columns("gate0", w_in2, Z_GATE, P)
            columns("zg", w_in2, Z_G, C96)
            columns("zmq", w_in2, Z_MQ, C96)
            columns("branch0", t["w_branch_2"][0], 0, P, C96)
            columns("gate1", w_in2, Z_GATE + D, P)
            columns("branch1", t["w_branch_2"][1], 0, P, C96)
            columns("gate2", w_in2, Z_GATE + 2 * D, P)
            columns("branch2", t["w_branch_2"][2], 0, P, C96)
            columns("out2", t["w_out_2"], 0, P)
            up = t["w_up_2"].rearrange("(k p) (v n) -> p v k n", p=P, v=2)
            looped("up", lambda n, v: up[:, v, :, n * P:(n + 1) * P] if isinstance(n, int)
                   else up[:, v, :, bass.ds(n * P, P)])
            for i, c in enumerate(plan["down"]):
                pr, g = divmod(i, 3)
                for v in range(2):
                    cols = slice((2 * pr + v) * P, (2 * pr + v + 1) * P)
                    load(c, v, t["w_down_2"][g * D:(g + 1) * D, cols].rearrange("(k p) n -> p k n", p=P))
            sp.wait_ge(normed, 3)
            sp.dma_start(t["yT"].rearrange("(k p) t -> p k t", p=P), yout[:, :, :]).then_inc(stored, 16)
            sp.wait_ge(stored, 16)

        @block.gpsimd
        def _(pool):
            pool.memset(ones[:, :], 1.0).then_inc(consts, 1)
            pool.memset(zeros[:, :], 0.0).then_inc(consts, 1)
            pool.memset(epsc[:, :], EPS).then_inc(consts, 1)
            pool.memset(zc[:, :, 0:PADC], 0.0).then_inc(consts, 1)
            pool.iota(iota[:, :], [[1, P]], base=0, channel_multiplier=0,
                      allow_small_or_imprecise_dtypes=True).then_inc(consts, 1)
            pool.memset(ident[:, :], 0.0).then_inc(consts, 1)
            pool.memset(mask, 0.0).then_inc(consts, 1)
            pool.memset(sel, 0.0).then_inc(consts, 1)
            pool.memset(keep[:, :], 1.0).then_inc(consts, 1)
            pool.wait_ge(consts, 9)
            pool.memset(keep[:, :].rearrange("p (n i) -> p n i", i=GCHUNK)[:, :, 0:1], 0.0).then_inc(consts, 1)
            pool.affine_select(out=ident[:, :], in_=ident[:, :], compare_op=ALU.not_equal, fill=1.0,
                               base=0, pattern=[[-1, P]], channel_multiplier=1)
            pool.affine_select(out=sel, in_=sel, compare_op=ALU.not_equal, fill=1.0, base=0,
                               pattern=[[-1, HEADS], [0, P]], channel_multiplier=1).then_inc(consts, 1)
            pool.affine_select(out=mask[:, P:T], in_=mask[:, P:T], compare_op=ALU.is_ge, fill=NEG, base=0,
                               pattern=[[-1, P]], channel_multiplier=1).then_inc(consts, 1)
            def sections(first, last):
                for c in order[plan[first][0].index:plan[last][-1].index + 1]:
                    if c.split is not None:
                        subtract(pool, c, n=floats[c.index])

            def planes(first, its, tiles):
                with pool.Fori(0, its) as it:
                    for c in order[first.index:first.index + BANKS]:
                        subtract(pool, c, it, tiles)

            sections("conv_in0", "peer_q")
            planes(plan["u"][0], ITS // 2, (0, 1))
            planes(plan["u"][HALF], ITS // 2, (1,))
            planes(plan["ev"][0], ITS // 2, (1,))
            for b in range(2):
                pool.wait_ge(planes_used[b], HALF + 1)
            pool.dma_start(memT, t["memT"].rearrange("(k p) t -> p k t", p=P)).then_inc(mem_in, 16)
            planes(plan["ev"][HALF], ITS // 2, (1,))
            pool.wait_ge(x2_done, BANKS)
            pool.dma_start(rwa, t["rg_w_a_2"].rearrange("h i j -> i h j")).then_inc(rg_in, 16)
            pool.dma_start(rwx, t["rg_w_x_2"].rearrange("h i j -> i h j")).then_inc(rg_in, 16)
            pool.dma_start(wdec, t["gla_w_decay_2"].rearrange("l (h d) -> l h d", h=GH)).then_inc(wdec_in, 16)
            pool.memset(zr[:, :, 0:RNN_CONV - 1], 0.0).then_inc(pads2, 1)
            sections("z_rnn", "zmq")
            for v in range(2):
                pool.wait_ge(lo_ready[v], plan["zmq"][-1].split + 1)
            pool.wait_ge(gla_scores_moved, 1)
            for hp in range(2):
                part = sT[hp * GCHUNK:(hp + 1) * GCHUNK].rearrange("p h n i -> p (h n) i")
                pool.affine_select(out=part, in_=part, compare_op=ALU.is_ge, fill=0.0, base=0,
                                   pattern=[[0, GH * TT], [1, GCHUNK]], channel_multiplier=-1
                                   ).then_inc(gla_masked, 1)
            pool.wait_ge(gla_masked, 2)
            sections("branch0", "gate2")
            pool.wait_ge(h_split, 8)
            pool.memset(ub[:, :, :, 0:2], 0.0).then_inc(ffn_pads, 1)
            with pool.Fori(0, KF // BANKS) as it:
                for c in plan["up"][:BANKS]:
                    subtract(pool, c, it)
            sections("down", "down")

        @block.tensor
        def _(pe):
            def product(c, m, it=None):
                if it is not None:
                    pe.wait_ge(evacuated[c.bank], it + (c.bank_use - 1))
                elif c.bank_use > 1:
                    pe.wait_ge(evacuated[c.bank], c.bank_use - 1)
                chunks = 0 if it is None else it * BANKS
                for v in range(2):
                    out = pair(gemm[c.bank], m)[:, v, :]
                    pe.wait_ge(hi_ready[v], chunks + (c.split + 1))
                    w = by_k(w_hi[v], m)
                    for n, act_part in enumerate((h_hi, h_lo)):
                        for k in range(KD):
                            mm = pe.matmul(out, w[:, k, :], act_part[:, k, :], start=(n == k == 0), stop=False)
                    mm.then_inc(hi_used[v], 1)
                    pe.wait_ge(lo_ready[v], chunks + (c.split + 1))
                    w = by_k(w_lo[v], m)
                    for k in range(KD):
                        mm = pe.matmul(out, w[:, k, :], h_hi[:, k, :], start=False, stop=(k == KD - 1))
                    mm.then_inc(tile_done[v], 1)

            def plain_product(c, m, src, rows=P):
                if c.bank_use > 1:
                    pe.wait_ge(evacuated[c.bank], c.bank_use - 1)
                for v in range(2):
                    pe.wait_ge(landed[c.raw][v], 16 * c.landing[v])
                    w = by_k(raw[c.raw][v], m, rows)
                    for k in range(KD):
                        mm = pe.matmul(pair(gemm[c.bank], m)[:, v, :], w[:, k, :], src[:, k, :],
                                       start=(k == 0), stop=(k == KD - 1))
                    mm.then_inc(tile_done[v], 1)

            def narrow(c, m, src):
                pe.wait_ge(landed[c.raw][1], 16 * c.landing[1])
                pe.wait_ge(evacuated[c.bank], c.bank_use - 1)
                w = by_k(raw[c.raw][1], m)
                for k in range(KD):
                    mm = pe.matmul(gemm[c.bank][0:m, 0:T], w[:, k, :], src[:, k, :],
                                   start=(k == 0), stop=(k == KD - 1))
                    if k == 0:
                        mm.then_inc(tile_done[0], 1)
                mm.then_inc(tile_done[1], 1)

            def by_token(c, src=None):
                pe.wait_ge(evacuated[c.bank], c.bank_use - 1)

                def part(x, w, v, begins=False, ends=False):
                    for tt in range(TT):
                        for k in range(KD // 2):
                            mm = pe.matmul(pair(gemm[c.bank])[:, tt, :],
                                           x[:, v * KD // 2 + k, tt * P:(tt + 1) * P], w[:, k, :],
                                           start=(begins and tt == k == 0), stop=(ends and k == KD // 2 - 1),
                                           skip_group_check=True)
                    return mm

                for v in range(2):
                    if c.split is None:
                        pe.wait_ge(landed[c.raw][v], 16 * c.landing[v])
                        part(src, by_k(raw[c.raw][v], CW, n=KD // 2), v, v == 0, v == 1).then_inc(tile_done[v], 1)
                        continue
                    pe.wait_ge(hi_ready[v], c.split + 1)
                    w = by_k(w_hi[v], CW, n=KD // 2)
                    part(h_hi, w, v, begins=(v == 0))
                    part(h_lo, w, v).then_inc(hi_used[v], 1)
                    pe.wait_ge(lo_ready[v], c.split + 1)
                    part(h_hi, by_k(w_lo[v], CW, n=KD // 2), v, ends=(v == 1)).then_inc(tile_done[v], 1)

            def sum_squares(i):
                for k in range(KD):
                    if k % 4 == 0:
                        pe.wait_ge(squared, 2 * i + k // 4 + 1)
                    part = (mem_sq if i == 2 else sq)[:, k, :]
                    mm = pe.matmul(aux[3][:, 0:T], ones[:, :], part, start=(k == 0), stop=(k == KD - 1))
                mm.then_inc(sumsq, 1)

            pe.wait_ge(consts, N_CONSTS)
            sum_squares(0)
            pe.wait_ge(h_split, 2)
            for j in range(4):
                for c in plan[f"conv_in{j}"]:
                    product(c, P)
            narrow(plan["f"][0], HEADS, sq)
            for c in plan["q"] + plan["k"]:
                product(c, P)
            for c in plan["v"]:
                by_token(c)
            pe.wait_ge(conv_done, 1)
            for k in range(KD):
                mm = pe.matmul(aux[2][:, 0:T], ones[:, :], zv[:, k, :], start=(k == 0), stop=(k == KD - 1))
            mm.then_inc(mean_ready, 1)
            product(plan["ga"][0], P)
            product(plan["ga"][1], P)
            pe.wait_ge(ln_squared, 2)
            for k in range(KD):
                mm = pe.matmul(aux[3][:, 0:T], ones[:, :], sq[:, k, :], start=(k == 0), stop=(k == KD - 1))
            mm.then_inc(ln_sumsq, 1)
            for c in plan["ga"][2:] + plan["gb"]:
                product(c, P)

            def scores(u):
                h, qb = divmod(u, QB)
                lo, nk = (h % 2) * HD, (qb + 1) * P
                if u >= 2:
                    pe.wait_ge(scores_moved, u - 1)
                pe.matmul(aux[u % 2][:, 0:nk], qT[lo:lo + HD, h // 2, qb * P:(qb + 1) * P],
                          kT[lo:lo + HD, h // 2, 0:nk], start=True, stop=False)
                pe.matmul(aux[u % 2][:, 0:nk], sel[:, h, :], fc8[:, 0:nk],
                          start=False, stop=True).then_inc(scores_ready, 1)

            def turn_probs(u):
                qb = u % QB
                pe.wait_ge(probs_ready, u + 1)
                if u >= 1:
                    pe.wait_ge(pT_ready, u)
                for kb in range(qb + 1):
                    mm = pe.transpose(aux[2][:, kb * P:(kb + 1) * P], p_sb[:, u % 2, kb * P:(kb + 1) * P],
                                      ident[:, :])
                mm.then_inc(pT_psum, 1)

            def values(u):
                h, qb = divmod(u, QB)
                lo = (h % 2) * HD
                pe.wait_ge(pT_ready, u + 1)
                if u % 4 == 0 and u:
                    pe.wait_ge(ob_ready, u // 4)
                for kb in range(qb + 1):
                    mm = pe.matmul(aux[3][lo:lo + HD, qb * P:(qb + 1) * P], vtok[:, kb, h * HD:(h + 1) * HD],
                                   pT_sb[:, u % 2, kb * P:(kb + 1) * P], start=(kb == 0), stop=(kb == qb))
                mm.then_inc(pv_done, 1)

            moved(pe, plan["q"] + plan["k"] + plan["v"])
            pe.wait_ge(c_ready, 1)
            pe.wait_ge(ln_std, 1)
            UNITS = HEADS * QB
            for u in range(UNITS + 3):
                if u < UNITS:
                    scores(u)
                if 2 <= u < UNITS + 2:
                    turn_probs(u - 2)
                if u >= 3:
                    values(u - 3)
                if u == 6:
                    pe.wait_ge(conv_act, 1)
                if u >= 6 and u % 6 == 0 and u // 6 <= 4:
                    plain_product(plan["conv_out"][u // 6 - 1], P, zv)
            pe.wait_ge(ob_ready, KD)
            for c in plan["fox_out"]:
                plain_product(c, P, ob)
            pe.wait_ge(mix_ready, 4)
            for c in plan["mix_out"]:
                plain_product(c, P, ga)

            sum_squares(1)
            pe.wait_ge(h_split, 4)
            for c in plan["peer_q"]:
                product(c, P)
            kc = plan["keys"][0]
            for v in range(2):
                pe.wait_ge(landed[kc.raw][v], 16 * kc.landing[v])
            moved(pe, plan["peer_q"])
            for g in range(TT * 4):
                tt, h0 = divmod(4 * g, HALVES)
                if g >= 4:
                    pe.wait_ge(keys_moved, g - 3)
                for i in range(4):
                    v, at = divmod(h0 + i, HALVES // 2)
                    mm = pe.matmul(aux[g % 4][:, i * NK:(i + 1) * NK], qp[:, h0 + i, tt * P:(tt + 1) * P],
                                   raw[kc.raw][v][:, at * NK:(at + 1) * NK], start=True, stop=True)
                mm.then_inc(keys_scored, 1)
            pe.wait_ge(keys_scored, TT * 4)
            pe.sem_inc(tile_done[0], 1)
            pe.sem_inc(tile_done[1], 1)

            with pe.Fori(0, ITS // 2) as it:
                for c in plan["u"][:BANKS]:
                    product(c, P, it)
            pe.wait_ge(gates_ready, 1)
            for n, src in enumerate((e1, e2, sc)):
                for tt in range(TT):
                    mm = pe.transpose(aux[n][:, tt * P:(tt + 1) * P],
                                      src[:, tt].rearrange("p h k -> p (h k)"), ident[:, :])
                mm.then_inc(routed_psum, 1)

            def gate_planes(half, s, it):
                b = s % 2
                pe.wait_ge(hots_ready[b], it * 2 + (half * HALF // 2 + s // 2 + 1))
                pe.wait_ge(planes_used[b], it * 2 + (half * HALF // 2 + s // 2 + 1))
                for n in range(GROUP):
                    mm = pe.matmul(aux[b][:, n * P // 2:(n + 1) * P // 2], hot2[:, b, n, :], hot1[:, b, n, :],
                                   start=True, stop=True)
                mm.then_inc(planes_ready[b], 1)

            with pe.Fori(0, ITS // 2) as it:
                for s in range(BANKS):
                    gate_planes(0, s, it)
                    product(plan["u"][HALF + s], P, it)
            moved(pe, plan["u"])
            for b in range(4):
                pe.matmul(gemm[b][:, :], zeros[:, :],
                          zeros[:, :].unsqueeze(1).to_broadcast([P, 4, P]), start=True, stop=False,
                          skip_group_check=True)

            def expert_values(c, it):
                for v in range(2):
                    pe.wait_ge(hi_ready[v], it * BANKS + (c.split + 1))
                    steps = ((w_hi, a_hi, a_rounded), (w_hi, a_lo, a_split), (w_lo, a_hi, lo_ready[v]))
                    for w, a, ready in steps:
                        n = c.split + 1 if w is w_lo else c.index - plan["ev"][0].index + 1
                        pe.wait_ge(ready, it * BANKS + n)
                        for d in range(KD):
                            mm = pe.matmul(pair(gemm[d // 2])[:, d % 2, :], w[v][:, d * P:(d + 1) * P],
                                           a[:, c.raw, v, :], start=False, stop=False, skip_group_check=True)
                        if a is a_lo:
                            mm.then_inc(hi_used[v], 1)
                    mm.then_inc(tile_done[v], 1)

            with pe.Fori(0, ITS // 2) as it:
                for s in range(BANKS):
                    gate_planes(1, s, it)
                    expert_values(plan["ev"][s], it)
            with pe.Fori(0, ITS // 4) as it:
                for c in plan["ev"][HALF:HALF + BANKS]:
                    expert_values(c, it)
            sum_squares(2)
            with pe.Fori(0, ITS // 4) as it:
                for c in plan["ev"][3 * HALF // 2:3 * HALF // 2 + BANKS]:
                    expert_values(c, it)
            for b in range(4):
                pe.matmul(gemm[b][:, :], zeros[:, :],
                          zeros[:, :].unsqueeze(1).to_broadcast([P, 4, P]), start=False, stop=True,
                          skip_group_check=True).then_inc(experts_done, 1)

            pe.wait_ge(normed, 1)
            for i, c in enumerate(plan["mem_k"]):
                pe.wait_ge(x2_done, c.bank + 1)
                plain_product(c, C96, memT)
                if i == 0:
                    sum_squares(3)
                if i == 2:
                    sum_squares(4)
            for c in plan["mem_v"]:
                by_token(c, memT)
            pe.wait_ge(h_split, 6)
            for c in plan["z_rnn"]:
                product(c, C96)
            narrow(plan["dec"][0], LOW, sq)
            for c in plan["zq"] + plan["zk"]:
                product(c, C96)
            for c in plan["zv"]:
                by_token(c)
            moved(pe, plan["dec"])
            pe.wait_ge(wdec_in, 16)
            for h in range(GH):
                mm = pe.matmul(pair(aux[h // 2], GDK)[:, h % 2, :], wdec[:, h, :], dec, start=True, stop=True)
            mm.then_inc(dec_psum, 1)
            pe.wait_ge(rnn_conv, K96)
            pe.wait_ge(rg_in, 32)
            for h in range(K96):
                if h >= 2:
                    pe.wait_ge(rg_moved, 2 * (h - 1))
                bank = pair(aux[2 + h % 2], C96)
                pe.matmul(bank[:, 0, :], rwa[:, h, :], xr[:, h, :], start=True, stop=True)
                pe.matmul(bank[:, 1, :], rwx[:, h, :], xr[:, h, :], start=True, stop=True).then_inc(rg_psum, 1)
            for c in plan["gate0"]:
                product(c, P)
            pe.wait_ge(gla_qk, 3)
            pe.wait_ge(gla_y, GH)
            for tt in range(TT):
                for h in range(GH):
                    mm = pe.transpose(aux[tt][:, h * GDK:(h + 1) * GDK], ekd[:, h, tt * P:(tt + 1) * P],
                                      ident[0:GDK, 0:GDK])
                mm.then_inc(kend_psum, 1)
            pe.wait_ge(rg_moved, 2 * K96)
            for h in range(GH):
                for n in range(NCH):
                    lo, cols = (n % 2) * GCHUNK, slice(n * GCHUNK, (n + 1) * GCHUNK)
                    at_col = (h * TT + n // 2) * GCHUNK
                    mm = pe.matmul(aux[2][lo:lo + GCHUNK, at_col:at_col + GCHUNK], emg[:, h, cols],
                                   eg[:, h, cols], start=True, stop=True)
            mm.then_inc(gla_scored, 1)
            for c in plan["zg"] + plan["zmq"]:
                product(c, C96)
            pe.wait_ge(kend_moved, TT)
            moved(pe, plan["zv"])
            for n in range(NCH - 1):
                lo = (n % 2) * GCHUNK
                for half in range(2):
                    bank = aux[half if n % 2 == 0 else 2 + half]
                    if n == 1:
                        pe.wait_ge(gla_scores_moved, 1)
                    if n == 2:
                        pe.wait_ge(states_done, half + 1)
                    for i in range(2):
                        h = 2 * half + i
                        mm = pe.matmul(bank[0:GDK, i * GDV:(i + 1) * GDV],
                                       kendT[lo:lo + GCHUNK, n // 2, h, :],
                                       vg[lo:lo + GCHUNK, n // 2, h * GDV:(h + 1) * GDV],
                                       start=True, stop=True)
                    mm.then_inc(states_psum, 1)
            pe.wait_ge(rnn_done, 1)
            for c in plan["branch0"]:
                plain_product(c, P, out_a, C96)
            pe.wait_ge(gla_masked, 2)
            pe.wait_ge(states_done, 2 + GH * (NCH - 2))
            def gla_out(h):
                for parity in range(2):
                    lo = parity * GCHUNK
                    bank = aux[2 * (h % 2) + parity][0:C96, 0:T].rearrange("p (v n i) -> p v n i", v=2, n=TT)
                    if h >= 2 and parity == 0:
                        pe.wait_ge(o_std, h - 1)
                    for vh in range(2):
                        vcols = slice(h * GDV + vh * C96, h * GDV + (vh + 1) * C96)
                        for half in range(TT):
                            n = 2 * half + parity
                            cols = slice(n * GCHUNK, (n + 1) * GCHUNK)
                            mm = pe.matmul(bank[:, vh, half, :], vg[lo:lo + GCHUNK, half, vcols],
                                           sT[lo:lo + GCHUNK, h, half, :], start=True, stop=(n == 0))
                            if n:
                                mm = pe.matmul(bank[:, vh, half, :], states[:, h, n - 1, vh * C96:(vh + 1) * C96],
                                               eg[:, h, cols], start=False, stop=True)
                    mm.then_inc(o_psum, 1)

            def gla_sumsq(h):
                pe.wait_ge(o_squared, 2 * h + 2)
                for vh in range(2):
                    mm = pe.matmul(aux[2 * (h % 2)][0:C96, 0:T], ones[0:C96, 0:C96], sq[0:C96, 2 * h + vh, :],
                                   start=(vh == 0), stop=(vh == 1))
                mm.then_inc(o_sumsq, 1)

            for h0 in range(0, GH, 2):
                for stage in (gla_out, gla_sumsq):
                    stage(h0)
                    stage(h0 + 1)

            def mem_scores(u):
                h, qb = divmod(u, QB)
                if u >= 2:
                    pe.wait_ge(ms_exp, u - 1)
                for vh in range(2):
                    mm = pe.matmul(aux[u % 2][:, 0:MEM], mq[:, 2 * h + vh, qb * P:(qb + 1) * P],
                                   mk[:, 2 * h + vh, :], start=(vh == 0), stop=(vh == 1))
                mm.then_inc(ms_psum, 1)

            def mem_turn(u):
                pe.wait_ge(ms_probs, u + 1)
                if u:
                    pe.wait_ge(mpT_moved, u)
                for mt in range(TT):
                    mm = pe.transpose(aux[2][:, mt * P:(mt + 1) * P], mp[:, u % 2, mt * P:(mt + 1) * P],
                                      ident[:, :])
                mm.then_inc(mpT_psum, 1)

            def mem_values(h):
                pe.wait_ge(mpT_moved, 2 * h + 2)
                if h:
                    pe.wait_ge(mo_moved, h)
                for vh in range(2):
                    for mt in range(TT):
                        mm = pe.matmul(pair(aux[3], C96)[:, vh, :],
                                       mv[:, mt, h * MHD + vh * C96:h * MHD + (vh + 1) * C96],
                                       mpT[:, mt, :], start=(mt == 0), stop=(mt == TT - 1))
                mm.then_inc(mo_psum, 1)

            pe.wait_ge(o_std, GH)
            moved(pe, plan["zmq"] + plan["mem_k"] + plan["mem_v"])
            for u in range(MH * QB + 1):
                if u < MH * QB:
                    mem_scores(u)
                if u % 2 == 0 and u < MH * QB:
                    product(plan["gate1"][u // 2], P)
                if u:
                    mem_turn(u - 1)
                if u and u % 2 == 0:
                    mem_values(u // 2 - 1)
            pe.wait_ge(out_b_done, 1)
            for c in plan["branch1"]:
                plain_product(c, P, out_b, C96)
            for c in plan["gate2"]:
                product(c, P)
            pe.wait_ge(mo_moved, MH)
            for c in plan["branch2"]:
                plain_product(c, P, out_c, C96)
            pe.wait_ge(merge_done, 8)
            for c in plan["out2"]:
                plain_product(c, P, merged)

            sum_squares(5)
            pe.wait_ge(h_split, 8)
            with pe.Fori(0, KF // BANKS) as it:
                for c in plan["up"][:BANKS]:
                    product(c, P, it)
            for i, c in enumerate(plan["down"]):
                pr, g = divmod(i, 3)
                pe.wait_ge(ffn_split, KD * (g + 1) if pr == 0 else KF)
                for v in range(2):
                    for w, x, ready in ((w_hi, ff_hi, hi_ready), (w_hi, ff_lo, hi_ready), (w_lo, ff_hi, lo_ready)):
                        pe.wait_ge(ready[v], c.split + 1)
                        for k in range(KD):
                            mm = pe.matmul(pair(aux[pr])[:, v, :], w[v][:, k * P:(k + 1) * P], x[:, g * KD + k, :],
                                           start=(g == v == k == 0 and w is w_hi and x is ff_hi),
                                           stop=(g == 2 and w is w_lo and k == KD - 1), skip_group_check=True)
                        if x is ff_lo:
                            mm.then_inc(hi_used[v], 1)
                    mm.then_inc(tile_done[v], 1)
            sum_squares(6)

        @block.scalar
        def _(act):
            def squares(src, dst=sq):
                for half in range(2):
                    part = slice(4 * half, 4 * half + 4)
                    act.activation(dst[:, part, :], src[:, part, :], ACT.Square).then_inc(squared, 1)

            def deviation(i):
                act.wait_ge(sumsq, i + 1)
                if i:
                    act.wait_ge(rstd_done, i)
                act.activation(std[:, :], aux[3][:, 0:T], ACT.Sqrt, bias=epsc[:, :],
                               scale=1.0 / D).then_inc(stdev, 1)

            def round_h(j):
                for half in range(2):
                    part = slice(4 * half, 4 * half + 4)
                    act.wait_ge(h_ready, 2 * j + half + 1)
                    act.activation(h_hi[:, part, :], sq[:, part, :], ACT.Copy).then_inc(h_rounded, 1)

            def round_weights(c, it=0):
                for v in range(2):
                    round_tile(c, v, it)

            def round_tile(c, v, it=0):
                act.wait_ge(landed[c.raw][v], it * (16 * BANKS // RAW) + 16 * c.landing[v])
                if c.split:
                    act.wait_ge(hi_used[v], it * BANKS + c.split)
                    act.wait_ge(lo_ready[v], it * BANKS + c.split)
                n = floats[c.index]
                act.activation(w_hi[v][:, 0:n], raw[c.raw][v][:, 0:n], ACT.Copy).then_inc(hi_ready[v], 1)

            ahead = [0]

            def look_ahead(upto):
                for c in order[ahead[0]:upto + 1]:
                    if c.split is not None:
                        round_weights(c)
                ahead[0] = max(ahead[0], upto + 1)

            def evacuate(c, out, src, func=ACT.Copy, **kw):
                look_ahead(c.index + 1)
                taken(act, c)
                act.activation(out, src, func, **kw).then_inc(evacuated[c.bank], 1)

            act.wait_ge(x_in, 16)
            squares(xres)
            act.wait_ge(consts, N_CONSTS)
            look_ahead(0)
            deviation(0)
            round_h(0)
            for j in range(4):
                gc, vc = plan[f"conv_in{j}"]
                if j >= 2:
                    moved(act, plan[f"conv_in{j - 2}"][1:])
                evacuate(gc, sig[:, j % 2], pair(gemm[gc.bank]), ACT.Sigmoid)
            fchunk = plan["f"][0]
            act.wait_ge(params_in, 16)
            evacuate(fchunk, fy, gemm[fchunk.bank][0:HEADS, 0:T], ACT.Identity, bias=par("fox_bf", rows=HEADS))
            for i, c in enumerate(plan["q"]):
                evacuate(c, qT[:, 2 * i:2 * i + 2, :], pair(gemm[c.bank]))
            for i, c in enumerate(plan["k"]):
                evacuate(c, kT[:, 2 * i:2 * i + 2, :], pair(gemm[c.bank]))
            for i, c in enumerate(plan["v"]):
                evacuate(c, vtok[:, :, i * CW:(i + 1) * CW], pair(gemm[c.bank]))
            act.wait_ge(f_abs, 1)
            act.activation(fe, fa, ACT.Exp).then_inc(f_exp, 1)
            act.wait_ge(f_exp, 1)
            act.activation(fl, fe, ACT.Ln, bias=1.0).then_inc(f_soft, 1)
            def gate_raw(i):
                c = (plan["ga"] + plan["gb"])[i]
                dst = ga if i < 4 else gb
                evacuate(c, dst[:, 2 * (i % 4):2 * (i % 4) + 2, :], pair(gemm[c.bank]))

            gate_raw(0)
            act.wait_ge(centered, 1)
            for half in range(2):
                part = slice(4 * half, 4 * half + 4)
                act.activation(sq[:, part, :], zv[:, part, :], ACT.Square).then_inc(ln_squared, 1)
            gate_raw(1)
            act.wait_ge(ln_sumsq, 1)
            act.wait_ge(rstd_done, 1)
            act.activation(std[:, :], aux[3][:, 0:T], ACT.Sqrt, bias=epsc[:, :], scale=1.0 / D).then_inc(ln_std, 1)
            for i in range(2, 8):
                gate_raw(i)
            for k in range(KD):
                act.wait_ge(ln_scaled, k + 1)
                act.activation(sq[:, k, :], zv[:, k, :], ACT.Sigmoid, bias=par("conv_ln_b", k)).then_inc(ln_sig, 1)
            moved(act, plan["ga"] + plan["gb"])
            act.activation(ga, ga, ACT.Sigmoid).then_inc(gates_on, 1)
            act.activation(gb, gb, ACT.Sigmoid).then_inc(gates_on, 1)

            def exponent(u):
                nk = (u % QB + 1) * P
                act.wait_ge(negmax_ready, u + 1)
                if u >= 2:
                    act.wait_ge(pT_psum, u - 1)
                act.activation(p_sb[:, u % 2, 0:nk], s_sb[:, u % 2, 0:nk], ACT.Exp, bias=nmax[:, u:u + 1],
                               accum_out=rsum[:, u:u + 1]).then_inc(exp_done, 1)

            def copy_turned(u):
                nk = (u % QB + 1) * P
                act.wait_ge(pT_psum, u + 1)
                if u >= 2:
                    act.wait_ge(pv_done, u - 1)
                act.activation(pT_sb[:, u % 2, 0:nk], aux[2][:, 0:nk], ACT.Copy).then_inc(pT_ready, 1)

            UNITS = HEADS * QB
            for u in range(UNITS + 4):
                if u < UNITS:
                    exponent(u)
                if 2 <= u < UNITS + 2:
                    copy_turned(u - 2)
                if u >= 7 and u % 4 == 3:
                    i = (u - 7) // 4
                    act.wait_ge(pv_done, 4 * i + 4)
                    act.activation(ob[:, i, :], aux[3][:, 0:T], ACT.Copy).then_inc(ob_ready, 1)

            moved(act, plan["mix_out"])
            squares(xres)
            look_ahead(plan["peer_q"][0].index)
            deviation(1)
            round_h(1)
            for i, c in enumerate(plan["peer_q"]):
                evacuate(c, qp[:, 2 * i:2 * i + 2, :], pair(gemm[c.bank]))
            for g in range(TT * 4):
                tt, h0 = divmod(4 * g, HALVES)
                act.wait_ge(keys_scored, g + 1)
                act.activation(ks[:, tt, h0:h0 + 4, :], aux[g % 4][:, :].rearrange("p (h n) -> p h n", h=4),
                               ACT.Copy).then_inc(keys_moved, 1)

            def gelu(c, plane, it):
                taken(act, c, it)
                act.activation(act_peer[:, plane, :], pair(gemm[c.bank]),
                               ACT.Gelu_apprx_tanh).then_inc(evacuated[c.bank], 1)

            def gelus(half):
                with act.Fori(0, ITS // 2) as it:
                    for s, c in enumerate(plan["u"][half * HALF:half * HALF + BANKS]):
                        round_weights(order[c.index + 1], it)
                        gelu(c, bass.ds(it * 2 * BANKS + 2 * (half * HALF + s), 2), it)

            def round_acts(c, plane, it=0):
                act.wait_ge(tile_done[1], it * BANKS + (c.index - 1))
                act.activation(a_hi[:, c.raw, :, :], act_peer[:, plane, :], ACT.Copy).then_inc(a_rounded, 1)

            def value_steps(first, its):
                with act.Fori(0, its) as it:
                    for s in range(first, first + BANKS):
                        c = plan["ev"][s + 1]
                        round_acts(c, bass.ds(it * 2 * BANKS + 2 * (s + 1), 2), it)
                        round_weights(c, it)

            def last_value_steps(first):
                for s in range(first, min(first + BANKS, P // 2 - 1)):
                    c = plan["ev"][s + 1]
                    if s + 1 == HALF:
                        for b in range(2):
                            act.wait_ge(planes_used[b], HALF + 1)
                    round_acts(c, slice(2 * (s + 1), 2 * (s + 1) + 2))
                    round_weights(c)

            look_ahead(plan["u"][0].index)
            gelus(0)
            act.wait_ge(topk_done, 1)
            act.activation(sc, sc, ACT.Exp).then_inc(gate_exp, 1)
            gelus(1)
            for b in range(2):
                act.wait_ge(planes_used[b], HALF // 2 + 1)
            act.wait_ge(tile_done[1], plan["u"][-1].index + 1)
            round_acts(plan["ev"][0], slice(0, 2))
            value_steps(0, ITS // 2 - 1)
            last_value_steps(HALF - BANKS)
            value_steps(HALF, ITS // 4)
            act.wait_ge(mem_in, 16)
            squares(memT, mem_sq)
            value_steps(3 * HALF // 2, ITS // 4 - 1)
            deviation(2)
            last_value_steps(2 * HALF - BANKS)
            ahead[0] = plan["ev"][-1].index + 1

            act.wait_ge(x2_done, BANKS)
            squares(xres)
            mem_k = plan["mem_k"]
            for i, c in enumerate(mem_k):
                evacuate(c, mk[:, 2 * i:2 * i + 2, :], pair(gemm[c.bank], C96))
                if i == 0:
                    deviation(3)
                    act.wait_ge(normed, 2)
                    squares(xres)
                if i == 2:
                    deviation(4)
                    round_h(2)
            for i, c in enumerate(plan["mem_v"]):
                evacuate(c, mv[:, :, i * CW:(i + 1) * CW], pair(gemm[c.bank]))
            act.wait_ge(lam_abs, 1)
            act.activation(lam[1], lam[0], ACT.Exp).then_inc(lam_exp, 1)
            act.wait_ge(lam_exp, 1)
            act.activation(lam[2], lam[1], ACT.Ln, bias=1.0).then_inc(lam_ln, 1)
            act.wait_ge(pads2, 1)
            for i, c in enumerate(plan["z_rnn"]):
                evacuate(c, zr[:, 2 * i:2 * i + 2, RNN_CONV - 1:], pair(gemm[c.bank], C96))
            c = plan["dec"][0]
            evacuate(c, dec, gemm[c.bank][0:LOW, 0:T])
            for name, dst in (("zq", zq), ("zk", zk)):
                for i, c in enumerate(plan[name]):
                    evacuate(c, dst[:, 2 * i:2 * i + 2, :], pair(gemm[c.bank], GDK))
            for i, c in enumerate(plan["zv"]):
                evacuate(c, vg[:, :, i * CW:(i + 1) * CW], pair(gemm[c.bank]))
            act.wait_ge(dec_psum, 1)
            for h in range(GH):
                act.activation(gy[:, h, :], pair(aux[h // 2], GDK)[:, h % 2, :], ACT.Identity,
                               bias=par("gla_b_decay_2", h, GDK)).then_inc(gla_y, 1)
            act.wait_ge(gla_abs, 1)
            act.activation(eg, eg, ACT.Exp).then_inc(gla_soft, 1)
            act.wait_ge(gla_soft, 1)
            act.activation(emg, eg, ACT.Ln, bias=1.0).then_inc(gla_soft, 1)
            for h in range(K96):
                act.wait_ge(rg_psum, h + 1)
                bank = pair(aux[2 + h % 2], C96)
                act.activation(rg[:, h, :], bank[:, 0, :], ACT.Sigmoid, bias=par("rg_b_a_2", h, C96)).then_inc(rg_moved, 1)
                act.activation(ig[:, h, :], bank[:, 1, :], ACT.Sigmoid, bias=par("rg_b_x_2", h, C96)).then_inc(rg_moved, 1)
            for i, c in enumerate(plan["gate0"]):
                evacuate(c, gate[:, 2 * i:2 * i + 2, :], pair(gemm[c.bank]), ACT.Sigmoid)
            act.wait_ge(gla_sum, 2)
            last = gl.rearrange("p h (n i) -> p (h n) i", i=GCHUNK)[:, :, GCHUNK - 1]
            act.activation(eg, gl, ACT.Exp, scale=1.0 / 16).then_inc(gla_exp, 1)
            act.activation(emg, gl, ACT.Exp, scale=-1.0 / 16).then_inc(gla_exp, 1)
            act.activation(ekd, gy, ACT.Exp, scale=1.0 / 16).then_inc(gla_exp, 1)
            act.activation(decay.rearrange("p h n -> p (h n)"), last, ACT.Exp, scale=1.0 / 16).then_inc(gla_exp, 1)
            act.wait_ge(la_ready, 1)
            act.activation(ra, rg, ACT.Exp).then_inc(a_ready, 1)
            act.wait_ge(a_ready, 1)
            act.activation(rg, rg, ACT.Tanh, scale=-1.0).then_inc(tanh_ready, 1)
            for tt in range(TT):
                act.wait_ge(kend_psum, tt + 1)
                act.activation(kendT[:, tt].rearrange("p h d -> p (h d)"), aux[tt][:, 0:GH * GDK],
                               ACT.Copy).then_inc(kend_moved, 1)
            act.wait_ge(gla_scored, 1)
            act.activation(sT, aux[2][:, :].rearrange("p (h n i) -> p h n i", h=GH, n=TT),
                           ACT.Copy).then_inc(gla_scores_moved, 1)
            act.wait_ge(w_ready, 1)
            act.activation(rg, rg, ACT.Sqrt).then_inc(root_ready, 1)
            act.wait_ge(ig_used, 1)
            for i, c in enumerate(plan["zg"]):
                look_ahead(c.index + 1)
                taken(act, c)
                act.activation(sg[:, 2 * i:2 * i + 2, :], pair(gemm[c.bank], C96), ACT.Sigmoid).then_inc(sg_sig, 1)
            act.wait_ge(rnn_done, 1)
            for i, c in enumerate(plan["zmq"]):
                evacuate(c, mq[:, 2 * i:2 * i + 2, :], pair(gemm[c.bank], C96))
            def by_parity(tile, h, parity):
                return tile[0:C96, 2 * h:2 * h + 2, :].rearrange(
                    "p v (n q i) -> p v n q i", q=2, i=GCHUNK)[:, :, :, parity, :]

            for h0 in range(0, GH, 2):
                for h in (h0, h0 + 1):
                    for parity in range(2):
                        bank = aux[2 * (h % 2) + parity][0:C96, 0:T].rearrange("p (v n i) -> p v n i", v=2, n=TT)
                        act.wait_ge(o_psum, 2 * h + parity + 1)
                        act.activation(by_parity(out_b, h, parity), bank, ACT.Copy).then_inc(o_moved, 1)
                        act.activation(by_parity(sq, h, parity), bank, ACT.Square).then_inc(o_squared, 1)
                for h in (h0, h0 + 1):
                    act.wait_ge(o_sumsq, h + 1)
                    act.activation(eg[:, h, :], aux[2 * (h % 2)][0:C96, 0:T], ACT.Sqrt, bias=epsc[0:C96, :],
                                   scale=1.0 / GDV).then_inc(o_std, 1)

            def gate_evac(b, i):
                c = plan[f"gate{b}"][i]
                look_ahead(c.index + 1)
                if b == 1:
                    moved(act, plan["branch0"][i:i + 1])
                else:
                    act.wait_ge(merge_done, i + 1)
                evacuate(c, gate[:, 2 * i:2 * i + 2, :], pair(gemm[c.bank]), ACT.Sigmoid)

            def mem_exp(u):
                act.wait_ge(ms_max, u + 1)
                if u >= 2:
                    act.wait_ge(mpT_psum, u - 1)
                act.activation(mp[:, u % 2, :], aux[u % 2][:, 0:MEM], ACT.Exp, bias=mnm[:, u:u + 1],
                               scale=MHD ** -0.5, accum_out=msum[:, u:u + 1]).then_inc(ms_exp, 1)

            def mem_copy(u):
                h, qb = divmod(u, QB)
                act.wait_ge(mpT_psum, u + 1)
                if qb == 0 and h:
                    act.wait_ge(mo_psum, h)
                act.activation(mpT[:, :, qb * P:(qb + 1) * P],
                               aux[2][:, 0:MEM].rearrange("p (m q) -> p m q", m=TT), ACT.Copy).then_inc(mpT_moved, 1)

            for u in range(MH * QB + 1):
                if u < MH * QB:
                    mem_exp(u)
                if u % 2 == 0 and u < MH * QB:
                    gate_evac(1, u // 2)
                if u:
                    mem_copy(u - 1)
                if u and u % 2 == 0:
                    h = u // 2 - 1
                    act.wait_ge(mo_psum, h + 1)
                    act.activation(out_c[:, 2 * h:2 * h + 2, :], pair(aux[3], C96), ACT.Copy).then_inc(mo_moved, 1)
            for i in range(4):
                gate_evac(2, i)
            moved(act, plan["out2"])
            squares(xres)
            look_ahead(plan["up"][0].index)
            deviation(5)
            round_h(3)
            act.wait_ge(ffn_pads, 1)

            def up_to_sbuf(c, b, n, it=0):
                taken(act, c, it)
                if not isinstance(n, int) or n >= 2:
                    act.wait_ge(ffn_conv, n - 1)
                act.activation(ub[:, b, :, 2:], pair(gemm[c.bank]), ACT.Copy).then_inc(evacuated[c.bank], 1)

            def ffn_gelus(b, n):
                act.wait_ge(ffn_conv, n + 1)
                act.activation(uc[:, b, 0, :], uc[:, b, 0, :], ACT.Gelu_apprx_tanh).then_inc(ffn_gelu, 1)

            def ffn_round(b, n):
                act.wait_ge(ffn_act, n + 1)
                plane = slice(n, n + 1) if isinstance(n, int) else bass.ds(n, 1)
                act.activation(ff_hi[:, plane, :].rearrange("p a t -> p (a t)"), ffp[:, b, :],
                               ACT.Copy).then_inc(ffn_rounded, 1)

            def up_step(s, n, it=0, first=False):
                c = plan["up"][s]
                up_to_sbuf(c, s % 2, n, it)
                if not first:
                    ffn_gelus((s + 1) % 2, n - 1)
                round_tile(order[c.index + 1], 0, it)
                if not first:
                    ffn_round((s + 1) % 2, n - 1)
                round_tile(order[c.index + 1], 1, it)

            for s in range(BANKS):
                up_step(s, s, first=(s == 0))
            with act.Fori(1, KF // BANKS) as it:
                for s in range(BANKS):
                    up_step(s, it * BANKS + s, it)
            ffn_gelus((KF - 1) % 2, KF - 1)
            ffn_round((KF - 1) % 2, KF - 1)
            ahead[0] = plan["down"][0].index + 1
            look_ahead(plan["down"][-1].index)
            act.wait_ge(x4_done, 4)
            squares(xres)
            deviation(6)

        @block.vector
        def _(dve):
            count = [0]

            def step(ins):
                count[0] += 1
                ins.then_inc(dve_step, 1)

            def settle(behind=0):
                if count[0] > behind:
                    dve.wait_ge(dve_step, count[0] - behind)

            def normalise(i, src, dst, gain):
                dve.wait_ge(stdev, i + 1)
                dve.reciprocal(rstd[:, :], std[:, :]).then_inc(rstd_done, 1)
                dve.wait_ge(rstd_done, i + 1)
                for k in range(KD):
                    ins = dve.scalar_tensor_tensor(dst[:, k, :], src[:, k, :], par(gain, k), rstd[:, :],
                                                   ALU.mult, ALU.mult)
                ins.then_inc(normed, 1)

            def normalise_split(i, j, gain):
                dve.wait_ge(stdev, i + 1)
                dve.reciprocal(rstd[:, :], std[:, :]).then_inc(rstd_done, 1)
                dve.wait_ge(rstd_done, i + 1)
                for k in range(KD):
                    ins = dve.scalar_tensor_tensor(sq[:, k, :], xres[:, k, :], par(gain, k), rstd[:, :],
                                                   ALU.mult, ALU.mult)
                    if k % 4 == 3:
                        ins.then_inc(h_ready, 1)
                for half in range(2):
                    part = slice(4 * half, 4 * half + 4)
                    dve.wait_ge(h_rounded, 2 * j + half + 1)
                    dve.tensor_tensor(h_lo[:, part, :], sq[:, part, :], h_hi[:, part, :],
                                      ALU.subtract).then_inc(h_split, 1)

            def add_to_residual(name):
                for i, c in enumerate(plan[name]):
                    taken(dve, c)
                    part = xres[:, 2 * i:2 * i + 2, :]
                    dve.tensor_tensor(part, part, pair(gemm[c.bank]), ALU.add).then_inc(evacuated[c.bank], 1)

            dve.wait_ge(params_in, 16)
            normalise_split(0, 0, "norm1_g")
            dve.wait_ge(consts, N_CONSTS)
            for j in range(4):
                gc, vc = plan[f"conv_in{j}"]
                taken(dve, vc)
                moved(dve, [gc])
                dve.tensor_tensor(zc[:, 2 * j:2 * j + 2, PADC:], pair(gemm[vc.bank]), sig[:, j % 2],
                                  ALU.mult).then_inc(evacuated[vc.bank], 1)
                moved(dve, [vc])
                for w in range(CONV_W):
                    for k in (2 * j, 2 * j + 1):
                        tap = par("conv_w", k * CONV_W + w)
                        if w == 0:
                            step(dve.tensor_scalar(zv[:, k, :], zc[:, k, 0:T], tap, par("conv_b", k),
                                                   ALU.mult, ALU.add))
                        else:
                            settle(1)
                            step(dve.scalar_tensor_tensor(zv[:, k, :], zc[:, k, w:w + T], tap, zv[:, k, :],
                                                          ALU.mult, ALU.add))
            settle()
            dve.tensor_copy(rrec[0:1, 0:1], ones[0:1, 0:1]).then_inc(conv_done, 1)
            moved(dve, plan["f"])
            dve.scalar_tensor_tensor(fa, fy, -1.0, fy, ALU.mult, ALU.min).then_inc(f_abs, 1)
            dve.wait_ge(f_soft, 1)
            step(dve.scalar_tensor_tensor(fa, fy, 0.0, fl, ALU.min, ALU.subtract))
            settle()
            step(dve.tensor_tensor_scan(fc, keep[0:HEADS, 1:2].to_broadcast([HEADS, T]), fa, 0.0, ALU.mult, ALU.add))
            settle()
            dve.tensor_scalar(fc8, fc, -math.sqrt(HD), None, ALU.mult).then_inc(c_ready, 1)
            dve.wait_ge(mean_ready, 1)
            for k in range(KD):
                ins = dve.scalar_tensor_tensor(zv[:, k, :], aux[2][:, 0:T], -1.0 / D, zv[:, k, :], ALU.mult, ALU.add)
            ins.then_inc(centered, 1)
            dve.wait_ge(ln_std, 1)
            step(dve.reciprocal(rstd[:, :], std[:, :]))
            settle()
            for k in range(KD):
                dve.scalar_tensor_tensor(zv[:, k, :], zv[:, k, :], par("conv_ln_g", k), rstd[:, :],
                                         ALU.mult, ALU.mult).then_inc(ln_scaled, 1)
            for k in range(KD):
                dve.wait_ge(ln_sig, k + 1)
                ins = dve.scalar_tensor_tensor(zv[:, k, :], zv[:, k, :], par("conv_ln_b", k), sq[:, k, :],
                                               ALU.add, ALU.mult)
            ins.then_inc(conv_act, 1)

            def move_scores(u):
                qb = u % QB
                nk = (qb + 1) * P
                dve.wait_ge(scores_ready, u + 1)
                if u >= 2:
                    dve.wait_ge(exp_done, u - 1)
                dve.scalar_tensor_tensor(s_sb[:, u % 2, 0:nk], aux[u % 2][:, 0:nk], HD ** -0.5,
                                         mask[:, T - nk:T], ALU.mult, ALU.add).then_inc(scores_moved, 1)
                dve.wait_ge(scores_moved, u + 1)
                dve.tensor_reduce(nmax[:, u:u + 1], s_sb[:, u % 2, 0:nk], AX.X, ALU.max,
                                  negate=True).then_inc(negmax_ready, 1)

            def divide(u):
                nk = (u % QB + 1) * P
                dve.wait_ge(exp_done, u + 1)
                step(dve.reciprocal(rrec[:, u:u + 1], rsum[:, u:u + 1]))
                settle()
                dve.tensor_scalar(p_sb[:, u % 2, 0:nk], p_sb[:, u % 2, 0:nk], rrec[:, u:u + 1], None,
                                  ALU.mult).then_inc(probs_ready, 1)

            UNITS = HEADS * QB
            for u in range(UNITS + 1):
                if u < UNITS:
                    move_scores(u)
                if u:
                    divide(u - 1)
                if u >= 7 and (u - 1) % 6 == 0 and (u - 1) // 6 <= 4:
                    i = (u - 1) // 6 - 1
                    c = plan["conv_out"][i]
                    taken(dve, c)
                    dve.wait_ge(gates_on, 2)
                    part = ga[:, 2 * i:2 * i + 2, :]
                    dve.tensor_tensor(part, part, pair(gemm[c.bank]), ALU.mult).then_inc(evacuated[c.bank], 1)
            for i, c in enumerate(plan["fox_out"]):
                taken(dve, c)
                a, b = ga[:, 2 * i:2 * i + 2, :], gb[:, 2 * i:2 * i + 2, :]
                dve.tensor_tensor(b, b, pair(gemm[c.bank]), ALU.mult).then_inc(evacuated[c.bank], 1)
                moved(dve, [c, plan["conv_out"][i]])
                dve.tensor_tensor(a, a, b, ALU.add).then_inc(mix_ready, 1)
            add_to_residual("mix_out")

            moved(dve, plan["mix_out"])
            normalise_split(1, 1, "norm2_g")

            def best(outs, src):
                for v, i, s in outs:
                    step(dve.max(v[:, 0:8], s))
                for n, (v, i, s) in enumerate(outs):
                    settle(len(outs) - 1)
                    step(dve.max_index(i[:, 0:8], v[:, 0:8], s))
                for v, i, s in outs:
                    settle(len(outs) - 1)
                    step(dve.match_replace(s, v[:, 0:8], s, LOWEST))
                for v, i, s in outs:
                    settle(len(outs) - 1)
                    step(dve.max(v[:, 8:16], s))
                for v, i, s in outs:
                    settle(len(outs) - 1)
                    step(dve.max_index(i[:, 8:16], v[:, 8:16], s))

            for tt in range(TT):
                dve.wait_ge(keys_moved, 4 * tt + 4)
                if tt == 0:
                    dve.wait_ge(keys_moved, 8)
                for h in range(PH):
                    best([(topv[:, h, f], topi[:, h, f], ks[:, tt, 2 * h + f, :]) for f in range(2)], None)
                settle()
                step(dve.tensor_copy(topif, topi))
                step(dve.tensor_tensor(cand.rearrange("p h (a b) -> p h a b", a=TOPK),
                                       topv[:, :, 0].unsqueeze(3).to_broadcast([P, PH, TOPK, TOPK]),
                                       topv[:, :, 1].unsqueeze(2).to_broadcast([P, PH, TOPK, TOPK]), ALU.add))
                settle()
                for h in range(0, PH, 2):
                    best([(sc[:, tt, g], pos[:, g], cand[:, g]) for g in (h, h + 1)], None)
                settle()
                step(dve.tensor_scalar(posp[:, 0], pos, 4, None, ALU.logical_shift_right))
                step(dve.tensor_scalar(posp[:, 1], pos, TOPK - 1, None, ALU.bitwise_and))
                settle()
                step(dve.tensor_copy(posf, posp))
                settle()
                for f, e in ((0, e1), (1, e2)):
                    step(dve.tensor_tensor(eq, posf[:, f].unsqueeze(3).to_broadcast([P, PH, TOPK, TOPK]),
                                           iota[:, 0:TOPK].unsqueeze(1).unsqueeze(1).to_broadcast([P, PH, TOPK, TOPK]),
                                           ALU.is_equal))
                    settle()
                    step(dve.tensor_tensor(eq, eq, topif[:, :, f].unsqueeze(2).to_broadcast([P, PH, TOPK, TOPK]),
                                           ALU.mult))
                    settle()
                    step(dve.tensor_reduce(e[:, tt], eq, AX.X, ALU.add))
                    settle()
            for tt in range(TT):
                step(dve.tensor_copy(grec[:, tt], sc[:, tt, :, 0]))
            settle()
            for tt in range(TT):
                ins = dve.tensor_tensor(sc[:, tt], sc[:, tt], grec[:, tt].unsqueeze(2).to_broadcast([P, PH, TOPK]),
                                        ALU.subtract)
            ins.then_inc(topk_done, 1)
            dve.wait_ge(gate_exp, 1)
            step(dve.tensor_reduce(gsum.rearrange("p t h -> p (t h)"), sc.rearrange("p t h k -> p (t h) k"),
                                   AX.X, ALU.add))
            settle()
            step(dve.reciprocal(grec, gsum))
            settle()
            dve.tensor_tensor(sc.rearrange("p t h k -> p (t h) k"), sc.rearrange("p t h k -> p (t h) k"),
                              grec.rearrange("p t h -> p (t h)").unsqueeze(2).to_broadcast([P, TT * PH, TOPK]),
                              ALU.mult).then_inc(gates_ready, 1)
            for n, (dst, done) in enumerate(((e1T, planes_used[0]), (e2T, planes_used[1]), (gT, routed))):
                dve.wait_ge(routed_psum, n + 1)
                dve.tensor_copy(dst, aux[n][:, 0:T]).then_inc(done, 1)
            for done in (planes_used[0], planes_used[1], routed):
                dve.wait_ge(done, 1)

            def hots(half, s, it):
                b = s % 2
                for n in range(GROUP):
                    tok = bass.ds(it * (BANKS * GROUP) + (GROUP * s + n), 1)
                    dve.tensor_scalar(hot1[:, b, n, :], iota[:, half * P // 2:(half + 1) * P // 2],
                                      e1T[:, tok], gT[:, tok], ALU.is_equal, ALU.mult)
                    ins = dve.tensor_scalar(hot2[:, b, n, :], iota[:, :], e2T[:, tok], None, ALU.is_equal)
                ins.then_inc(hots_ready[b], 1)

            def apply_gates(half, s, it):
                b = s % 2
                dve.wait_ge(planes_ready[b], it * 2 + (half * HALF // 2 + s // 2 + 1))
                part = act_peer[:, half * P // 2:(half + 1) * P // 2,
                                bass.ds(it * (BANKS * GROUP) + GROUP * s, GROUP)]
                dve.tensor_tensor(part, part, aux[b][:, :].rearrange("p (t i) -> p i t", t=GROUP),
                                  ALU.mult).then_inc(planes_used[b], 1)

            def subtract_acts(c, plane, it):
                dve.wait_ge(a_rounded, it * BANKS + (c.index - plan["ev"][0].index + 1))
                dve.tensor_tensor(a_lo[:, c.raw, :, :], act_peer[:, plane, :], a_hi[:, c.raw, :, :],
                                  ALU.subtract).then_inc(a_split, 1)

            def value_steps(first, its, gates):
                with dve.Fori(0, its) as it:
                    for s in range(first, first + BANKS):
                        c = plan["ev"][s]
                        if gates:
                            hots(1, s, it)
                        subtract_acts(c, bass.ds(it * 2 * BANKS + 2 * s, 2), it)
                        subtract(dve, c, it, (0,))
                        if gates:
                            apply_gates(1, s, it)

            moved(dve, plan["u"][:HALF])
            with dve.Fori(0, ITS // 2) as it:
                for s in range(BANKS):
                    hots(0, s, it)
                    subtract(dve, plan["u"][HALF + s], it, (0,))
                    apply_gates(0, s, it)
            moved(dve, plan["u"])
            value_steps(0, ITS // 2, True)
            value_steps(HALF, ITS // 4, False)
            value_steps(3 * HALF // 2, ITS // 4 - 1, False)
            normalise(2, memT, memT, "mem_norm_2")
            value_steps(2 * HALF - BANKS, 1, False)
            for b in range(BANKS):
                dve.wait_ge(experts_done, b + 1)
                part = xres[:, 2 * b:2 * b + 2, :]
                dve.tensor_tensor(part, part, pair(gemm[b]), ALU.add).then_inc(x2_done, 1)

            dve.wait_ge(x2_done, BANKS)
            normalise(3, xres, xres, "normf_g")
            dve.wait_ge(normed, 2)
            normalise_split(4, 2, "norm_mix_2")
            lamv = par("rg_lambda_2", 0, C96, K96)
            dve.scalar_tensor_tensor(lam[0], lamv, -1.0, lamv, ALU.mult, ALU.min).then_inc(lam_abs, 1)
            dve.wait_ge(lam_ln, 1)
            step(dve.tensor_scalar(lam[3], lam[1], 1.0, 1.0, ALU.add, ALU.subtract))
            settle()
            step(dve.tensor_scalar(lam[4], lam[3], 0.0, None, ALU.is_equal))
            settle()
            step(dve.tensor_tensor(lam[3], lam[3], lam[4], ALU.add))
            step(dve.tensor_tensor(lam[2], lam[2], lam[4], ALU.add))
            settle()
            step(dve.reciprocal(lam[5], lam[3]))
            step(dve.tensor_tensor(lam[2], lam[2], lam[1], ALU.mult))
            settle()
            step(dve.tensor_tensor(lam[2], lam[2], lam[5], ALU.mult))
            settle()
            step(dve.scalar_tensor_tensor(lam[6], lamv, 0.0, lam[2], ALU.min, ALU.subtract))
            settle()
            dve.tensor_scalar(lam[6], lam[6], 8.0, None, ALU.mult).then_inc(lam_ready, 1)
            for h0 in range(0, K96, 2):
                moved(dve, [plan["z_rnn"][h0 // 2]])
                for w in range(RNN_CONV):
                    for h in (h0, h0 + 1):
                        tap = par("rnn_conv_w_2", h * RNN_CONV + w, C96)
                        if w == 0:
                            step(dve.tensor_scalar(xr[:, h, :], zr[:, h, 0:T], tap, par("rnn_conv_b_2", h, C96),
                                                   ALU.mult, ALU.add))
                            continue
                        settle(0 if w == RNN_CONV - 1 and h > h0 else 1)
                        ins = dve.scalar_tensor_tensor(xr[:, h, :], zr[:, h, w:w + T], tap, xr[:, h, :],
                                                       ALU.mult, ALU.add)
                        if w < RNN_CONV - 1:
                            step(ins)
                        else:
                            ins.then_inc(rnn_conv, 1)
            dve.wait_ge(gla_y, GH)
            dve.scalar_tensor_tensor(eg, gy, -1.0, gy, ALU.mult, ALU.min).then_inc(gla_abs, 1)
            dve.wait_ge(gla_soft, 2)
            step(dve.scalar_tensor_tensor(gy, gy, 0.0, emg, ALU.min, ALU.subtract))
            settle()
            for h in range(GH):
                ins = dve.tensor_tensor_scan(gl[:, h, :], keep[0:GDK, :], gy[:, h, :], 0.0, ALU.mult, ALU.add)
            ins.then_inc(gla_sum, 1)
            dve.wait_ge(gla_sum, 1)
            glc = gl.rearrange("p h (n i) -> p (h n) i", i=GCHUNK)
            dve.tensor_tensor(gy.rearrange("p h (n i) -> p (h n) i", i=GCHUNK),
                              glc[:, :, GCHUNK - 1:GCHUNK].to_broadcast([GDK, GH * NCH, GCHUNK]), glc,
                              ALU.subtract).then_inc(gla_sum, 1)
            dve.wait_ge(lam_ready, 1)
            dve.wait_ge(rg_moved, 2 * K96)
            dve.tensor_tensor(rg, rg, lam[6].unsqueeze(2).to_broadcast([C96, K96, T]), ALU.mult).then_inc(la_ready, 1)
            moved(dve, plan["zq"] + plan["zk"])
            dve.wait_ge(gla_exp, 3)
            dve.scalar_tensor_tensor(eg, zq, GDK ** -0.5, eg, ALU.mult, ALU.mult).then_inc(gla_qk, 1)
            dve.tensor_tensor(emg, zk, emg, ALU.mult).then_inc(gla_qk, 1)
            dve.tensor_tensor(ekd, zk, ekd, ALU.mult).then_inc(gla_qk, 1)
            step(dve.tensor_tensor(ig, ig, xr, ALU.mult))
            settle()
            dve.wait_ge(a_ready, 1)
            step(dve.tensor_tensor(rt, ra, ra, ALU.mult))
            settle()
            dve.wait_ge(tanh_ready, 1)
            dve.scalar_tensor_tensor(rg, rt, 1.0, rg, ALU.add, ALU.mult).then_inc(w_ready, 1)
            dve.wait_ge(root_ready, 1)
            dve.tensor_tensor(ig, ig, rg, ALU.mult).then_inc(ig_used, 1)
            dve.wait_ge(ig_used, 1)
            for h in range(K96):
                ins = dve.tensor_tensor_scan(out_a[:, h, :], ra[:, h, :], ig[:, h, :], 0.0, ALU.mult, ALU.add)
            ins.then_inc(rnn_done, 1)
            for i, c in enumerate(plan["zg"]):
                dve.wait_ge(sg_sig, i + 1)
                part = sg[:, 2 * i:2 * i + 2, :]
                dve.tensor_tensor(part, part, pair(gemm[c.bank], C96), ALU.mult).then_inc(evacuated[c.bank], 1)
            dve.wait_ge(gla_exp, 4)
            for n in range(NCH - 1):
                for half in range(2):
                    bank = aux[half if n % 2 == 0 else 2 + half]
                    dve.wait_ge(states_psum, 2 * n + half + 1)
                    if n == 0:
                        dve.tensor_copy(states[:, 2 * half:2 * half + 2, 0, :],
                                        bank[0:GDK, 0:2 * GDV].rearrange("p (h v) -> p h v", h=2)).then_inc(states_done, 1)
                        continue
                    for i in range(2):
                        h = 2 * half + i
                        dve.wait_ge(states_done, 2 if n == 1 else 2 + h + 1)
                        dve.scalar_tensor_tensor(states[:, h, n, :], states[:, h, n - 1, :], decay[:, h, n:n + 1],
                                                 bank[0:GDK, i * GDV:(i + 1) * GDV],
                                                 ALU.mult, ALU.add).then_inc(states_done, 1)

            def merge(b, i):
                c = plan[f"branch{b}"][i]
                m, g = merged[:, 2 * i:2 * i + 2, :], gate[:, 2 * i:2 * i + 2, :]
                taken(dve, c)
                moved(dve, [plan[f"gate{b}"][i]])
                if b == 0:
                    dve.tensor_tensor(m, g, pair(gemm[c.bank]), ALU.mult).then_inc(evacuated[c.bank], 1)
                    return
                dve.tensor_tensor(g, g, pair(gemm[c.bank]), ALU.mult).then_inc(evacuated[c.bank], 1)
                moved(dve, [c, plan["branch0"][i]])
                if b == 2:
                    dve.wait_ge(merge_done, i + 1)
                dve.tensor_tensor(m, m, g, ALU.add).then_inc(merge_done, 1)

            for i in range(4):
                merge(0, i)
            dve.wait_ge(o_std, GH)
            step(dve.reciprocal(eg, eg))
            settle()
            for h in range(GH):
                for vh in range(2):
                    k = 2 * h + vh
                    step(dve.scalar_tensor_tensor(out_b[:, k, :], out_b[:, k, :], par("gla_norm_2", k, C96),
                                                  eg[:, h, :], ALU.mult, ALU.mult))
            settle()
            moved(dve, plan["zg"])
            dve.tensor_tensor(out_b, out_b, sg, ALU.mult).then_inc(out_b_done, 1)

            def mem_max(u):
                dve.wait_ge(ms_psum, u + 1)
                step(dve.tensor_reduce(mnm[:, u:u + 1], aux[u % 2][:, 0:MEM], AX.X, ALU.max, negate=True))
                settle()
                dve.tensor_scalar(mnm[:, u:u + 1], mnm[:, u:u + 1], MHD ** -0.5, None, ALU.mult).then_inc(ms_max, 1)

            def mem_divide(u):
                dve.wait_ge(ms_exp, u + 1)
                step(dve.reciprocal(mrec[:, u:u + 1], msum[:, u:u + 1]))
                settle()
                dve.tensor_scalar(mp[:, u % 2, :], mp[:, u % 2, :], mrec[:, u:u + 1], None, ALU.mult).then_inc(ms_probs, 1)

            for u in range(MH * QB + 1):
                if u < MH * QB:
                    mem_max(u)
                if u:
                    mem_divide(u - 1)
            for b in (1, 2):
                for i in range(4):
                    merge(b, i)
            add_to_residual("out2")
            moved(dve, plan["out2"])

            normalise_split(5, 3, "norm_ffn_2")
            dve.wait_ge(ffn_pads, 1)
            settled = count[0]

            def ffn_convolve(s, n, it=0):
                b = s % 2
                dve.wait_ge(evacuated[plan["up"][s].bank], it + plan["up"][s].bank_use)
                for w in range(3):
                    for v in range(2):
                        j = n + v * KF
                        at = j * 3 + (PCOL["ffn_conv_w_2"] + w)
                        tap = params[:, at:at + 1] if isinstance(n, int) else params[:, bass.ds(at, 1)]
                        if w == 0:
                            at = j + PCOL["ffn_conv_b_2"]
                            bias = params[:, at:at + 1] if isinstance(n, int) else params[:, bass.ds(at, 1)]
                            ins = dve.tensor_scalar(uc[:, b, v, :], ub[:, b, v, 0:T], tap, bias, ALU.mult, ALU.add)
                        else:
                            dve.wait_ge(dve_step, n * 4 + (settled + 2 * w + v - 1))
                            ins = dve.scalar_tensor_tensor(uc[:, b, v, :], ub[:, b, v, w:w + T], tap,
                                                           uc[:, b, v, :], ALU.mult, ALU.add)
                        if w < 2:
                            ins.then_inc(dve_step, 1)
                        elif v == 1:
                            ins.then_inc(ffn_conv, 1)

            def ffn_multiply(b, n):
                dve.wait_ge(ffn_gelu, n + 1)
                dve.tensor_tensor(ffp[:, b, :], uc[:, b, 0, :], uc[:, b, 1, :], ALU.mult).then_inc(ffn_act, 1)

            def ffn_subtract(b, n):
                dve.wait_ge(ffn_rounded, n + 1)
                plane = slice(n, n + 1) if isinstance(n, int) else bass.ds(n, 1)
                dve.tensor_tensor(ff_lo[:, plane, :].rearrange("p a t -> p (a t)"), ffp[:, b, :],
                                  ff_hi[:, plane, :].rearrange("p a t -> p (a t)"),
                                  ALU.subtract).then_inc(ffn_split, 1)

            def ffn_step(s, n, it=0, first=False):
                if not first:
                    ffn_multiply((s + 1) % 2, n - 1)
                ffn_convolve(s, n, it)
                if not first:
                    ffn_subtract((s + 1) % 2, n - 1)

            for s in range(BANKS):
                ffn_step(s, s, first=(s == 0))
            with dve.Fori(1, KF // BANKS) as it:
                for s in range(BANKS):
                    ffn_step(s, it * BANKS + s, it)
            ffn_multiply((KF - 1) % 2, KF - 1)
            ffn_subtract((KF - 1) % 2, KF - 1)
            count[0] += 4 * KF
            for pr in range(4):
                c = plan["down"][3 * pr + 2]
                taken(dve, c)
                part = xres[:, 2 * pr:2 * pr + 2, :]
                dve.tensor_tensor(part, part, pair(aux[pr]), ALU.add).then_inc(x4_done, 1)
            dve.wait_ge(x4_done, 4)
            normalise(6, xres, yout, "final_norm_2")


def _per_partition(v, rows=P):
    v = np.moveaxis(np.asarray(v), -1, 0)
    v = v.reshape((v.shape[0] // rows, rows) + v.shape[1:])
    v = np.moveaxis(v, 1, 0).reshape(rows, -1)
    return np.concatenate([v, np.zeros((P - rows, v.shape[1]), v.dtype)]) if rows < P else v


def _layout(a):
    names = list(_VEC128) + ["conv_w", "ffn_conv_w_2", "ffn_conv_b_2"]
    flat = {n: (a[n][0] if n.endswith("_2") and a[n].ndim > 1 else a[n]) for n in names}
    cols = [_per_partition(flat[n]) for n in names]
    cols.append(_per_partition(a["fox_bf"], HEADS))
    for n in ("rnn_conv_w_2", "rnn_conv_b_2"):
        cols.append(_per_partition(a[n][0], C96))
    for n in ("rg_b_a_2", "rg_b_x_2", "rg_lambda_2", "gla_b_decay_2", "gla_norm_2"):
        cols.append(_per_partition(a[n][0].reshape(-1), C96))
    params = np.concatenate(cols, axis=1)
    keys = np.stack([a["peer_k1"], a["peer_k2"]], axis=1).reshape(HALVES, NK, DK // 2)
    u = a["peer_u"].reshape(P, P, KD, P)
    return {
        "xT": a["x"][0].T, "memT": a["mem_2"][0].T, "params": params, "w_in": a["w_in"],
        "w_conv_out": a["w_conv_out"], "w_fox_out": a["w_fox_out"], "w_out": a["w_out"],
        "peer_wq": a["peer_wq"], "keys": keys.transpose(2, 0, 1).reshape(P, -1),
        "uT": u.transpose(0, 3, 2, 1).reshape(P, P, D), "peer_v": a["peer_v"].reshape(P, P, D),
        "w_in_2": a["w_in_2"][0], "rg_w_a_2": a["rg_w_a_2"][0], "rg_w_x_2": a["rg_w_x_2"][0],
        "gla_w_decay_2": a["gla_w_decay_2"][0], "w_mem_kv_2": a["w_mem_kv_2"][0],
        "w_branch_2": a["w_branch_2"][0], "w_out_2": a["w_out_2"][0], "w_up_2": a["w_up_2"][0],
        "w_down_2": a["w_down_2"][0],
    }


def kernel(**inputs):
    import concourse.bacc as bacc
    from concourse.bass_utils import run_bass_kernel_spmd

    arrays = {n: np.ascontiguousarray(v) for n, v in _layout({n: np.asarray(v) for n, v in inputs.items()}).items()}
    nc = bacc.Bacc("TRN2", target_bir_lowering=False, num_devices=1)
    t = {n: nc.dram_tensor(f"in_{n}", v.shape, F32, kind="ExternalInput").ap() for n, v in arrays.items()}
    t["yT"] = nc.dram_tensor("yT", (D, T), F32, kind="ExternalOutput").ap()
    build(nc, t)
    r = run_bass_kernel_spmd(nc, [{f"in_{n}": v for n, v in arrays.items()}], core_ids=[0])
    return r.results[0]["yT"].T.reshape(1, T, D)
```

```python
from contextlib import ExitStack
import math

import numpy as np

import concourse.bass as bass
from concourse import mybir

F32 = mybir.dt.float32
F32R = mybir.dt.float32r
BF16 = mybir.dt.bfloat16
U32 = mybir.dt.uint32
ALU = mybir.AluOpType
ACT = mybir.ActivationFunctionType
AX = mybir.AxisListType

P = 128
T = 256
TT = T // P
D = 1024
KD = D // P
EPS = 1e-6
NEG = -1e30
TILE = 1024
RAW = 2
BANKS = 4
CW = 256
GROUP = 8

CONV_W = 31
HEADS, HD = 16, 64
QB = T // P
PH, NK, DK, TOPK = 8, 128, 256, 16
HALVES = 2 * PH
LOWEST = -3.4e38
A_VAL, A_GATE, Q0, K0, V0 = 0, 1024, 2048, 3072, 4096
F0 = 5120
GA0, GB0 = F0 + HEADS, F0 + HEADS + D

MEM = 256
MW = 768
C96 = 96
K96 = MW // C96
RNN_CONV = 4
GH, GDK, GDV, LOW = 4, 96, 192, 16
GCHUNK = 64
NCH = T // GCHUNK
MH, MHD = 4, 192
DFF = 3072
KF = DFF // P
Z_RNN = 0
Z_Q = Z_RNN + MW
Z_K = Z_Q + GH * GDK
Z_V = Z_K + GH * GDK
Z_G = Z_V + MW
Z_DEC = Z_G + MW
Z_MQ = Z_DEC + LOW
Z_GATE = Z_MQ + MW

_VEC128 = ["norm1_g", "conv_b", "conv_ln_g", "conv_ln_b", "norm2_g", "normf_g",
           "norm_mix_2", "mem_norm_2", "norm_ffn_2", "final_norm_2"]
PCOL = {}
_at = 0
for _n in _VEC128:
    PCOL[_n] = _at
    _at += KD
for _n, _w in (("conv_w", KD * CONV_W), ("ffn_conv_w_2", 2 * KF * 3), ("ffn_conv_b_2", 2 * KF),
               ("fox_bf", 1), ("rnn_conv_w_2", K96 * RNN_CONV), ("rnn_conv_b_2", K96),
               ("rg_b_a_2", K96), ("rg_b_x_2", K96), ("rg_lambda_2", K96),
               ("gla_b_decay_2", GH), ("gla_norm_2", K96)):
    PCOL[_n] = _at
    _at += _w
NPAR = _at


class Chunk:

    def __init__(self, index, raw, bank, split):
        self.index = index
        self.raw = raw
        self.bank = bank
        self.split = split
        self.landing = {}
        self.last = {}
        self.bank_use = 0
        self.tenant = 0


def plan_chunks():
    plan, order = {}, []
    landings, holder, bank_uses = {}, {}, [0] * BANKS
    banked_so_far, splits, tenant = 0, 0, 0

    def section(name, count, banked=True, split=True, tiles=(0, 1)):
        nonlocal banked_so_far, splits, tenant
        plan[name] = []
        for _ in range(count):
            c = Chunk(len(order), len(order) % RAW, banked_so_far % BANKS, splits if split else None)
            for v in tiles:
                at = (c.raw, v)
                landings[at] = landings.get(at, 0) + 1
                c.landing[v], c.last[v] = landings[at], holder.get(at)
                holder[at] = c
            if banked:
                bank_uses[c.bank] += 1
                c.bank_use = bank_uses[c.bank]
                banked_so_far += 1
            c.tenant = tenant
            if split:
                splits += 1
                tenant = c.index + 1
            order.append(c)
            plan[name].append(c)

    for j in range(4):
        section(f"conv_in{j}", 2)
    section("f", 1, split=False, tiles=(1,))
    for name in ("q", "k", "v", "ga", "gb"):
        section(name, 4)
    for name in ("conv_out", "fox_out", "mix_out"):
        section(name, 4)
    section("peer_q", 8)
    section("keys", 1, banked=False, split=False)
    section("u", P // 2)
    section("ev", P // 2, banked=False)
    section("mem_k", 4)
    section("mem_v", 3)
    section("z_rnn", 4)
    section("dec", 1, split=False, tiles=(1,))
    for name, count in (("zq", 2), ("zk", 2), ("zv", 3), ("zmq", 4), ("gate0", 4), ("zg", 4), ("branch0", 4),
                        ("gate1", 4), ("branch1", 4), ("gate2", 4), ("branch2", 4), ("out2", 4)):
        section(name, count)
    section("up", KF)
    section("down", 3 * 4, banked=False)
    return plan, order


def build(nc, t):
    plan, order = plan_chunks()
    ctx = ExitStack()
    with ctx:
        def sb(name, shape, dt=F32):
            return ctx.enter_context(nc.sbuf_tensor(name, shape, dt))

        def sem(name):
            return ctx.enter_context(nc.semaphore(name))

        gemm = [ctx.enter_context(nc.psum_tensor(f"gemm{i}", [P, 512], F32)) for i in range(BANKS)]
        aux = [ctx.enter_context(nc.psum_tensor(f"aux{i}", [P, 512], F32)) for i in range(4)]

        def pair(bank, rows=P):
            return bank[0:rows, :].rearrange("p (n t) -> p n t", n=2)

        raw = [[sb(f"raw{r}{v}", [P, TILE]) for v in range(2)] for r in range(RAW)]
        w_hi = [sb(f"w_hi{v}", [P, TILE], F32R) for v in range(2)]
        w_lo = [sb(f"w_lo{v}", [P, TILE], F32R) for v in range(2)]
        xres = sb("xres", [P, KD, T])
        h_hi = sb("h_hi", [P, KD, T], F32R)
        with nc.sbuf_tensor("mem_sq", [P, KD, T], F32) as mem_sq:
            pass
        h_lo = sb("h_lo", [P, KD, T], F32R)
        std = sb("std", [P, T])
        rstd = sb("rstd", [P, T])
        params = sb("params", [P, NPAR])
        ones = sb("ones", [P, P])
        ident = sb("ident", [P, P])
        zeros = sb("zeros", [P, P], BF16)
        iota = sb("iota", [P, P])
        keep = sb("keep", [P, T])
        epsc = sb("epsc", [P, 1])
        root = sb("root", [P, 1])
        with nc.sbuf_tensor("small", [P, 15 * T], F32) as small:
            pass
        mem_lo = sb("mem_lo", [P, KD, T], F32R)
        sb("small_rest", [P, 7 * T])
        with nc.sbuf_tensor("big", [P, P * T], F32) as big:
            pass
        y_hi = sb("y_hi", [P, KD, T], F32R)
        y_lo = sb("y_lo", [P, KD, T], F32R)
        m_lo = sb("m_lo", [P, KD, T], F32R)
        f_hi = sb("f_hi", [P, KF, T], F32R)
        f_lo = sb("f_lo", [P, KF, T], F32R)
        x_hi = sb("x_hi", [P, KD, T], F32R)
        x_lo = sb("x_lo", [P, KD, T], F32R)
        AT_M, AT_X, AFTER_X = (n * KD * T for n in (2, 9, 11))

        def carver(base, start=0):
            at = [start]

            def carve(*shape, rows=P, dt=F32):
                n = math.prod(shape) // (2 if dt == BF16 else 1)
                v = base[0:rows, at[0]:at[0] + n]
                at[0] += n
                assert at[0] <= base.shape[1], (at[0], shape)
                if dt != F32:
                    v = v.bitcast(dt)[:, 0:math.prod(shape)]
                names = "abcd"[:len(shape)]
                if len(shape) == 1:
                    return v
                return v.rearrange(f"p ({' '.join(names)}) -> p {' '.join(names)}",
                                   **dict(zip(names, shape)))
            return carve

        PROBS = 3
        carve = carver(big)
        PADC = CONV_W - 1
        sq = carve(KD, T)
        zc = carve(KD, PADC + T)
        zv = carve(KD, T)
        sig = carve(KD, T)
        qT = carve(KD, T)
        kT = carve(KD, T)
        vtok = carve(TT, D)
        fy, fa, fe, fl, fc, fc8 = [carve(T, rows=HEADS) for _ in range(6)]
        CPARTS, APART = 3, 32
        fc_parts = carve(T, rows=CPARTS * APART, dt=BF16)
        sel = carve(HEADS, P, rows=CPARTS * APART, dt=BF16)
        fc_part = carve(T, rows=HEADS, dt=BF16)
        mask = carve(T)
        carve = carver(big, AFTER_X)
        s_sb = carve(2, T)
        p_sb = carve(PROBS, T)
        pT_sb = carve(2, T)
        ob = carve(KD, T)
        x_sq = zv
        ga = carve(KD, T)
        gb = carve(KD, T)
        nmax, rsum, rrec = [carve(HEADS * QB) for _ in range(3)]
        act_peer = big[:, :].rearrange("p (i t) -> p i t", t=T)
        carve = carver(big, 64 * T)
        qp = carve(HALVES, T)
        ks = carve(TT, HALVES, NK)
        cand = carve(PH, TOPK * TOPK)
        eq = carve(PH, TOPK, TOPK)
        topv = carve(PH, 2, TOPK)
        topi = carve(PH, 2, TOPK, dt=U32)
        topif = carve(PH, 2, TOPK)
        sc = carve(TT, PH, TOPK)
        pos = carve(PH, TOPK, dt=U32)
        posp = carve(2, PH, TOPK, dt=U32)
        posf = carve(2, PH, TOPK)
        e1 = carve(TT, PH, TOPK)
        e2 = carve(TT, PH, TOPK)
        gsum = carve(TT, PH)
        grec = carve(TT, PH)
        carve = carver(small)
        e1T, e2T, gT = [carve(T) for _ in range(3)]
        gate_parts = carve(3, T, dt=BF16)
        hot = gT.bitcast(BF16).rearrange("p (g i) -> p g i", g=GROUP)
        hot1 = carve(2, 3, GROUP, P // 2, dt=BF16)
        hot2 = carve(2, GROUP, P, dt=BF16)
        a_hi, a_lo = [h_hi[:, i:i + 4, :].rearrange("p (c v) t -> p c v t", c=2) for i in (0, 4)]
        memT = small[:, 0:KD * T].rearrange("p (k t) -> p k t", t=T)
        carve = carver(big, KD * T)
        gate = carve(KD, T)
        merged = carve(KD, T)
        out_a = carve(K96, T, rows=C96)
        out_b = carve(K96, T, rows=C96)
        mk = carve(K96, T, rows=C96)
        xr = carve(K96, T, rows=C96)
        zq = carve(GH, T, rows=GDK)
        zk = carve(GH, T, rows=GDK)
        eg = carve(GH, T, rows=GDK)
        emg = carve(GH, T, rows=GDK)
        rg = carve(K96, T, rows=C96)
        ig = carve(K96, T, rows=C96)
        mv = carve(TT, MW)
        zr = carve(K96, RNN_CONV - 1 + T, rows=C96)
        states = carve(GH, NCH - 1, GDV, rows=GDK)
        vg = carve(TT, MW)
        kendT = carve(TT, GH, GDK)
        rwa = carve(K96, C96, rows=C96)
        rwx = carve(K96, C96, rows=C96)
        lam = [carve(K96, rows=C96) for _ in range(7)]
        decay = carve(GH, NCH, rows=GDK)
        mnm, msum, mrec = [carve(MH * QB) for _ in range(3)]
        ra = zr.rearrange("p a b -> p (a b)")[:, 0:K96 * T].rearrange("p (a b) -> p a b", b=T)
        rt = states.rearrange("p h n v -> p (h n v)")[:, 0:K96 * T].rearrange("p (a b) -> p a b", b=T)
        sg = xr
        carve = carver(big, AT_M)
        mq = carve(K96, T, rows=C96)
        dec = carve(T, rows=LOW)
        wdec = carve(GH, GDK, rows=LOW)
        carve = carver(big, AT_M + 5 * KD * T)
        out_c = carve(K96, T, rows=C96)
        third = [slice(n * KD, (n + 1) * KD) for n in range(3)]
        a_parts = (x_hi[0:C96], f_hi[0:C96, third[0], :])
        b_parts = (x_lo[0:C96], f_hi[0:C96, third[1], :])
        c_parts = (f_hi[0:C96, third[2], :], f_lo[0:C96, third[1], :])
        m_parts = (x_hi, m_lo)
        carve = carver(small)
        gy = carve(GH, T, rows=GDK)
        gl = carve(GH, T, rows=GDK)
        ekd = gy
        mp = carve(2, MEM)
        sT = carve(GH, TT, GCHUNK)
        mpT = carve(TT, T)
        carve = carver(big, KD * T)
        ub = carve(2, 2, 2 + T)
        uc = carve(2, 2, T)
        ffp = carve(2, T)
        carve = carver(big, AT_X)
        yout = carve(KD, T)

        landed = [[sem(f"landed{r}{v}") for v in range(2)] for r in range(RAW)]
        hi_ready = [sem(f"hi_ready{v}") for v in range(2)]
        lo_ready = [sem(f"lo_ready{v}") for v in range(2)]
        hi_used = [sem(f"hi_used{v}") for v in range(2)]
        tile_done = [sem(f"tile_done{v}") for v in range(2)]
        evacuated = [sem(f"evacuated{i}") for i in range(BANKS)]
        x_in = [sem(f"x_in{n}") for n in range(4)]
        (params_in, consts, squared, paired, sumsq, stdev, rstd_done, normed, h_ready, h_rounded, h_split,
         y_rounded, y_split, ob_rounded, ob_split,
         dve_step, f_abs, f_exp, f_soft, c_ready, sel_ready, conv_done, mean_ready, centered,
         ln_squared, ln_paired, ln_sumsq, ln_std, ln_scaled, ln_sig, conv_act, gates_on,
         scores_ready, scores_moved, negmax_ready, exp_done, probs_ready, pT_psum, pT_ready, pv_done,
         ob_ready, mix_ready) = [sem(n) for n in (
             "params_in consts squared paired sumsq stdev rstd_done normed h_ready h_rounded h_split "
             "y_rounded y_split ob_rounded ob_split "
             "dve_step f_abs f_exp f_soft c_ready sel_ready conv_done mean_ready centered "
             "ln_squared ln_paired ln_sumsq ln_std ln_scaled ln_sig conv_act gates_on "
             "scores_ready scores_moved negmax_ready exp_done probs_ready pT_psum pT_ready pv_done "
             "ob_ready mix_ready").split()]
        (keys_scored, keys_moved, topk_done, gate_exp, gates_ready, routed_psum, routed,
         mem_rounded, mem_split, a_rounded, a_split, x2_done, experts_done) = [sem(n) for n in (
             "keys_scored keys_moved topk_done gate_exp gates_ready routed_psum routed "
             "mem_rounded mem_split a_rounded a_split x2_done experts_done").split()]
        hot_ready = sem("hot_ready")
        hots_ready = [sem(f"hots_ready{b}") for b in range(2)]
        planes_ready = [sem(f"planes_ready{b}") for b in range(2)]
        planes_used = [sem(f"planes_used{b}") for b in range(2)]
        (mem_in, rg_in, wdec_in, pads2, rnn_conv, rg_psum, rg_moved, lam_abs, lam_exp, lam_ln, lam_ready,
         la_ready, a_ready, tanh_ready, w_ready, root_ready, ig_used, rnn_done,
         dec_psum, gla_y, gla_abs, gla_soft, gla_sum, gla_exp, gla_qk, kend_psum, kend_moved,
         gla_scored, gla_scores_moved, gla_masked, states_psum, states_done, o_psum, o_squared,
         o_sumsq, o_std, out_b_done, sg_sig, gate0_on,
         outa_rounded, outa_split, outb_rounded, outb_split, outc_rounded, outc_split,
         m_rounded, m_split,
         ms_psum, ms_max, ms_exp, ms_probs, mpT_psum, mpT_moved, mo_psum, mo_moved, merge_done,
         ffn_pads, ffn_conv, ffn_gelu, ffn_act, ffn_rounded, ffn_split, x4_done, stored) = [sem(n) for n in (
             "mem_in rg_in wdec_in pads2 rnn_conv rg_psum rg_moved lam_abs lam_exp lam_ln lam_ready "
             "la_ready a_ready tanh_ready w_ready root_ready ig_used rnn_done "
             "dec_psum gla_y gla_abs gla_soft gla_sum gla_exp gla_qk kend_psum kend_moved "
             "gla_scored gla_scores_moved gla_masked states_psum states_done o_psum o_squared "
             "o_sumsq o_std out_b_done sg_sig gate0_on "
             "outa_rounded outa_split outb_rounded outb_split outc_rounded outc_split "
             "m_rounded m_split "
             "ms_psum ms_max ms_exp ms_probs mpT_psum mpT_moved mo_psum mo_moved merge_done "
             "ffn_pads ffn_conv ffn_gelu ffn_act ffn_rounded ffn_split x4_done stored").split()]
        N_CONSTS = 13
        GATE_STEPS, CONV_STEPS = (3, 7, 11, 15), (19, 23, 27, 31)

        def par(name, col=0, rows=P, n=1):
            c = PCOL[name] + col
            return params[0:rows, c:c + n]

        def by_k(tile, m, rows=P, n=KD):
            return tile[0:rows, 0:n * m].rearrange("p (k m) -> p k m", m=m)

        def taken(eng, c, it=0):
            eng.wait_ge(tile_done[1], it * BANKS + (c.index + 1))

        def moved(eng, chunks):
            for b in sorted({c.bank for c in chunks}):
                eng.wait_ge(evacuated[b], max(c.bank_use for c in chunks if c.bank == b))

        def subtract(eng, c, it=None, tiles=(0, 1), n=TILE):
            for v in tiles:
                if it is None:
                    eng.wait_ge(hi_ready[v], c.split + 1)
                    if c.tenant:
                        eng.wait_ge(tile_done[v], c.tenant)
                else:
                    eng.wait_ge(hi_ready[v], it * BANKS + (c.split + 1))
                    eng.wait_ge(tile_done[v], it * BANKS + c.index)
                rows = tile_rows.get(c.index, P)
                eng.tensor_tensor(w_lo[v][0:rows, 0:n], raw[c.raw][v][0:rows, 0:n], w_hi[v][0:rows, 0:n],
                                  ALU.subtract).then_inc(lo_ready[v], 1)

        NARROW = {name: KD * C96 for name in ("mem_k", "z_rnn", "zq", "zk", "zg", "zmq")}
        floats = {c.index: NARROW.get(name, TILE) for name, chunks in plan.items() for c in chunks}
        tile_rows = {c.index: C96 for name in ("branch0", "branch1", "branch2") for c in plan[name]}
        ITS = P // (2 * BANKS)
        HALF = P // 4
        MEM_NORM = 2 * HALF - 3 * BANKS
        ROUTED = 5

        NORM_WAIT = 16

        block = ctx.enter_context(nc.Block())

        @block.sync
        def _(sp):
            for n in range(4):
                part = slice(2 * n, 2 * n + 2)
                sp.dma_start(xres[:, part, :], t["xT"].rearrange("(k p) t -> p k t", p=P)[:, part, :]).then_inc(x_in[n], 16)
            sp.dma_start(params[:, :], t["params"]).then_inc(params_in, 16)

            def load(c, v, src):
                last = c.last[v]
                if last is not None and last.split is not None:
                    sp.wait_ge(lo_ready[v], last.split + 1)
                elif last is not None:
                    sp.wait_ge(tile_done[v], last.index + 1)
                rows, n = src.shape
                sp.dma_start(raw[c.raw][v][0:rows, 0:n], src).then_inc(landed[c.raw][v], 16)

            def looped(name):
                for s in range(BANKS):
                    for v in range(2):
                        load(plan[name][s], v, t[f"w_{name}"][2 * s + v])
                with sp.Fori(1, len(plan[name]) // BANKS) as it:
                    for s in range(BANKS):
                        c = plan[name][s]
                        for v in range(2):
                            sp.wait_ge(lo_ready[v], it * BANKS + (c.split - RAW + 1))
                            src = t[f"w_{name}"][bass.ds(it * 2 * BANKS + (2 * s + v), 1), :, :]
                            sp.dma_start(raw[c.raw][v][:, :], src.rearrange("i p n -> p (i n)")
                                         ).then_inc(landed[c.raw][v], 16)

            for name, chunks in plan.items():
                if name in ("u", "ev", "up"):
                    looped(name)
                    continue
                for i, c in enumerate(chunks):
                    for n, v in enumerate(c.landing):
                        load(c, v, t[f"w_{name}"][len(c.landing) * i + n])
            for n in range(4):
                part = slice(2 * n, 2 * n + 2)
                sp.wait_ge(normed, 2 + n + 1)
                sp.dma_start(t["yT"].rearrange("(k p) t -> p k t", p=P)[:, part, :], yout[:, part, :]).then_inc(stored, 16)
            sp.wait_ge(stored, 4 * 16)

        @block.gpsimd
        def _(pool):
            pool.memset(epsc[:, :], EPS).then_inc(consts, 1)
            pool.memset(ones[:, :], 1.0).then_inc(consts, 1)
            pool.memset(zeros[:, :], 0.0).then_inc(consts, 1)
            pool.memset(zc[:, :, 0:PADC], 0.0).then_inc(consts, 1)
            pool.iota(iota[:, :], [[1, P]], base=0, channel_multiplier=0,
                      allow_small_or_imprecise_dtypes=True).then_inc(consts, 1)
            pool.memset(ident[:, :], 0.0).then_inc(consts, 1)
            pool.memset(mask, 0.0).then_inc(consts, 1)
            pool.memset(sel, 0.0).then_inc(consts, 1)
            pool.memset(fc_parts, 0.0).then_inc(consts, 1)
            pool.memset(keep[:, :], 1.0).then_inc(consts, 1)
            pool.wait_ge(consts, 10)
            pool.memset(keep[:, :].rearrange("p (n i) -> p n i", i=GCHUNK)[:, :, 0:1], 0.0).then_inc(consts, 1)
            pool.affine_select(out=ident[:, :], in_=ident[:, :], compare_op=ALU.not_equal, fill=1.0,
                               base=0, pattern=[[-1, P]], channel_multiplier=1).then_inc(consts, 1)
            pool.affine_select(out=mask[:, P:T], in_=mask[:, P:T], compare_op=ALU.is_ge, fill=NEG, base=0,
                               pattern=[[-1, P]], channel_multiplier=1).then_inc(consts, 1)
            def sections(first, last):
                for c in order[plan[first][0].index:plan[last][-1].index + 1]:
                    if c.split is not None:
                        subtract(pool, c, n=floats[c.index])

            def planes(first, its, tiles):
                with pool.Fori(0, its) as it:
                    for c in order[first.index:first.index + BANKS]:
                        subtract(pool, c, it, tiles)

            sections("conv_in0", "peer_q")
            planes(plan["u"][0], ITS // 2, (0, 1))
            planes(plan["u"][HALF], ITS // 2, (1,))
            planes(plan["ev"][0], ITS // 2, (1,))
            for b in range(2):
                pool.wait_ge(planes_used[b], HALF + 1)
            pool.dma_start(memT, t["memT"].rearrange("(k p) t -> p k t", p=P)).then_inc(mem_in, 16)
            planes(plan["ev"][HALF], ITS // 2, (1,))
            subtract(pool, plan["mem_k"][0], n=floats[plan["mem_k"][0].index])
            pool.wait_ge(x2_done, BANKS)
            pool.dma_start(rwa, t["rg_w_a_2"].rearrange("h i j -> i h j")).then_inc(rg_in, 16)
            pool.dma_start(rwx, t["rg_w_x_2"].rearrange("h i j -> i h j")).then_inc(rg_in, 16)
            pool.dma_start(wdec, t["gla_w_decay_2"].rearrange("l (h d) -> l h d", h=GH)).then_inc(wdec_in, 16)
            pool.memset(zr[:, :, 0:RNN_CONV - 1], 0.0).then_inc(pads2, 1)
            for c in plan["mem_k"][1:]:
                subtract(pool, c, n=floats[c.index])
            sections("mem_v", "zg")
            for v in range(2):
                pool.wait_ge(lo_ready[v], plan["zg"][-1].split + 1)
            pool.wait_ge(gla_scores_moved, 1)
            for hp in range(2):
                part = sT[hp * GCHUNK:(hp + 1) * GCHUNK].rearrange("p h n i -> p (h n) i")
                pool.affine_select(out=part, in_=part, compare_op=ALU.is_ge, fill=0.0, base=0,
                                   pattern=[[0, GH * TT], [1, GCHUNK]], channel_multiplier=-1
                                   ).then_inc(gla_masked, 1)
            pool.wait_ge(gla_masked, 2)
            sections("branch0", "out2")
            with pool.Fori(0, KF // BANKS) as it:
                for c in plan["up"][:BANKS]:
                    subtract(pool, c, it)
            sections("down", "down")

        @block.tensor
        def _(pe):
            def product(c, m, it=None, x=(h_hi, h_lo), rows=P):
                for v in range(2):
                    product_tile(c, v, m, it, x, rows)

            def bank_free(c, it=None):
                if it is not None:
                    pe.wait_ge(evacuated[c.bank], it + (c.bank_use - 1))
                elif c.bank_use > 1:
                    pe.wait_ge(evacuated[c.bank], c.bank_use - 1)

            def product_tile(c, v, m, it=None, x=(h_hi, h_lo), rows=P):
                if v == 0:
                    bank_free(c, it)
                chunks = 0 if it is None else it * BANKS
                out = pair(gemm[c.bank], m)[:, v, :]
                pe.wait_ge(hi_ready[v], chunks + (c.split + 1))
                w = by_k(w_hi[v], m, rows)
                for n, act_part in enumerate(x):
                    for k in range(KD):
                        mm = pe.matmul(out, w[:, k, :], act_part[:, k, :], start=(n == k == 0), stop=False)
                mm.then_inc(hi_used[v], 1)
                pe.wait_ge(lo_ready[v], chunks + (c.split + 1))
                w = by_k(w_lo[v], m, rows)
                for k in range(KD):
                    mm = pe.matmul(out, w[:, k, :], x[0][:, k, :], start=False, stop=(k == KD - 1))
                mm.then_inc(tile_done[v], 1)

            def paced_product(c, m, rounded, split, before, x=(h_hi, h_lo), step=2):
                bank_free(c)
                both = pair(gemm[c.bank], m)
                hi, lo = [by_k(w, m) for w in w_hi], by_k(w_lo[0], m)
                for v in range(2):
                    pe.wait_ge(hi_ready[v], c.split + 1)
                for k in range(KD):
                    if k % step == 0:
                        pe.wait_ge(rounded, before + k // step + 1)
                    for v in range(2):
                        pe.matmul(both[:, v, :], hi[v][:, k, :], x[0][:, k, :], start=(v == k == 0), stop=False,
                                  skip_group_check=True)
                    if k == 0:
                        pe.wait_ge(lo_ready[0], c.split + 1)
                    mm = pe.matmul(both[:, 0, :], lo[:, k, :], x[0][:, k, :], start=False, stop=False,
                                   skip_group_check=True)
                mm.then_inc(tile_done[0], 1)
                for v in range(2):
                    for k in range(KD):
                        if v == 0 and k % step == 0:
                            pe.wait_ge(split, before + k // step + 1)
                        mm = pe.matmul(both[:, v, :], hi[v][:, k, :], x[1][:, k, :], start=False,
                                       stop=(v == 0 and k == KD - 1), skip_group_check=True)
                    mm.then_inc(hi_used[v], 1)
                pe.wait_ge(lo_ready[1], c.split + 1)
                lo = by_k(w_lo[1], m)
                for k in range(KD):
                    mm = pe.matmul(both[:, 1, :], lo[:, k, :], x[0][:, k, :], start=False, stop=(k == KD - 1),
                                   skip_group_check=True)
                mm.then_inc(tile_done[1], 1)

            def keep_warm(count):
                for _ in range(count):
                    pe.matmul(aux[2][:, :], zeros[:, :], zeros[:, :].unsqueeze(1).to_broadcast([P, 4, P]),
                              start=True, stop=True)

            def narrow(c, m, src):
                pe.wait_ge(landed[c.raw][1], 16 * c.landing[1])
                pe.wait_ge(evacuated[c.bank], c.bank_use - 1)
                w = by_k(raw[c.raw][1], m)
                for k in range(KD):
                    mm = pe.matmul(gemm[c.bank][0:m, 0:T], w[:, k, :], src[:, k, :],
                                   start=(k == 0), stop=(k == KD - 1))
                    if k == 0:
                        mm.then_inc(tile_done[0], 1)
                mm.then_inc(tile_done[1], 1)

            def by_token(c, x=(h_hi, h_lo)):
                pe.wait_ge(evacuated[c.bank], c.bank_use - 1)

                def part(x, w, v, begins=False, ends=False):
                    for tt in range(TT):
                        for k in range(KD // 2):
                            mm = pe.matmul(pair(gemm[c.bank])[:, tt, :],
                                           x[:, v * KD // 2 + k, tt * P:(tt + 1) * P], w[:, k, :],
                                           start=(begins and tt == k == 0), stop=(ends and k == KD // 2 - 1),
                                           skip_group_check=True)
                    return mm

                for v in range(2):
                    pe.wait_ge(hi_ready[v], c.split + 1)
                    w = by_k(w_hi[v], CW, n=KD // 2)
                    part(x[0], w, v, begins=(v == 0))
                    part(x[1], w, v).then_inc(hi_used[v], 1)
                    pe.wait_ge(lo_ready[v], c.split + 1)
                    part(x[0], by_k(w_lo[v], CW, n=KD // 2), v, ends=(v == 1)).then_inc(tile_done[v], 1)

            def sum_pair(i, n, src=sq, bank=aux[3]):
                pe.wait_ge(paired, 4 * i + n + 1)
                mm = pe.matmul(bank[:, 0:T], ones[:, :], src[:, 2 * n, :], start=(n == 0), stop=(n == 3),
                               skip_group_check=True)
                if n == 3:
                    mm.then_inc(sumsq, 1)

            def sum_squares(i, src=sq):
                for n in range(4):
                    sum_pair(i, n, src)

            pe.wait_ge(consts, 3)
            keep_warm(7)
            sum_squares(0)
            keep_warm(NORM_WAIT)
            paced_product(order[0], P, h_rounded, h_split, 0)
            for c in order[1:plan["f"][0].index]:
                product(c, P)
            narrow(plan["f"][0], HEADS, sq)
            for c in plan["q"] + plan["k"]:
                product(c, P)
            for c in plan["v"]:
                by_token(c)
            product(plan["ga"][0], P)
            pe.wait_ge(conv_done, 1)
            for k in range(KD // 2):
                mm = pe.matmul(aux[2][:, 0:T], ones[:, :], sq[:, k, :], start=(k == 0), stop=(k == KD // 2 - 1))
            mm.then_inc(mean_ready, 1)
            product(plan["ga"][1], P)
            pe.wait_ge(ln_paired, 1)
            for k in range(KD // 2):
                mm = pe.matmul(aux[3][:, 0:T], ones[:, :], sq[:, k, :], start=(k == 0), stop=(k == KD // 2 - 1))
            mm.then_inc(ln_sumsq, 1)
            product(plan["ga"][2], P)

            def scores(u):
                h, qb = divmod(u, QB)
                lo, nk = (h % 2) * HD, (qb + 1) * P
                if u >= 2:
                    pe.wait_ge(scores_moved, u - 1)
                pe.matmul(aux[u % 2][:, 0:nk], qT[lo:lo + HD, h // 2, qb * P:(qb + 1) * P],
                          kT[lo:lo + HD, h // 2, 0:nk], start=True, stop=False)
                pe.matmul(aux[u % 2][:, 0:nk], sel[:, h, :], fc_parts[:, 0:nk],
                          start=False, stop=True).then_inc(scores_ready, 1)

            def turn_probs(u):
                qb = u % QB
                pe.wait_ge(probs_ready, u + 1)
                if u >= 1:
                    pe.wait_ge(pT_ready, u)
                for kb in range(qb + 1):
                    mm = pe.transpose(aux[2][:, kb * P:(kb + 1) * P], p_sb[:, u % PROBS, kb * P:(kb + 1) * P],
                                      ident[:, :])
                mm.then_inc(pT_psum, 1)

            def values(u):
                h, qb = divmod(u, QB)
                lo = (h % 2) * HD
                pe.wait_ge(pT_ready, u + 1)
                if u % 4 == 0 and u:
                    pe.wait_ge(ob_ready, u // 4)
                for kb in range(qb + 1):
                    mm = pe.matmul(aux[3][lo:lo + HD, qb * P:(qb + 1) * P], vtok[:, kb, h * HD:(h + 1) * HD],
                                   pT_sb[:, u % 2, kb * P:(kb + 1) * P], start=(kb == 0), stop=(kb == qb))
                mm.then_inc(pv_done, 1)

            pe.wait_ge(consts, N_CONSTS)
            moved(pe, plan["q"] + plan["k"] + plan["v"])
            pe.wait_ge(c_ready, 1)
            pe.wait_ge(sel_ready, CPARTS)
            scores(0)
            scores(1)
            product(plan["ga"][3], P)
            pe.wait_ge(ln_std, 1)
            UNITS = HEADS * QB
            for u in range(UNITS + PROBS + 1):
                if 2 <= u < UNITS:
                    scores(u)
                if PROBS <= u < UNITS + PROBS:
                    turn_probs(u - PROBS)
                for v, at in enumerate((u + 2, u)):
                    if at in GATE_STEPS:
                        product_tile(plan["gb"][GATE_STEPS.index(at)], v, P)
                    if at in CONV_STEPS:
                        if u + 2 == CONV_STEPS[0]:
                            pe.wait_ge(y_split, 2)
                        product_tile(plan["conv_out"][CONV_STEPS.index(at)], v, P, x=(y_hi, y_lo))
                if u > PROBS:
                    values(u - PROBS - 1)
            paced_product(plan["fox_out"][0], P, ob_rounded, ob_split, 0, (x_hi, x_lo), step=1)
            for c in plan["fox_out"][1:]:
                product(c, P, x=(x_hi, x_lo))
            paced_product(plan["mix_out"][0], P, y_rounded, y_split, 2, (y_hi, y_lo))
            for i, c in enumerate(plan["mix_out"][1:]):
                product(c, P, x=(y_hi, y_lo))
                sum_pair(1, i, x_sq)
            sum_pair(1, 3, x_sq)
            keep_warm(NORM_WAIT)

            paced_product(plan["peer_q"][0], P, h_rounded, h_split, 4)
            for c in plan["peer_q"][1:]:
                product(c, P)
            kc = plan["keys"][0]
            for v in range(2):
                pe.wait_ge(landed[kc.raw][v], 16 * kc.landing[v])
            for g in range(TT * 4):
                tt, h0 = divmod(4 * g, HALVES)
                if g >= 4:
                    pe.wait_ge(keys_moved, g - 3)
                else:
                    moved(pe, plan["peer_q"][2 * g:2 * g + 2])
                for i in range(4):
                    v, at = divmod(h0 + i, HALVES // 2)
                    mm = pe.matmul(aux[g % 4][:, i * NK:(i + 1) * NK], qp[:, h0 + i, tt * P:(tt + 1) * P],
                                   raw[kc.raw][v][:, at * NK:(at + 1) * NK], start=True, stop=True)
                mm.then_inc(keys_scored, 1)
            pe.wait_ge(keys_scored, TT * 4)
            pe.sem_inc(tile_done[0], 1)
            pe.sem_inc(tile_done[1], 1)

            def expert_scores(first, last):
                with pe.Fori(first, last) as it:
                    for c in plan["u"][:BANKS]:
                        product(c, P, it)

            expert_scores(0, ROUTED + 1)
            pe.wait_ge(gates_ready, 1)
            for n, src in enumerate((e1, e2, sc)):
                for tt in range(TT):
                    mm = pe.transpose(aux[n][:, tt * P:(tt + 1) * P],
                                      src[:, tt].rearrange("p h k -> p (h k)"), ident[:, :])
                mm.then_inc(routed_psum, 1)
            expert_scores(ROUTED + 1, ITS // 2)

            def gate_planes(half, s, it):
                b = s % 2
                pe.wait_ge(hots_ready[b], it * 2 + (half * HALF // 2 + s // 2 + 1))
                pe.wait_ge(planes_used[b], it * 2 + (half * HALF // 2 + s // 2 + 1))
                for n in range(GROUP):
                    for part in range(3):
                        mm = pe.matmul(aux[b][:, n * P // 2:(n + 1) * P // 2], hot2[:, b, n, :],
                                       hot1[:, b, part, n, :], start=(part == 0), stop=(part == 2))
                mm.then_inc(planes_ready[b], 1)

            with pe.Fori(0, ITS // 2) as it:
                for s in range(BANKS):
                    gate_planes(0, s, it)
                    product(plan["u"][HALF + s], P, it)
            moved(pe, plan["u"])
            for b in range(4):
                pe.matmul(gemm[b][:, :], zeros[:, :],
                          zeros[:, :].unsqueeze(1).to_broadcast([P, 4, P]), start=True, stop=False,
                          skip_group_check=True)

            def expert_values(c, it):
                for v in range(2):
                    pe.wait_ge(hi_ready[v], it * BANKS + (c.split + 1))
                    steps = ((w_hi, a_hi, a_rounded), (w_hi, a_lo, a_split), (w_lo, a_hi, lo_ready[v]))
                    for w, a, ready in steps:
                        n = c.split + 1 if w is w_lo else c.index - plan["ev"][0].index + 1
                        pe.wait_ge(ready, it * BANKS + n)
                        for d in range(KD):
                            mm = pe.matmul(pair(gemm[d // 2])[:, d % 2, :], w[v][:, d * P:(d + 1) * P],
                                           a[:, c.raw, v, :], start=False, stop=False, skip_group_check=True)
                        if a is a_lo:
                            mm.then_inc(hi_used[v], 1)
                    mm.then_inc(tile_done[v], 1)

            with pe.Fori(0, ITS // 2) as it:
                for s in range(BANKS):
                    gate_planes(1, s, it)
                    expert_values(plan["ev"][s], it)
            for first, last in ((HALF, MEM_NORM), (MEM_NORM, 2 * HALF)):
                with pe.Fori(0, (last - first) // BANKS) as it:
                    for c in plan["ev"][first:first + BANKS]:
                        expert_values(c, it)
                if first == HALF:
                    sum_squares(2, mem_sq)
            for b in range(4):
                pe.matmul(gemm[b][:, :], zeros[:, :],
                          zeros[:, :].unsqueeze(1).to_broadcast([P, 4, P]), start=False, stop=True,
                          skip_group_check=True).then_inc(experts_done, 1)

            pe.wait_ge(mem_split, 2)
            for i, c in enumerate(plan["mem_k"]):
                pe.wait_ge(x2_done, c.bank + 1)
                product(c, C96, x=(h_lo, mem_lo))
                if i == 0:
                    sum_squares(3)
                if i == 2:
                    sum_squares(4)
            for c in plan["mem_v"]:
                by_token(c, (h_lo, mem_lo))
            paced_product(plan["z_rnn"][0], C96, h_rounded, h_split, 8)
            for c in plan["z_rnn"][1:]:
                product(c, C96)
            narrow(plan["dec"][0], LOW, sq)
            for c in plan["zq"] + plan["zk"]:
                product(c, C96)
            moved(pe, plan["dec"])
            pe.wait_ge(wdec_in, 16)
            for h in range(GH):
                mm = pe.matmul(pair(aux[h // 2], GDK)[:, h % 2, :], wdec[:, h, :], dec, start=True, stop=True)
            mm.then_inc(dec_psum, 1)
            for c in plan["zv"]:
                by_token(c)
            pe.wait_ge(rg_in, 32)
            for h in range(K96):
                if h % 2 == 0:
                    product(plan["zmq"][h // 2], C96)
                pe.wait_ge(rnn_conv, h + 1)
                if h >= 2:
                    pe.wait_ge(rg_moved, 2 * (h - 1))
                bank = pair(aux[2 + h % 2], C96)
                pe.matmul(bank[:, 0, :], rwa[:, h, :], xr[:, h, :], start=True, stop=True)
                pe.matmul(bank[:, 1, :], rwx[:, h, :], xr[:, h, :], start=True, stop=True).then_inc(rg_psum, 1)

            def mem_scores(u):
                h, qb = divmod(u, QB)
                if u >= 2:
                    pe.wait_ge(ms_exp, u - 1)
                if qb == 0:
                    moved(pe, plan["zmq"][h:h + 1])
                for vh in range(2):
                    mm = pe.matmul(aux[u % 2][:, 0:MEM], mq[:, 2 * h + vh, qb * P:(qb + 1) * P],
                                   mk[:, 2 * h + vh, :], start=(vh == 0), stop=(vh == 1))
                mm.then_inc(ms_psum, 1)

            def mem_turn(u):
                pe.wait_ge(ms_probs, u + 1)
                if u:
                    pe.wait_ge(mpT_moved, u)
                for mt in range(TT):
                    mm = pe.transpose(aux[2][:, mt * P:(mt + 1) * P], mp[:, u % 2, mt * P:(mt + 1) * P],
                                      ident[:, :])
                mm.then_inc(mpT_psum, 1)

            def mem_values(h):
                pe.wait_ge(mpT_moved, 2 * h + 2)
                if h:
                    pe.wait_ge(mo_moved, h)
                for vh in range(2):
                    for mt in range(TT):
                        mm = pe.matmul(pair(aux[3], C96)[:, vh, :],
                                       mv[:, mt, h * MHD + vh * C96:h * MHD + (vh + 1) * C96],
                                       mpT[:, mt, :], start=(mt == 0), stop=(mt == TT - 1))
                mm.then_inc(mo_psum, 1)

            pe.wait_ge(gla_y, GH)
            moved(pe, plan["mem_k"] + plan["mem_v"])
            for u in range(MH * QB):
                mem_scores(u)
                if u >= 3 and u % 2:
                    mem_values((u - 3) // 2)
                product_tile(plan["gate0"][u // 2], u % 2, P)
                if u == 1:
                    pe.wait_ge(rg_moved, 2 * K96)
                if u:
                    mem_turn(u - 1)
            product_tile(plan["zg"][0], 0, C96)
            mem_turn(MH * QB - 1)
            pe.wait_ge(gla_qk, 3)
            pe.wait_ge(ms_exp, MH * QB)
            for tt in range(TT):
                for h in range(GH):
                    mm = pe.transpose(aux[tt][:, h * GDK:(h + 1) * GDK], ekd[:, h, tt * P:(tt + 1) * P],
                                      ident[0:GDK, 0:GDK])
                mm.then_inc(kend_psum, 1)
            product_tile(plan["zg"][0], 1, C96)
            mem_values(MH - 1)
            pe.wait_ge(mpT_moved, MH * QB)
            for h in range(GH):
                for n in range(NCH):
                    lo, cols = (n % 2) * GCHUNK, slice(n * GCHUNK, (n + 1) * GCHUNK)
                    at_col = (h * TT + n // 2) * GCHUNK
                    mm = pe.matmul(aux[2][lo:lo + GCHUNK, at_col:at_col + GCHUNK], emg[:, h, cols],
                                   eg[:, h, cols], start=True, stop=True)
            mm.then_inc(gla_scored, 1)

            def gla_states(n):
                lo = (n % 2) * GCHUNK
                for half in range(2):
                    bank = aux[half if n % 2 == 0 else 2 + half]
                    if n == 1:
                        pe.wait_ge(gla_scores_moved, 1)
                        pe.wait_ge(mo_moved, MH)
                    if n == 2:
                        pe.wait_ge(states_done, half + 1)
                    for i in range(2):
                        h = 2 * half + i
                        mm = pe.matmul(bank[0:GDK, i * GDV:(i + 1) * GDV],
                                       kendT[lo:lo + GCHUNK, n // 2, h, :],
                                       vg[lo:lo + GCHUNK, n // 2, h * GDV:(h + 1) * GDV],
                                       start=True, stop=True)
                    mm.then_inc(states_psum, 1)

            product(plan["zg"][1], C96)
            pe.wait_ge(kend_moved, TT)
            moved(pe, plan["zv"])
            gla_states(0)
            gla_states(1)
            product(plan["zg"][2], C96)
            gla_states(2)
            product(plan["zg"][3], C96)
            pe.wait_ge(gla_masked, 2)
            pe.wait_ge(states_done, 2 + GH * (NCH - 2))
            def gla_out(h):
                for parity in range(2):
                    lo = parity * GCHUNK
                    bank = aux[2 * (h % 2) + parity][0:C96, 0:T].rearrange("p (v n i) -> p v n i", v=2, n=TT)
                    if h >= 2 and parity == 0:
                        pe.wait_ge(o_std, h - 1)
                    for vh in range(2):
                        vcols = slice(h * GDV + vh * C96, h * GDV + (vh + 1) * C96)
                        for half in range(TT):
                            n = 2 * half + parity
                            cols = slice(n * GCHUNK, (n + 1) * GCHUNK)
                            mm = pe.matmul(bank[:, vh, half, :], vg[lo:lo + GCHUNK, half, vcols],
                                           sT[lo:lo + GCHUNK, h, half, :], start=True, stop=(n == 0))
                            if n:
                                mm = pe.matmul(bank[:, vh, half, :], states[:, h, n - 1, vh * C96:(vh + 1) * C96],
                                               eg[:, h, cols], start=False, stop=True)
                    mm.then_inc(o_psum, 1)

            def gla_sumsq(h):
                pe.wait_ge(o_squared, 2 * h + 2)
                for vh in range(2):
                    mm = pe.matmul(aux[2 * (h % 2)][0:C96, 0:T], ones[0:C96, 0:C96], sq[0:C96, 2 * h + vh, :],
                                   start=(vh == 0), stop=(vh == 1))
                mm.then_inc(o_sumsq, 1)

            for h0 in range(0, GH, 2):
                for i, stage in enumerate((gla_out, gla_sumsq)):
                    stage(h0)
                    stage(h0 + 1)
                    pe.wait_ge(outa_split, 2)
                    product(plan["branch0"][h0 + i], P, x=a_parts, rows=C96)
            for c in plan["gate1"]:
                product(c, P)
            pe.wait_ge(outb_split, 2)
            for c in plan["branch1"]:
                product(c, P, x=b_parts, rows=C96)
            for c in plan["gate2"]:
                product(c, P)
            pe.wait_ge(outc_split, 2)
            for c in plan["branch2"]:
                product(c, P, x=c_parts, rows=C96)
            paced_product(plan["out2"][0], P, m_rounded, m_split, 0, m_parts)
            for i, c in enumerate(plan["out2"][1:]):
                product(c, P, x=m_parts)
                sum_pair(5, i)
            sum_pair(5, 3)
            keep_warm(NORM_WAIT)

            paced_product(plan["up"][0], P, h_rounded, h_split, 12)
            for c in plan["up"][1:BANKS]:
                product(c, P)
            with pe.Fori(1, KF // BANKS) as it:
                for c in plan["up"][:BANKS]:
                    product(c, P, it)
            for i, c in enumerate(plan["down"]):
                pr, g = divmod(i, 3)
                pe.wait_ge(ffn_split, KD * (g + 1) if pr == 0 else KF)
                for v in range(2):
                    for w, x, ready in ((w_hi, f_hi, hi_ready), (w_hi, f_lo, hi_ready), (w_lo, f_hi, lo_ready)):
                        pe.wait_ge(ready[v], c.split + 1)
                        for k in range(KD):
                            mm = pe.matmul(pair(aux[pr])[:, v, :], w[v][:, k * P:(k + 1) * P], x[:, g * KD + k, :],
                                           start=(g == v == k == 0 and w is w_hi and x is f_hi),
                                           stop=(g == 2 and w is w_lo and k == KD - 1), skip_group_check=True)
                        if x is f_lo:
                            mm.then_inc(hi_used[v], 1)
                    mm.then_inc(tile_done[v], 1)
                if pr == 1 and g == 1:
                    moved(pe, plan["up"])
                if pr and g == 1:
                    sum_pair(6, pr - 1, bank=gemm[0])
            sum_pair(6, 3, bank=gemm[0])

        @block.scalar
        def _(act):
            def squares(src, dst=sq, ready=None):
                act.activation(root[:, :], epsc[:, :], ACT.Sqrt)
                for n in range(4):
                    part = slice(2 * n, 2 * n + 2)
                    if ready:
                        ready(n)
                    act.activation(dst[:, part, :], src[:, part, :], ACT.Square).then_inc(squared, 1)

            def deviation(i, bank=aux[3]):
                act.wait_ge(sumsq, i + 1)
                if i:
                    act.wait_ge(rstd_done, i)
                act.activation(std[:, :], bank[:, 0:T], ACT.Sqrt, bias=epsc[:, :],
                               scale=1.0 / D).then_inc(stdev, 1)

            def round_h(j):
                for q in range(4):
                    part = slice(2 * q, 2 * q + 2)
                    act.wait_ge(h_ready, 4 * j + q + 1)
                    act.activation(h_hi[:, part, :], sq[:, part, :], ACT.Copy).then_inc(h_rounded, 1)

            def round_parts(dst, src, signal, parts=2):
                n = KD // parts
                for i in range(parts):
                    act.activation(dst[:, n * i:n * i + n, :], src[:, n * i:n * i + n, :], ACT.Copy).then_inc(signal, 1)

            def round_weights(c, it=0):
                for v in range(2):
                    round_tile(c, v, it)

            def round_tile(c, v, it=0):
                act.wait_ge(landed[c.raw][v], it * (16 * BANKS // RAW) + 16 * c.landing[v])
                if c.split:
                    act.wait_ge(hi_used[v], it * BANKS + c.split)
                    act.wait_ge(lo_ready[v], it * BANKS + c.split)
                n, rows = floats[c.index], tile_rows.get(c.index, P)
                act.activation(w_hi[v][0:rows, 0:n], raw[c.raw][v][0:rows, 0:n], ACT.Copy).then_inc(hi_ready[v], 1)

            ahead = [0]

            def look_ahead(upto, tiles=2):
                end = min(2 * upto + tiles, 2 * len(order))
                for n in range(ahead[0], end):
                    c, v = order[n // 2], n % 2
                    if c.split is not None:
                        round_tile(c, v)
                ahead[0] = max(ahead[0], end)

            def evacuate(c, out, src, func=ACT.Copy, **kw):
                look_ahead(c.index + 1)
                taken(act, c)
                act.activation(out, src, func, **kw).then_inc(evacuated[c.bank], 1)

            act.wait_ge(consts, 1)
            squares(xres, ready=lambda n: act.wait_ge(x_in[n], 16))
            deviation(0)
            look_ahead(0)
            round_h(0)
            for j in range(4):
                gc, vc = plan[f"conv_in{j}"]
                evacuate(gc, sig[:, 2 * j:2 * j + 2, :], pair(gemm[gc.bank]), ACT.Sigmoid)
                evacuate(vc, zc[:, 2 * j:2 * j + 2, PADC:], pair(gemm[vc.bank]))
            fchunk = plan["f"][0]
            act.wait_ge(params_in, 16)
            evacuate(fchunk, fy, gemm[fchunk.bank][0:HEADS, 0:T], ACT.Identity, bias=par("fox_bf", rows=HEADS))
            for i, c in enumerate(plan["q"]):
                evacuate(c, qT[:, 2 * i:2 * i + 2, :], pair(gemm[c.bank]))
                if i < CPARTS:
                    act.wait_ge(consts, N_CONSTS)
                    rows = slice(i * APART, i * APART + HEADS)
                    act.activation(sel[rows], ident[rows, rows].unsqueeze(2).to_broadcast([HEADS, HEADS, P]),
                                   ACT.Copy).then_inc(sel_ready, 1)
            for i, c in enumerate(plan["k"]):
                evacuate(c, kT[:, 2 * i:2 * i + 2, :], pair(gemm[c.bank]))
            for i, c in enumerate(plan["v"]):
                evacuate(c, vtok[:, :, i * CW:(i + 1) * CW], pair(gemm[c.bank]))
            look_ahead(plan["ga"][1].index)
            act.wait_ge(f_abs, 1)
            act.activation(fe, fa, ACT.Exp).then_inc(f_exp, 1)
            act.wait_ge(f_exp, 1)
            act.activation(fl, fe, ACT.Ln, bias=1.0).then_inc(f_soft, 1)
            def gate_raw(i, func=ACT.Copy):
                c = (plan["ga"] + plan["gb"])[i]
                dst = ga if i < 4 else gb
                evacuate(c, dst[:, 2 * (i % 4):2 * (i % 4) + 2, :], pair(gemm[c.bank]), func)

            gate_raw(0)
            act.wait_ge(centered, 1)
            for half in range(2):
                part = slice(4 * half, 4 * half + 4)
                act.activation(sq[:, part, :], zv[:, part, :], ACT.Square).then_inc(ln_squared, 1)
            gate_raw(1)
            act.wait_ge(ln_sumsq, 1)
            act.wait_ge(rstd_done, 1)
            act.activation(std[:, :], aux[3][:, 0:T], ACT.Sqrt, bias=epsc[:, :], scale=1.0 / D).then_inc(ln_std, 1)
            moved(act, plan["ga"][:2])
            act.activation(ga[:, 0:4, :], ga[:, 0:4, :], ACT.Sigmoid).then_inc(gates_on, 1)

            def norm_gate(first, last):
                for k in range(first, last):
                    act.wait_ge(ln_scaled, k + 1)
                    act.activation(sq[:, k, :], zv[:, k, :], ACT.Sigmoid,
                                   bias=par("conv_ln_b", k)).then_inc(ln_sig, 1)

            look_ahead(plan["ga"][2].index + 1)
            norm_gate(0, 3)
            gate_raw(2, ACT.Sigmoid)
            look_ahead(plan["ga"][3].index + 1, 1)
            norm_gate(3, 6)
            look_ahead(plan["ga"][3].index + 1)
            norm_gate(6, KD)
            gate_raw(3, ACT.Sigmoid)

            def exponent(u):
                nk = (u % QB + 1) * P
                act.wait_ge(negmax_ready, u + 1)
                if u >= PROBS:
                    act.wait_ge(pT_psum, u - PROBS + 1)
                act.activation(p_sb[:, u % PROBS, 0:nk], s_sb[:, u % 2, 0:nk], ACT.Exp, bias=nmax[:, u:u + 1],
                               accum_out=rsum[:, u:u + 1]).then_inc(exp_done, 1)

            def copy_turned(u):
                nk = (u % QB + 1) * P
                act.wait_ge(pT_psum, u + 1)
                if u >= 2:
                    act.wait_ge(pv_done, u - 1)
                act.activation(pT_sb[:, u % 2, 0:nk], aux[2][:, 0:nk], ACT.Copy).then_inc(pT_ready, 1)

            UNITS = HEADS * QB
            for u in range(UNITS + PROBS + 2):
                if PROBS <= u < UNITS + PROBS:
                    copy_turned(u - PROBS)
                if u < UNITS:
                    exponent(u)
                if u == CONV_STEPS[0] - 6:
                    act.wait_ge(conv_act, 1)
                    round_parts(y_hi, zv, y_rounded)
                if u >= 7 and u % 4 == 3:
                    i = (u - 7) // 4
                    act.wait_ge(pv_done, 4 * i + 4)
                    act.activation(ob[:, i, :], aux[3][:, 0:T], ACT.Copy).then_inc(ob_ready, 1)
                if u >= 8 and u % 4 == 0:
                    i = (u - 8) // 4
                    act.wait_ge(ob_ready, i + 1)
                    act.activation(x_hi[:, i, :], ob[:, i, :], ACT.Copy).then_inc(ob_rounded, 1)
                for steps, name in ((GATE_STEPS, "gb"), (CONV_STEPS, "conv_out")):
                    for tile, at in ((1, u + 1), (2, u - 1)):
                        if at in steps:
                            look_ahead(plan[name][steps.index(at)].index + 1, tile)
                if u - 1 in GATE_STEPS:
                    gate_raw(4 + GATE_STEPS.index(u - 1))
            act.activation(gb, gb, ACT.Sigmoid).then_inc(gates_on, 1)
            act.wait_ge(tile_done[1], plan["conv_out"][-1].index + 1)
            for i in range(4):
                part = slice(2 * i, 2 * i + 2)
                look_ahead(plan["fox_out"][i].index + 1)
                act.wait_ge(mix_ready, i + 1)
                act.activation(y_hi[:, part, :], ga[:, part, :], ACT.Copy).then_inc(y_rounded, 1)

            def added(name):
                def ready(n):
                    look_ahead(plan[name][n].index + 1)
                    moved(act, plan[name][n:n + 1])
                return ready

            squares(xres, x_sq, added("mix_out"))
            deviation(1)
            round_h(1)
            for i, c in enumerate(plan["peer_q"]):
                evacuate(c, qp[:, 2 * i:2 * i + 2, :], pair(gemm[c.bank]))
            look_ahead(plan["u"][0].index)
            for g in range(TT * 4):
                tt, h0 = divmod(4 * g, HALVES)
                act.wait_ge(keys_scored, g + 1)
                act.activation(ks[:, tt, h0:h0 + 4, :], aux[g % 4][:, :].rearrange("p (h n) -> p h n", h=4),
                               ACT.Copy).then_inc(keys_moved, 1)

            def gelu(c, plane, it):
                taken(act, c, it)
                act.activation(act_peer[:, plane, :], pair(gemm[c.bank]),
                               ACT.Gelu_apprx_tanh).then_inc(evacuated[c.bank], 1)

            def gelus(first, last):
                with act.Fori(first, last) as it:
                    for s, c in enumerate(plan["u"][:BANKS]):
                        round_weights(order[c.index + 1], it)
                        gelu(c, bass.ds(it * 2 * BANKS + 2 * s, 2), it)

            def round_acts(c, plane, it=0):
                act.wait_ge(tile_done[1], it * BANKS + (c.index - 1))
                act.activation(a_hi[:, c.raw, :, :], act_peer[:, plane, :], ACT.Copy).then_inc(a_rounded, 1)

            def value_steps(first, its):
                with act.Fori(0, its) as it:
                    for s in range(first, first + BANKS):
                        c = plan["ev"][s + 1]
                        round_acts(c, bass.ds(it * 2 * BANKS + 2 * (s + 1), 2), it)
                        round_weights(c, it)

            def value_ahead(s):
                c = plan["ev"][s + 1]
                round_acts(c, slice(2 * (s + 1), 2 * (s + 1) + 2))
                round_weights(c)

            def last_value_steps(first):
                for s in range(first, min(first + BANKS, P // 2 - 1)):
                    if s + 1 == HALF:
                        for b in range(2):
                            act.wait_ge(planes_used[b], HALF + 1)
                    value_ahead(s)

            gelus(0, ROUTED)
            act.wait_ge(topk_done, 1)
            act.activation(sc, sc, ACT.Exp).then_inc(gate_exp, 1)
            gelus(ROUTED, ITS // 2)
            act.wait_ge(routed, 1)
            gelus(ITS // 2, ITS)
            for b in range(2):
                act.wait_ge(planes_used[b], HALF // 2 + 1)
            act.wait_ge(tile_done[1], plan["u"][-1].index + 1)
            round_acts(plan["ev"][0], slice(0, 2))
            value_steps(0, ITS // 2 - 1)
            last_value_steps(HALF - BANKS)
            value_steps(HALF, (MEM_NORM - HALF) // BANKS - 1)
            act.wait_ge(mem_in, 16)
            squares(memT, mem_sq, ready=lambda n: value_ahead(MEM_NORM - BANKS + n - 1) if n else None)
            value_ahead(MEM_NORM - 1)
            value_steps(MEM_NORM, (2 * HALF - MEM_NORM) // BANKS - 1)
            deviation(2)
            last_value_steps(2 * HALF - BANKS)
            ahead[0] = 2 * (plan["ev"][-1].index + 1)

            act.wait_ge(normed, 1)
            round_parts(h_lo, memT, mem_rounded)
            look_ahead(plan["mem_k"][0].index)
            squares(xres, ready=lambda n: act.wait_ge(x2_done, n + 1))
            mem_k = plan["mem_k"]
            for i, c in enumerate(mem_k):
                evacuate(c, mk[:, 2 * i:2 * i + 2, :], pair(gemm[c.bank], C96))
                if i == 0:
                    deviation(3)
                    look_ahead(mem_k[2].index)
                    act.wait_ge(normed, 2)
                    squares(xres)
                if i == 2:
                    deviation(4)
                    look_ahead(plan["mem_v"][0].index, 1)
                    round_h(2)
            for i, c in enumerate(plan["mem_v"]):
                evacuate(c, mv[:, :, i * CW:(i + 1) * CW], pair(gemm[c.bank]))
            act.wait_ge(lam_abs, 1)
            act.activation(lam[1], lam[0], ACT.Exp).then_inc(lam_exp, 1)
            act.wait_ge(lam_exp, 1)
            act.activation(lam[2], lam[1], ACT.Ln, bias=1.0).then_inc(lam_ln, 1)
            act.wait_ge(pads2, 1)
            for i, c in enumerate(plan["z_rnn"]):
                evacuate(c, zr[:, 2 * i:2 * i + 2, RNN_CONV - 1:], pair(gemm[c.bank], C96))
            c = plan["dec"][0]
            evacuate(c, dec, gemm[c.bank][0:LOW, 0:T])
            for name, dst in (("zq", zq), ("zk", zk)):
                for i, c in enumerate(plan[name]):
                    evacuate(c, dst[:, 2 * i:2 * i + 2, :], pair(gemm[c.bank], GDK))
            act.wait_ge(dec_psum, 1)
            for h in range(GH):
                act.activation(gy[:, h, :], pair(aux[h // 2], GDK)[:, h % 2, :], ACT.Identity,
                               bias=par("gla_b_decay_2", h, GDK)).then_inc(gla_y, 1)
            look_ahead(plan["zv"][1].index, 1)
            act.wait_ge(gla_abs, 1)
            act.activation(eg, eg, ACT.Exp).then_inc(gla_soft, 1)
            look_ahead(plan["zv"][1].index)
            act.wait_ge(gla_soft, 1)
            act.activation(emg, eg, ACT.Ln, bias=1.0).then_inc(gla_soft, 1)
            for i, c in enumerate(plan["zv"]):
                evacuate(c, vg[:, :, i * CW:(i + 1) * CW], pair(gemm[c.bank]))
            for h in range(K96):
                if h % 2 == 0:
                    c = plan["zmq"][h // 2]
                    evacuate(c, mq[:, h:h + 2, :], pair(gemm[c.bank], C96))
                act.wait_ge(rg_psum, h + 1)
                bank = pair(aux[2 + h % 2], C96)
                act.activation(rg[:, h, :], bank[:, 0, :], ACT.Sigmoid, bias=par("rg_b_a_2", h, C96)).then_inc(rg_moved, 1)
                act.activation(ig[:, h, :], bank[:, 1, :], ACT.Sigmoid, bias=par("rg_b_x_2", h, C96)).then_inc(rg_moved, 1)

            def mem_exp(u):
                act.wait_ge(ms_max, u + 1)
                if u >= 2:
                    act.wait_ge(mpT_psum, u - 1)
                act.activation(mp[:, u % 2, :], aux[u % 2][:, 0:MEM], ACT.Exp, bias=mnm[:, u:u + 1],
                               scale=MHD ** -0.5, accum_out=msum[:, u:u + 1]).then_inc(ms_exp, 1)

            def mem_copy(u):
                h, qb = divmod(u, QB)
                act.wait_ge(mpT_psum, u + 1)
                if qb == 0 and h:
                    act.wait_ge(mo_psum, h)
                act.activation(mpT[:, :, qb * P:(qb + 1) * P],
                               aux[2][:, 0:MEM].rearrange("p (m q) -> p m q", m=TT), ACT.Copy).then_inc(mpT_moved, 1)

            def gla_decays():
                act.wait_ge(gla_sum, 2)
                last = gl.rearrange("p h (n i) -> p (h n) i", i=GCHUNK)[:, :, GCHUNK - 1]
                act.activation(eg, gl, ACT.Exp, scale=1.0 / 16).then_inc(gla_exp, 1)
                act.activation(emg, gl, ACT.Exp, scale=-1.0 / 16).then_inc(gla_exp, 1)
                act.activation(ekd, gy, ACT.Exp, scale=1.0 / 16).then_inc(gla_exp, 1)
                act.activation(decay.rearrange("p h n -> p (h n)"), last, ACT.Exp, scale=1.0 / 16).then_inc(gla_exp, 1)

            def rnn_decay():
                act.wait_ge(la_ready, 1)
                act.activation(ra, rg, ACT.Exp).then_inc(a_ready, 1)

            def rnn_tanh():
                act.wait_ge(a_ready, 1)
                act.activation(rg, rg, ACT.Tanh, scale=-1.0).then_inc(tanh_ready, 1)

            def rnn_root():
                act.wait_ge(w_ready, 1)
                act.activation(rg, rg, ACT.Sqrt).then_inc(root_ready, 1)

            beside = {0: gla_decays, 1: rnn_decay, 2: rnn_tanh}
            for u in range(MH * QB + 2):
                if u < MH * QB:
                    mem_exp(u)
                if u >= 3 and u % 2:
                    h = (u - 3) // 2
                    act.wait_ge(mo_psum, h + 1)
                    act.wait_ge(gla_qk, 3)
                    act.activation(out_c[:, 2 * h:2 * h + 2, :], pair(aux[3], C96), ACT.Copy).then_inc(mo_moved, 1)
                if u and u % 2 == 0:
                    c = plan["gate0"][u // 2 - 1]
                    evacuate(c, gate[:, u - 2:u, :], pair(gemm[c.bank]))
                elif 0 < u < MH * QB:
                    look_ahead(plan["gate0"][u // 2].index + 1, 1)
                if 1 <= u <= MH * QB:
                    mem_copy(u - 1)
                if u in beside:
                    beside[u]()
                if u == MH * QB:
                    look_ahead(plan["zg"][1].index)
                    rnn_root()
            for tt in range(TT):
                act.wait_ge(kend_psum, tt + 1)
                act.activation(kendT[:, tt].rearrange("p h d -> p (h d)"), aux[tt][:, 0:GH * GDK],
                               ACT.Copy).then_inc(kend_moved, 1)
            act.wait_ge(gla_scored, 1)
            act.activation(sT, aux[2][:, :].rearrange("p (h n i) -> p h n i", h=GH, n=TT),
                           ACT.Copy).then_inc(gla_scores_moved, 1)
            act.wait_ge(ig_used, 1)
            for i, c in enumerate(plan["zg"]):
                look_ahead(c.index + 1)
                taken(act, c)
                act.activation(sg[:, 2 * i:2 * i + 2, :], pair(gemm[c.bank], C96), ACT.Sigmoid).then_inc(sg_sig, 1)
                if i == 1:
                    act.wait_ge(rnn_done, 1)
                    round_parts(a_parts[0], out_a, outa_rounded)
                if i == 2:
                    moved(act, plan["gate0"])
                    act.activation(gate, gate, ACT.Sigmoid).then_inc(gate0_on, 1)
            look_ahead(plan["branch0"][0].index)

            def by_parity(tile, h, parity):
                return tile[0:C96, 2 * h:2 * h + 2, :].rearrange(
                    "p v (n q i) -> p v n q i", q=2, i=GCHUNK)[:, :, :, parity, :]

            def gate_evac(b, i):
                c = plan[f"gate{b}"][i]
                look_ahead(c.index + 1)
                if b == 1:
                    moved(act, plan["branch0"][i:i + 1])
                else:
                    act.wait_ge(merge_done, i + 1)
                evacuate(c, gate[:, 2 * i:2 * i + 2, :], pair(gemm[c.bank]), ACT.Sigmoid)

            for h0 in range(0, GH, 2):
                for h in (h0, h0 + 1):
                    for parity in range(2):
                        bank = aux[2 * (h % 2) + parity][0:C96, 0:T].rearrange("p (v n i) -> p v n i", v=2, n=TT)
                        act.wait_ge(o_psum, 2 * h + parity + 1)
                        act.activation(by_parity(out_b, h, parity), bank, ACT.Copy)
                        act.activation(by_parity(sq, h, parity), bank, ACT.Square).then_inc(o_squared, 1)
                look_ahead(plan["branch0"][h0].index + 1)
                for h in (h0, h0 + 1):
                    act.wait_ge(o_sumsq, h + 1)
                    act.activation(eg[:, h, :], aux[2 * (h % 2)][0:C96, 0:T], ACT.Sqrt, bias=epsc[0:C96, :],
                                   scale=1.0 / GDV).then_inc(o_std, 1)
                look_ahead(plan["branch0"][h0 + 1].index + 1)
            for i in range(4):
                if i == 3:
                    act.wait_ge(out_b_done, 1)
                    round_parts(b_parts[0], out_b, outb_rounded)
                gate_evac(1, i)
            act.wait_ge(mo_moved, MH)
            round_parts(c_parts[0], out_c, outc_rounded)
            look_ahead(plan["gate2"][0].index)
            for i in range(4):
                gate_evac(2, i)
            for i in range(4):
                look_ahead(plan["branch2"][i].index + 1)
                act.wait_ge(merge_done, 4 + i + 1)
                part = slice(2 * i, 2 * i + 2)
                act.activation(x_hi[:, part, :], merged[:, part, :], ACT.Copy).then_inc(m_rounded, 1)
            squares(xres, ready=added("out2"))
            deviation(5)
            round_h(3)
            act.wait_ge(ffn_pads, 1)

            def up_to_sbuf(c, b, n, it=0):
                taken(act, c, it)
                if not isinstance(n, int) or n >= 2:
                    act.wait_ge(ffn_conv, n - 1)
                act.activation(ub[:, b, :, 2:], pair(gemm[c.bank]), ACT.Copy).then_inc(evacuated[c.bank], 1)

            def ffn_gelus(b, n):
                act.wait_ge(ffn_conv, n + 1)
                act.activation(uc[:, b, 0, :], uc[:, b, 0, :], ACT.Gelu_apprx_tanh).then_inc(ffn_gelu, 1)

            def ffn_round(b, n):
                act.wait_ge(ffn_act, n + 1)
                plane = slice(n, n + 1) if isinstance(n, int) else bass.ds(n, 1)
                act.activation(f_hi[:, plane, :].rearrange("p a t -> p (a t)"), ffp[:, b, :],
                               ACT.Copy).then_inc(ffn_rounded, 1)

            def up_step(s, n, it=0, first=False):
                c = plan["up"][s]
                round_tile(order[c.index + 1], 0, it)
                if not first:
                    ffn_gelus((s + 1) % 2, n - 1)
                round_tile(order[c.index + 1], 1, it)
                if not first:
                    ffn_round((s + 1) % 2, n - 1)
                up_to_sbuf(c, s % 2, n, it)

            for s in range(BANKS):
                up_step(s, s, first=(s == 0))
            with act.Fori(1, KF // BANKS) as it:
                for s in range(BANKS):
                    up_step(s, it * BANKS + s, it)
            ahead[0] = 2 * (plan["down"][0].index + 1)
            look_ahead(plan["down"][1].index, 1)
            ffn_gelus((KF - 1) % 2, KF - 1)
            ffn_round((KF - 1) % 2, KF - 1)
            look_ahead(plan["down"][1].index)

            def down_added(n):
                look_ahead(plan["down"][3 * n + 2].index + 1)
                act.wait_ge(x4_done, n + 1)

            squares(xres, ready=down_added)
            deviation(6, gemm[0])

        @block.vector
        def _(dve):
            count = [0]

            def step(ins):
                count[0] += 1
                ins.then_inc(dve_step, 1)

            def settle(behind=0):
                if count[0] > behind:
                    dve.wait_ge(dve_step, count[0] - behind)

            def pair_squares(i, n, src=sq):
                dve.wait_ge(squared, 4 * i + n + 1)
                dve.tensor_tensor(src[:, 2 * n, :], src[:, 2 * n, :], src[:, 2 * n + 1, :], ALU.add).then_inc(paired, 1)

            def normalise(i, src, dst, gain, step_tiles=KD, beside=None):
                if beside:
                    beside(0)
                dve.wait_ge(stdev, i + 1)
                dve.reciprocal(rstd[:, :], std[:, :]).then_inc(rstd_done, 1)
                dve.wait_ge(rstd_done, i + 1)
                for k in range(KD):
                    ins = dve.scalar_tensor_tensor(dst[:, k, :], src[:, k, :], par(gain, k), rstd[:, :],
                                                   ALU.mult, ALU.mult)
                    if k % step_tiles == step_tiles - 1:
                        ins.then_inc(normed, 1)
                    if beside and k in (1, 3, 5):
                        beside(k // 2 + 1)

            def normalise_split(i, j, gain):
                dve.wait_ge(stdev, i + 1)
                dve.reciprocal(rstd[:, :], std[:, :]).then_inc(rstd_done, 1)
                dve.wait_ge(rstd_done, i + 1)

                def rest(q):
                    part = slice(2 * q, 2 * q + 2)
                    if i == 4 and q == 0:
                        taken(dve, plan["mem_v"][-1])
                    dve.wait_ge(h_rounded, 4 * j + q + 1)
                    dve.tensor_tensor(h_lo[:, part, :], sq[:, part, :], h_hi[:, part, :],
                                      ALU.subtract).then_inc(h_split, 1)

                for k in range(KD):
                    ins = dve.scalar_tensor_tensor(sq[:, k, :], xres[:, k, :], par(gain, k), rstd[:, :],
                                                   ALU.mult, ALU.mult)
                    if k % 2:
                        ins.then_inc(h_ready, 1)
                    if k == KD - 1:
                        rest(0)
                for q in range(1, 4):
                    rest(q)

            def rest_parts(dst, src, part_hi, rounded, split, parts=2):
                n = KD // parts
                for i in range(parts):
                    part = slice(n * i, n * i + n)
                    dve.wait_ge(rounded, i + 1)
                    dve.tensor_tensor(dst[:, part, :], src[:, part, :], part_hi[:, part, :],
                                      ALU.subtract).then_inc(split, 1)

            def add_to_residual(name, norm, src=sq):
                for i, c in enumerate(plan[name]):
                    taken(dve, c)
                    part = xres[:, 2 * i:2 * i + 2, :]
                    dve.tensor_tensor(part, part, pair(gemm[c.bank]), ALU.add).then_inc(evacuated[c.bank], 1)
                    pair_squares(norm, i, src)

            for n in range(4):
                pair_squares(0, n)
            dve.wait_ge(params_in, 16)
            normalise_split(0, 0, "norm1_g")
            dve.wait_ge(consts, N_CONSTS)
            for j in range(4):
                moved(dve, plan[f"conv_in{j}"])
                gated = zc[:, 2 * j:2 * j + 2, PADC:]
                step(dve.tensor_tensor(gated, gated, sig[:, 2 * j:2 * j + 2, :], ALU.mult))
                settle()
                for w in range(CONV_W):
                    for k in (2 * j, 2 * j + 1):
                        tap = par("conv_w", k * CONV_W + w)
                        if w == 0:
                            step(dve.tensor_scalar(zv[:, k, :], zc[:, k, 0:T], tap, par("conv_b", k),
                                                   ALU.mult, ALU.add))
                        else:
                            settle(1)
                            step(dve.scalar_tensor_tensor(zv[:, k, :], zc[:, k, w:w + T], tap, zv[:, k, :],
                                                          ALU.mult, ALU.add))
            settle()
            moved(dve, plan["f"])
            dve.tensor_tensor(sq[:, 0:4, :], zv[:, 0:4, :], zv[:, 4:8, :], ALU.add).then_inc(conv_done, 1)
            dve.scalar_tensor_tensor(fa, fy, -1.0, fy, ALU.mult, ALU.min).then_inc(f_abs, 1)
            dve.wait_ge(mean_ready, 1)
            for k in range(KD):
                ins = dve.scalar_tensor_tensor(zv[:, k, :], aux[2][:, 0:T], -1.0 / D, zv[:, k, :], ALU.mult, ALU.add)
            ins.then_inc(centered, 1)
            dve.wait_ge(f_soft, 1)
            step(dve.scalar_tensor_tensor(fa, fy, 0.0, fl, ALU.min, ALU.subtract))
            settle()
            step(dve.tensor_tensor_scan(fc, keep[0:HEADS, 1:2].to_broadcast([HEADS, T]), fa, 0.0, ALU.mult, ALU.add))
            settle()
            dve.wait_ge(ln_squared, 2)
            dve.tensor_tensor(sq[:, 0:4, :], sq[:, 0:4, :], sq[:, 4:8, :], ALU.add).then_inc(ln_paired, 1)
            step(dve.tensor_scalar(fc8, fc, -math.sqrt(HD), None, ALU.mult))
            settle()
            for n in range(CPARTS):
                step(dve.tensor_copy(fc_parts[0:HEADS] if n == 0 else fc_part, fc8))
                settle()
                if n:
                    ins = dve.tensor_copy(fc_parts[n * APART:n * APART + HEADS], fc_part)
                if n < CPARTS - 1:
                    step(dve.tensor_tensor(fc8, fc8, fc_parts[0:HEADS] if n == 0 else fc_part, ALU.subtract))
                    settle()
            ins.then_inc(c_ready, 1)
            dve.wait_ge(ln_std, 1)
            step(dve.reciprocal(rstd[:, :], std[:, :]))
            settle()
            for k in range(KD):
                dve.scalar_tensor_tensor(zv[:, k, :], zv[:, k, :], par("conv_ln_g", k), rstd[:, :],
                                         ALU.mult, ALU.mult).then_inc(ln_scaled, 1)
            def move_scores(u):
                qb = u % QB
                nk = (qb + 1) * P
                dve.wait_ge(scores_ready, u + 1)
                if u >= 2:
                    dve.wait_ge(exp_done, u - 1)
                dve.scalar_tensor_tensor(s_sb[:, u % 2, 0:nk], aux[u % 2][:, 0:nk], HD ** -0.5,
                                         mask[:, T - nk:T], ALU.mult, ALU.add).then_inc(scores_moved, 1)
                dve.wait_ge(scores_moved, u + 1)
                dve.tensor_reduce(nmax[:, u:u + 1], s_sb[:, u % 2, 0:nk], AX.X, ALU.max,
                                  negate=True).then_inc(negmax_ready, 1)

            def divide(u):
                nk = (u % QB + 1) * P
                dve.wait_ge(exp_done, u + 1)
                step(dve.reciprocal(rrec[:, u:u + 1], rsum[:, u:u + 1]))
                settle()
                dve.tensor_scalar(p_sb[:, u % PROBS, 0:nk], p_sb[:, u % PROBS, 0:nk], rrec[:, u:u + 1], None,
                                  ALU.mult).then_inc(probs_ready, 1)

            UNITS = HEADS * QB
            for u in range(CONV_STEPS[-1] + 2):
                if u < UNITS:
                    move_scores(u)
                if u == 1:
                    for k in range(KD):
                        dve.wait_ge(ln_sig, k + 1)
                        ins = dve.scalar_tensor_tensor(zv[:, k, :], zv[:, k, :], par("conv_ln_b", k), sq[:, k, :],
                                                       ALU.add, ALU.mult)
                    ins.then_inc(conv_act, 1)
                if 1 <= u <= UNITS:
                    divide(u - 1)
                if u == CONV_STEPS[0] - 4:
                    rest_parts(y_lo, zv, y_hi, y_rounded, y_split)
                if u >= 10 and u % 4 == 2:
                    i = (u - 10) // 4
                    dve.wait_ge(ob_rounded, i + 1)
                    dve.tensor_tensor(x_lo[:, i, :], ob[:, i, :], x_hi[:, i, :], ALU.subtract).then_inc(ob_split, 1)
                if u - 1 in CONV_STEPS:
                    i = CONV_STEPS.index(u - 1)
                    c = plan["conv_out"][i]
                    taken(dve, c)
                    dve.wait_ge(gates_on, 1)
                    moved(dve, plan["ga"][2:])
                    part = ga[:, 2 * i:2 * i + 2, :]
                    dve.tensor_tensor(part, part, pair(gemm[c.bank]), ALU.mult).then_inc(evacuated[c.bank], 1)
            for i in range((UNITS - 10) // 4 + 1, KD):
                dve.wait_ge(ob_rounded, i + 1)
                dve.tensor_tensor(x_lo[:, i, :], ob[:, i, :], x_hi[:, i, :], ALU.subtract).then_inc(ob_split, 1)
            dve.wait_ge(gates_on, 2)

            def mix_rest(i):
                part = slice(2 * i, 2 * i + 2)
                dve.wait_ge(y_rounded, 2 + i + 1)
                dve.tensor_tensor(y_lo[:, part, :], ga[:, part, :], y_hi[:, part, :], ALU.subtract).then_inc(y_split, 1)

            for i, c in enumerate(plan["fox_out"]):
                taken(dve, c)
                a, b = ga[:, 2 * i:2 * i + 2, :], gb[:, 2 * i:2 * i + 2, :]
                dve.tensor_tensor(b, b, pair(gemm[c.bank]), ALU.mult).then_inc(evacuated[c.bank], 1)
                moved(dve, [c, plan["conv_out"][i]])
                dve.tensor_tensor(a, a, b, ALU.add).then_inc(mix_ready, 1)
                if i:
                    mix_rest(i - 1)
            mix_rest(3)
            add_to_residual("mix_out", 1, x_sq)

            moved(dve, plan["mix_out"])
            normalise_split(1, 1, "norm2_g")

            def best(outs, src):
                for v, i, s in outs:
                    step(dve.max(v[:, 0:8], s))
                for n, (v, i, s) in enumerate(outs):
                    settle(len(outs) - 1)
                    step(dve.max_index(i[:, 0:8], v[:, 0:8], s))
                for v, i, s in outs:
                    settle(len(outs) - 1)
                    step(dve.match_replace(s, v[:, 0:8], s, LOWEST))
                for v, i, s in outs:
                    settle(len(outs) - 1)
                    step(dve.max(v[:, 8:16], s))
                for v, i, s in outs:
                    settle(len(outs) - 1)
                    step(dve.max_index(i[:, 8:16], v[:, 8:16], s))

            for tt in range(TT):
                dve.wait_ge(keys_moved, 4 * tt + 4)
                if tt == 0:
                    dve.wait_ge(keys_moved, 8)
                for h in range(PH):
                    best([(topv[:, h, f], topi[:, h, f], ks[:, tt, 2 * h + f, :]) for f in range(2)], None)
                settle()
                step(dve.tensor_copy(topif, topi))
                step(dve.tensor_tensor(cand.rearrange("p h (a b) -> p h a b", a=TOPK),
                                       topv[:, :, 0].unsqueeze(3).to_broadcast([P, PH, TOPK, TOPK]),
                                       topv[:, :, 1].unsqueeze(2).to_broadcast([P, PH, TOPK, TOPK]), ALU.add))
                settle()
                for h in range(0, PH, 2):
                    best([(sc[:, tt, g], pos[:, g], cand[:, g]) for g in (h, h + 1)], None)
                settle()
                step(dve.tensor_scalar(posp[:, 0], pos, 4, None, ALU.logical_shift_right))
                step(dve.tensor_scalar(posp[:, 1], pos, TOPK - 1, None, ALU.bitwise_and))
                settle()
                step(dve.tensor_copy(posf, posp))
                settle()
                for f, e in ((0, e1), (1, e2)):
                    step(dve.tensor_tensor(eq, posf[:, f].unsqueeze(3).to_broadcast([P, PH, TOPK, TOPK]),
                                           iota[:, 0:TOPK].unsqueeze(1).unsqueeze(1).to_broadcast([P, PH, TOPK, TOPK]),
                                           ALU.is_equal))
                    settle()
                    step(dve.tensor_tensor(eq, eq, topif[:, :, f].unsqueeze(2).to_broadcast([P, PH, TOPK, TOPK]),
                                           ALU.mult))
                    settle()
                    step(dve.tensor_reduce(e[:, tt], eq, AX.X, ALU.add))
                    settle()
            for tt in range(TT):
                step(dve.tensor_copy(grec[:, tt], sc[:, tt, :, 0]))
            settle()
            for tt in range(TT):
                ins = dve.tensor_tensor(sc[:, tt], sc[:, tt], grec[:, tt].unsqueeze(2).to_broadcast([P, PH, TOPK]),
                                        ALU.subtract)
            ins.then_inc(topk_done, 1)
            dve.wait_ge(gate_exp, 1)
            step(dve.tensor_reduce(gsum.rearrange("p t h -> p (t h)"), sc.rearrange("p t h k -> p (t h) k"),
                                   AX.X, ALU.add))
            settle()
            step(dve.reciprocal(grec, gsum))
            settle()
            dve.tensor_tensor(sc.rearrange("p t h k -> p (t h) k"), sc.rearrange("p t h k -> p (t h) k"),
                              grec.rearrange("p t h -> p (t h)").unsqueeze(2).to_broadcast([P, TT * PH, TOPK]),
                              ALU.mult).then_inc(gates_ready, 1)
            for n, (dst, done) in enumerate(((e1T, planes_used[0]), (e2T, planes_used[1]), (gT, routed))):
                dve.wait_ge(routed_psum, n + 1)
                dve.tensor_copy(dst, aux[n][:, 0:T]).then_inc(done, 1)
            for done in (planes_used[0], planes_used[1], routed):
                dve.wait_ge(done, 1)
            for part in range(3):
                step(dve.tensor_copy(gate_parts[:, part, :], gT))
                settle()
                if part < 2:
                    step(dve.tensor_tensor(gT, gT, gate_parts[:, part, :], ALU.subtract))
                    settle()

            def hots(half, s, it):
                b = s % 2
                tokens = bass.ds(it * (BANKS * GROUP) + GROUP * s, GROUP)

                def along(tile, n):
                    return tile.unsqueeze(2).to_broadcast([P, GROUP, n])

                keys1 = iota[:, half * P // 2:(half + 1) * P // 2].unsqueeze(1).to_broadcast([P, GROUP, P // 2])
                dve.tensor_tensor(hot, keys1, along(e1T[:, tokens], P // 2), ALU.is_equal).then_inc(hot_ready, 1)
                dve.tensor_tensor(hot2[:, b], iota[:, :].unsqueeze(1).to_broadcast([P, GROUP, P]),
                                  along(e2T[:, tokens], P), ALU.is_equal)
                dve.wait_ge(hot_ready, it * BANKS + (half * HALF + s + 1))
                for part in range(3):
                    ins = dve.tensor_tensor(hot1[:, b, part], hot, along(gate_parts[:, part, tokens], P // 2), ALU.mult)
                ins.then_inc(hots_ready[b], 1)

            def apply_gates(half, s, it):
                b = s % 2
                dve.wait_ge(planes_ready[b], it * 2 + (half * HALF // 2 + s // 2 + 1))
                part = act_peer[:, half * P // 2:(half + 1) * P // 2,
                                bass.ds(it * (BANKS * GROUP) + GROUP * s, GROUP)]
                dve.tensor_tensor(part, part, aux[b][:, :].rearrange("p (t i) -> p i t", t=GROUP),
                                  ALU.mult).then_inc(planes_used[b], 1)

            def subtract_acts(c, plane, it):
                dve.wait_ge(a_rounded, it * BANKS + (c.index - plan["ev"][0].index + 1))
                dve.tensor_tensor(a_lo[:, c.raw, :, :], act_peer[:, plane, :], a_hi[:, c.raw, :, :],
                                  ALU.subtract).then_inc(a_split, 1)

            def value_step(s, it, gates):
                c = plan["ev"][s]
                if gates:
                    hots(1, s, it)
                subtract_acts(c, bass.ds(it * 2 * BANKS + 2 * s, 2) if gates is not None
                              else slice(2 * s, 2 * s + 2), it)
                subtract(dve, c, it, (0,))
                if gates:
                    moved(dve, plan["u"][-1:])
                    apply_gates(1, s, it)

            def value_steps(first, its, gates):
                with dve.Fori(0, its) as it:
                    for s in range(first, first + BANKS):
                        value_step(s, it, gates)

            with dve.Fori(0, ITS // 2) as it:
                for s in range(BANKS):
                    hots(0, s, it)
                    subtract(dve, plan["u"][HALF + s], it, (0,))
                    moved(dve, plan["u"][HALF - 1:HALF])
                    apply_gates(0, s, it)
            value_steps(0, ITS // 2, True)
            value_steps(HALF, (MEM_NORM - HALF) // BANKS - 1, False)
            for n in range(4):
                value_step(MEM_NORM - BANKS + n, 0, None)
                pair_squares(2, n, mem_sq)
            value_steps(MEM_NORM, (2 * HALF - MEM_NORM) // BANKS - 1, False)
            normalise(2, memT, memT, "mem_norm_2",
                      beside=lambda n: value_step(2 * HALF - BANKS + n, 0, None))
            rest_parts(mem_lo, memT, h_lo, mem_rounded, mem_split)
            for b in range(BANKS):
                dve.wait_ge(experts_done, b + 1)
                part = xres[:, 2 * b:2 * b + 2, :]
                dve.tensor_tensor(part, part, pair(gemm[b]), ALU.add).then_inc(x2_done, 1)

            dve.wait_ge(x2_done, BANKS)
            for n in range(4):
                pair_squares(3, n)
            normalise(3, xres, xres, "normf_g")
            dve.wait_ge(normed, 2)
            for n in range(4):
                pair_squares(4, n)
            normalise_split(4, 2, "norm_mix_2")
            lamv = par("rg_lambda_2", 0, C96, K96)
            dve.scalar_tensor_tensor(lam[0], lamv, -1.0, lamv, ALU.mult, ALU.min).then_inc(lam_abs, 1)
            dve.wait_ge(lam_ln, 1)
            step(dve.tensor_scalar(lam[3], lam[1], 1.0, 1.0, ALU.add, ALU.subtract))
            settle()
            step(dve.tensor_scalar(lam[4], lam[3], 0.0, None, ALU.is_equal))
            settle()
            step(dve.tensor_tensor(lam[3], lam[3], lam[4], ALU.add))
            step(dve.tensor_tensor(lam[2], lam[2], lam[4], ALU.add))
            settle()
            step(dve.reciprocal(lam[5], lam[3]))
            step(dve.tensor_tensor(lam[2], lam[2], lam[1], ALU.mult))
            settle()
            step(dve.tensor_tensor(lam[2], lam[2], lam[5], ALU.mult))
            settle()
            step(dve.scalar_tensor_tensor(lam[6], lamv, 0.0, lam[2], ALU.min, ALU.subtract))
            settle()
            dve.tensor_scalar(lam[6], lam[6], 8.0, None, ALU.mult).then_inc(lam_ready, 1)
            for h0 in range(0, K96, 2):
                moved(dve, [plan["z_rnn"][h0 // 2]])
                for w in range(RNN_CONV):
                    for h in (h0, h0 + 1):
                        tap = par("rnn_conv_w_2", h * RNN_CONV + w, C96)
                        if w == 0:
                            step(dve.tensor_scalar(xr[:, h, :], zr[:, h, 0:T], tap, par("rnn_conv_b_2", h, C96),
                                                   ALU.mult, ALU.add))
                            continue
                        settle(0 if w == RNN_CONV - 1 and h > h0 else 1)
                        ins = dve.scalar_tensor_tensor(xr[:, h, :], zr[:, h, w:w + T], tap, xr[:, h, :],
                                                       ALU.mult, ALU.add)
                        if w < RNN_CONV - 1:
                            step(ins)
                        else:
                            ins.then_inc(rnn_conv, 1)
            dve.wait_ge(gla_y, GH)
            dve.scalar_tensor_tensor(eg, gy, -1.0, gy, ALU.mult, ALU.min).then_inc(gla_abs, 1)
            dve.wait_ge(gla_soft, 2)
            step(dve.scalar_tensor_tensor(gy, gy, 0.0, emg, ALU.min, ALU.subtract))
            settle()
            for h in range(GH):
                ins = dve.tensor_tensor_scan(gl[:, h, :], keep[0:GDK, :], gy[:, h, :], 0.0, ALU.mult, ALU.add)
            ins.then_inc(gla_sum, 1)
            dve.wait_ge(gla_sum, 1)
            glc = gl.rearrange("p h (n i) -> p (h n) i", i=GCHUNK)
            dve.tensor_tensor(gy.rearrange("p h (n i) -> p (h n) i", i=GCHUNK),
                              glc[:, :, GCHUNK - 1:GCHUNK].to_broadcast([GDK, GH * NCH, GCHUNK]), glc,
                              ALU.subtract).then_inc(gla_sum, 1)

            def mem_max(u):
                dve.wait_ge(ms_psum, u + 1)
                step(dve.tensor_reduce(mnm[:, u:u + 1], aux[u % 2][:, 0:MEM], AX.X, ALU.max, negate=True))
                settle()
                dve.tensor_scalar(mnm[:, u:u + 1], mnm[:, u:u + 1], MHD ** -0.5, None, ALU.mult).then_inc(ms_max, 1)

            def mem_divide(u):
                dve.wait_ge(ms_exp, u + 1)
                step(dve.reciprocal(mrec[:, u:u + 1], msum[:, u:u + 1]))
                settle()
                dve.tensor_scalar(mp[:, u % 2, :], mp[:, u % 2, :], mrec[:, u:u + 1], None, ALU.mult).then_inc(ms_probs, 1)

            def log_decay():
                dve.wait_ge(lam_ready, 1)
                dve.wait_ge(rg_moved, 2 * K96)
                dve.tensor_tensor(rg, rg, lam[6].unsqueeze(2).to_broadcast([C96, K96, T]), ALU.mult).then_inc(la_ready, 1)

            def gla_decayed():
                moved(dve, plan["zq"] + plan["zk"])
                dve.wait_ge(gla_exp, 3)
                dve.scalar_tensor_tensor(eg, zq, GDK ** -0.5, eg, ALU.mult, ALU.mult).then_inc(gla_qk, 1)
                dve.tensor_tensor(emg, zk, emg, ALU.mult).then_inc(gla_qk, 1)
                dve.tensor_tensor(ekd, zk, ekd, ALU.mult).then_inc(gla_qk, 1)

            def gated_input():
                step(dve.tensor_tensor(ig, ig, xr, ALU.mult))

            def squared_decay():
                dve.wait_ge(a_ready, 1)
                step(dve.tensor_tensor(rt, ra, ra, ALU.mult))
                settle()

            def one_minus():
                dve.wait_ge(tanh_ready, 1)
                dve.scalar_tensor_tensor(rg, rt, 1.0, rg, ALU.add, ALU.mult).then_inc(w_ready, 1)

            def recur():
                settle()
                dve.wait_ge(root_ready, 1)
                dve.tensor_tensor(ig, ig, rg, ALU.mult).then_inc(ig_used, 1)
                dve.wait_ge(ig_used, 1)
                for h in range(K96):
                    ins = dve.tensor_tensor_scan(out_a[:, h, :], ra[:, h, :], ig[:, h, :], 0.0, ALU.mult, ALU.add)
                ins.then_inc(rnn_done, 1)

            beside = (log_decay, gla_decayed, gated_input, squared_decay, one_minus)
            for u in range(MH * QB + 1):
                if u < MH * QB:
                    mem_max(u)
                if u:
                    mem_divide(u - 1)
                if u < len(beside):
                    beside[u]()
            recur()

            def silu(i):
                dve.wait_ge(sg_sig, i + 1)
                bank = plan["zg"][i].bank
                part = sg[:, 2 * i:2 * i + 2, :]
                dve.tensor_tensor(part, part, pair(gemm[bank], C96), ALU.mult).then_inc(evacuated[bank], 1)

            def gla_states(n):
                for half in range(2):
                    bank = aux[half if n % 2 == 0 else 2 + half]
                    dve.wait_ge(states_psum, 2 * n + half + 1)
                    if n == 0:
                        dve.tensor_copy(states[:, 2 * half:2 * half + 2, 0, :],
                                        bank[0:GDK, 0:2 * GDV].rearrange("p (h v) -> p h v", h=2)).then_inc(states_done, 1)
                        continue
                    for i in range(2):
                        h = 2 * half + i
                        dve.wait_ge(states_done, 2 if n == 1 else 2 + h + 1)
                        dve.scalar_tensor_tensor(states[:, h, n, :], states[:, h, n - 1, :], decay[:, h, n:n + 1],
                                                 bank[0:GDK, i * GDV:(i + 1) * GDV],
                                                 ALU.mult, ALU.add).then_inc(states_done, 1)

            silu(0)
            silu(1)
            dve.wait_ge(gla_exp, 4)
            gla_states(0)
            gla_states(1)
            rest_parts(a_parts[1], out_a, a_parts[0], outa_rounded, outa_split)
            silu(2)
            gla_states(2)
            silu(3)

            def merge(b, i):
                c = plan[f"branch{b}"][i]
                m, g = merged[:, 2 * i:2 * i + 2, :], gate[:, 2 * i:2 * i + 2, :]
                taken(dve, c)
                moved(dve, [plan[f"gate{b}"][i]])
                if b == 0:
                    dve.tensor_tensor(m, g, pair(gemm[c.bank]), ALU.mult).then_inc(evacuated[c.bank], 1)
                    return
                dve.tensor_tensor(g, g, pair(gemm[c.bank]), ALU.mult).then_inc(evacuated[c.bank], 1)
                moved(dve, [c, plan["branch0"][i]])
                if b == 2:
                    dve.wait_ge(merge_done, i + 1)
                dve.tensor_tensor(m, m, g, ALU.add).then_inc(merge_done, 1)

            def merged_rest(i):
                part = slice(2 * i, 2 * i + 2)
                dve.wait_ge(m_rounded, i + 1)
                dve.tensor_tensor(m_lo[:, part, :], merged[:, part, :], x_hi[:, part, :], ALU.subtract).then_inc(m_split, 1)

            dve.wait_ge(gate0_on, 1)
            for i in range(4):
                merge(0, i)
            dve.wait_ge(o_std, GH)
            step(dve.reciprocal(eg, eg))
            settle()
            for h in range(GH):
                for vh in range(2):
                    k = 2 * h + vh
                    step(dve.scalar_tensor_tensor(out_b[:, k, :], out_b[:, k, :], par("gla_norm_2", k, C96),
                                                  eg[:, h, :], ALU.mult, ALU.mult))
            settle()
            moved(dve, plan["zg"])
            dve.tensor_tensor(out_b, out_b, sg, ALU.mult).then_inc(out_b_done, 1)

            rest_parts(b_parts[1], out_b, b_parts[0], outb_rounded, outb_split)
            rest_parts(c_parts[1], out_c, c_parts[0], outc_rounded, outc_split)
            for i in range(4):
                merge(1, i)
            for i in range(4):
                merge(2, i)
                if i:
                    merged_rest(i - 1)
            merged_rest(3)
            add_to_residual("out2", 5)
            moved(dve, plan["out2"])

            normalise_split(5, 3, "norm_ffn_2")
            dve.memset(ub[:, :, :, 0:2], 0.0).then_inc(ffn_pads, 1)
            dve.wait_ge(ffn_pads, 1)
            settled = count[0]

            def ffn_convolve(s, n, it=0):
                b = s % 2
                dve.wait_ge(evacuated[plan["up"][s].bank], it + plan["up"][s].bank_use)
                for w in range(3):
                    for v in range(2):
                        j = n + v * KF
                        at = j * 3 + (PCOL["ffn_conv_w_2"] + w)
                        tap = params[:, at:at + 1] if isinstance(n, int) else params[:, bass.ds(at, 1)]
                        if w == 0:
                            at = j + PCOL["ffn_conv_b_2"]
                            bias = params[:, at:at + 1] if isinstance(n, int) else params[:, bass.ds(at, 1)]
                            ins = dve.tensor_scalar(uc[:, b, v, :], ub[:, b, v, 0:T], tap, bias, ALU.mult, ALU.add)
                        else:
                            dve.wait_ge(dve_step, n * 4 + (settled + 2 * w + v - 1))
                            ins = dve.scalar_tensor_tensor(uc[:, b, v, :], ub[:, b, v, w:w + T], tap,
                                                           uc[:, b, v, :], ALU.mult, ALU.add)
                        if w < 2:
                            ins.then_inc(dve_step, 1)
                        elif v == 1:
                            ins.then_inc(ffn_conv, 1)

            def ffn_multiply(b, n):
                dve.wait_ge(ffn_gelu, n + 1)
                dve.tensor_tensor(ffp[:, b, :], uc[:, b, 0, :], uc[:, b, 1, :], ALU.mult).then_inc(ffn_act, 1)

            def ffn_subtract(b, n):
                dve.wait_ge(ffn_rounded, n + 1)
                plane = slice(n, n + 1) if isinstance(n, int) else bass.ds(n, 1)
                dve.tensor_tensor(f_lo[:, plane, :].rearrange("p a t -> p (a t)"), ffp[:, b, :],
                                  f_hi[:, plane, :].rearrange("p a t -> p (a t)"),
                                  ALU.subtract).then_inc(ffn_split, 1)

            def ffn_step(s, n, it=0, first=False):
                if not first:
                    ffn_multiply((s + 1) % 2, n - 1)
                ffn_convolve(s, n, it)
                if not first:
                    ffn_subtract((s + 1) % 2, n - 1)

            for s in range(BANKS):
                ffn_step(s, s, first=(s == 0))
            with dve.Fori(1, KF // BANKS) as it:
                for s in range(BANKS):
                    ffn_step(s, it * BANKS + s, it)
            ffn_multiply((KF - 1) % 2, KF - 1)
            ffn_subtract((KF - 1) % 2, KF - 1)
            count[0] += 4 * KF
            for pr in range(4):
                c = plan["down"][3 * pr + 2]
                taken(dve, c)
                part = xres[:, 2 * pr:2 * pr + 2, :]
                dve.tensor_tensor(part, part, pair(aux[pr]), ALU.add).then_inc(x4_done, 1)
                pair_squares(6, pr)
            dve.wait_ge(x4_done, 4)
            normalise(6, xres, yout, "final_norm_2", step_tiles=2)


def _per_partition(v, rows=P):
    v = np.moveaxis(np.asarray(v), -1, 0)
    v = v.reshape((v.shape[0] // rows, rows) + v.shape[1:])
    v = np.moveaxis(v, 1, 0).reshape(rows, -1)
    return np.concatenate([v, np.zeros((P - rows, v.shape[1]), v.dtype)]) if rows < P else v


def _columns(w, m, rows=P):
    k, n = w.shape
    return w.reshape(k // rows, rows, n // m, m).transpose(2, 1, 0, 3).reshape(n // m, rows, -1)


def _half_columns(w):
    k, n = w.shape
    return w.reshape(2, k // P // 2, P, n // CW, CW).transpose(3, 0, 2, 1, 4).reshape(2 * n // CW, P, -1)


def _weights(a):
    w_in, w_in2, w_kv = a["w_in"], a["w_in_2"][0], a["w_mem_kv_2"][0]

    def part(w, first, n):
        return w[:, first:first + n]

    w = {}
    for j in range(4):
        w[f"conv_in{j}"] = np.concatenate([_columns(part(w_in, first + j * CW, CW), P) for first in (A_GATE, A_VAL)])
    w["f"] = _columns(part(w_in, F0, HEADS), HEADS)
    for name, first in (("q", Q0), ("k", K0), ("ga", GA0), ("gb", GB0)):
        w[name] = _columns(part(w_in, first, D), P)
    w["v"] = _half_columns(part(w_in, V0, D))
    for name, source in (("conv_out", "w_conv_out"), ("fox_out", "w_fox_out"), ("mix_out", "w_out"),
                         ("peer_q", "peer_wq")):
        w[name] = _columns(a[source], P)
    keys = np.stack([a["peer_k1"], a["peer_k2"]], axis=1).reshape(2, HALVES // 2, NK, DK // 2)
    w["keys"] = keys.transpose(0, 3, 1, 2).reshape(2, P, TILE)
    w["u"] = a["peer_u"].reshape(P, P, KD, P).transpose(0, 3, 2, 1).reshape(P, P, TILE)
    w["ev"] = a["peer_v"].reshape(P, P, TILE)
    w["mem_k"] = _columns(part(w_kv, 0, MW), C96)
    w["mem_v"] = _half_columns(part(w_kv, MW, MW))
    for name, first, n in (("z_rnn", Z_RNN, MW), ("zq", Z_Q, GH * GDK), ("zk", Z_K, GH * GDK), ("zmq", Z_MQ, MW),
                           ("zg", Z_G, MW)):
        w[name] = _columns(part(w_in2, first, n), C96)
    w["dec"] = _columns(part(w_in2, Z_DEC, LOW), LOW)
    w["zv"] = _half_columns(part(w_in2, Z_V, MW))
    for b in range(3):
        w[f"gate{b}"] = _columns(part(w_in2, Z_GATE + b * D, D), P)
        w[f"branch{b}"] = _columns(a["w_branch_2"][0, b], P, C96)
    w["out2"] = _columns(a["w_out_2"][0], P)
    w["up"] = np.stack([_columns(part(a["w_up_2"][0], v * DFF, DFF), P) for v in range(2)], axis=1).reshape(2 * KF, P, TILE)
    w["down"] = np.stack([_columns(g, P) for g in a["w_down_2"][0].reshape(3, D, D)]).reshape(
        3, 4, 2, P, TILE).transpose(1, 0, 2, 3, 4).reshape(-1, P, TILE)
    return {f"w_{name}": v for name, v in w.items()}


def _layout(a):
    names = list(_VEC128) + ["conv_w", "ffn_conv_w_2", "ffn_conv_b_2"]
    flat = {n: (a[n][0] if n.endswith("_2") and a[n].ndim > 1 else a[n]) for n in names}
    cols = [_per_partition(flat[n]) for n in names]
    cols.append(_per_partition(a["fox_bf"], HEADS))
    for n in ("rnn_conv_w_2", "rnn_conv_b_2"):
        cols.append(_per_partition(a[n][0], C96))
    for n in ("rg_b_a_2", "rg_b_x_2", "rg_lambda_2", "gla_b_decay_2", "gla_norm_2"):
        cols.append(_per_partition(a[n][0].reshape(-1), C96))
    return {
        "xT": a["x"][0].T, "memT": a["mem_2"][0].T, "params": np.concatenate(cols, axis=1),
        "rg_w_a_2": a["rg_w_a_2"][0], "rg_w_x_2": a["rg_w_x_2"][0], "gla_w_decay_2": a["gla_w_decay_2"][0],
        **_weights(a),
    }


def kernel(**inputs):
    import concourse.bacc as bacc
    from concourse.bass_utils import run_bass_kernel_spmd

    arrays = {n: np.ascontiguousarray(v) for n, v in _layout({n: np.asarray(v) for n, v in inputs.items()}).items()}
    nc = bacc.Bacc("TRN2", target_bir_lowering=False, num_devices=1)
    t = {n: nc.dram_tensor(f"in_{n}", v.shape, F32, kind="ExternalInput").ap() for n, v in arrays.items()}
    t["yT"] = nc.dram_tensor("yT", (D, T), F32, kind="ExternalOutput").ap()
    build(nc, t)
    r = run_bass_kernel_spmd(nc, [{f"in_{n}": v for n, v in arrays.items()}], core_ids=[0])
    return r.results[0]["yT"].T.reshape(1, T, D)
```
